# Optimizing a Trainium2 kernel written in Bass

```python
import jax, jax.numpy as jnp
from jax import lax
import numpy as np

D_MODEL = 1024
BATCH = 1
SEQ = 2048
DEPTH = 1

GRID_W = 64
HEAD_DIM = 64
N_Q_HEADS = 8
N_KV_HEADS = 2
Q_PER_KV = N_Q_HEADS // N_KV_HEADS
ATTN_WIDTH = N_Q_HEADS * HEAD_DIM
KV_WIDTH = N_KV_HEADS * HEAD_DIM
N_FOURIER_GROUPS = 4
FOURIER_GROUP_DIM = 128
FOURIER_WIDTH = N_FOURIER_GROUPS * FOURIER_GROUP_DIM
IN_WIDTH = ATTN_WIDTH + 2 * KV_WIDTH + FOURIER_WIDTH + 2 * D_MODEL
ROPE_THETA = 10000.0
ROPE_PAIRS_PER_AXIS = HEAD_DIM // 4
Q_BLOCK = 128
D_FF = 2816
CONV_WIDTH = 3
NORM_EPS = 1e-6

kernel_name = "hybrid_gqa_fnet_convffn_block"

def rms_norm(x, g):
    xf = x.astype(jnp.float32)
    y = xf * lax.rsqrt(jnp.mean(xf * xf, axis=-1, keepdims=True) + NORM_EPS)
    return (y * g.astype(jnp.float32)).astype(x.dtype)

def axial_rope_tables(seq_len):
    rows_count = seq_len // GRID_W
    row = jnp.repeat(jnp.arange(rows_count, dtype=jnp.float32), GRID_W)
    col = jnp.tile(jnp.arange(GRID_W, dtype=jnp.float32), rows_count)
    inv = ROPE_THETA ** (-jnp.arange(ROPE_PAIRS_PER_AXIS, dtype=jnp.float32) / ROPE_PAIRS_PER_AXIS)
    ang = jnp.concatenate([row[:, None] * inv, col[:, None] * inv], axis=-1)
    return jnp.cos(ang), jnp.sin(ang)

def apply_rope(x, cos, sin):
    xf = x.astype(jnp.float32).reshape(*x.shape[:-1], HEAD_DIM // 2, 2)
    x0, x1 = xf[..., 0], xf[..., 1]
    c = cos[None, :, None, :]
    s = sin[None, :, None, :]
    out = jnp.stack([x0 * c - x1 * s, x0 * s + x1 * c], axis=-1).reshape(x.shape)
    return out.astype(x.dtype)

def block_attention(q, k, v):
    B, S = q.shape[0], q.shape[1]
    nb = S // Q_BLOCK
    qb = q.reshape(B, nb, Q_BLOCK, N_KV_HEADS, Q_PER_KV, HEAD_DIM).transpose(1, 0, 2, 3, 4, 5)
    scale = HEAD_DIM ** -0.5

    def one_block(qi):
        s = jnp.einsum('bqkgd,bskd->bkgqs', qi, k, preferred_element_type=jnp.float32) * scale
        p = jax.nn.softmax(s, axis=-1).astype(v.dtype)
        return jnp.einsum('bkgqs,bskd->bqkgd', p, v)

    o = lax.map(one_block, qb)
    return o.transpose(1, 0, 2, 3, 4, 5).reshape(B, S, ATTN_WIDTH)

def fourier_mix(f):
    B, S = f.shape[0], f.shape[1]
    ff = f.astype(jnp.float32).reshape(B, S, N_FOURIER_GROUPS, FOURIER_GROUP_DIM)
    y = jnp.fft.fft2(ff, axes=(1, 3), norm="ortho").real
    return y.reshape(B, S, FOURIER_WIDTH).astype(f.dtype)

def depthwise_conv_centred(u, w, b):
    S = u.shape[1]
    half = CONV_WIDTH // 2
    up = jnp.pad(u, ((0, 0), (half, CONV_WIDTH - 1 - half), (0, 0)))
    y = up[:, 0:S] * w[0]
    for i in range(1, CONV_WIDTH):
        y = y + up[:, i:i + S] * w[i]
    return y + b

def setup_inputs(seed: int = 0) -> dict:
    key = jax.random.key(seed)
    ks = jax.random.split(key, 19)
    L = DEPTH

    def nrm(k, shape, scale):
        return jax.random.normal(k, shape, jnp.float32) * scale

    return {
        "x": nrm(ks[0], (BATCH, SEQ, D_MODEL), 1.0),
        "c": nrm(ks[1], (BATCH, D_MODEL), 1.0),
        "w_ada": nrm(ks[2], (L, D_MODEL, 6 * D_MODEL), 0.5 * D_MODEL ** -0.5),
        "b_ada": nrm(ks[3], (L, 6 * D_MODEL), 0.01),
        "mix_pre_g": 1.0 + nrm(ks[4], (L, D_MODEL), 0.02),
        "w_in": nrm(ks[5], (L, D_MODEL, IN_WIDTH), D_MODEL ** -0.5),
        "q_norm_g": 1.0 + nrm(ks[6], (L, HEAD_DIM), 0.02),
        "k_norm_g": 1.0 + nrm(ks[7], (L, HEAD_DIM), 0.02),
        "b_gate": nrm(ks[8], (L, 2 * D_MODEL), 0.01),
        "w_attn_branch": nrm(ks[9], (L, ATTN_WIDTH, D_MODEL), ATTN_WIDTH ** -0.5),
        "w_fourier_branch": nrm(ks[10], (L, FOURIER_WIDTH, D_MODEL), FOURIER_WIDTH ** -0.5),
        "w_out": nrm(ks[11], (L, D_MODEL, D_MODEL), D_MODEL ** -0.5),
        "mix_post_g": 1.0 + nrm(ks[12], (L, D_MODEL), 0.02),
        "ffn_pre_g": 1.0 + nrm(ks[13], (L, D_MODEL), 0.02),
        "w_up": nrm(ks[14], (L, D_MODEL, 2 * D_FF), D_MODEL ** -0.5),
        "conv_w": nrm(ks[15], (L, CONV_WIDTH, 2 * D_FF), CONV_WIDTH ** -0.5),
        "conv_b": nrm(ks[16], (L, 2 * D_FF), 0.01),
        "w_down": nrm(ks[17], (L, D_FF, D_MODEL), D_FF ** -0.5),
        "ffn_post_g": 1.0 + nrm(ks[18], (L, D_MODEL), 0.02),
    }

def reference(x, c, w_ada, b_ada, mix_pre_g, w_in, q_norm_g, k_norm_g, b_gate,
              w_attn_branch, w_fourier_branch, w_out, mix_post_g, ffn_pre_g,
              w_up, conv_w, conv_b, w_down, ffn_post_g):
    B, S = x.shape[0], x.shape[1]
    cos, sin = axial_rope_tables(S)
    c_act = jax.nn.silu(c)
    o1 = ATTN_WIDTH
    o2 = o1 + KV_WIDTH
    o3 = o2 + KV_WIDTH
    o4 = o3 + FOURIER_WIDTH
    o5 = o4 + D_MODEL
    for l in range(DEPTH):
        mod = (c_act @ w_ada[l] + b_ada[l])[:, None, :]
        shift1, scale1, gate1, shift2, scale2, gate2 = jnp.split(mod, 6, axis=-1)

        h = rms_norm(x, mix_pre_g[l]) * (1.0 + scale1) + shift1
        z = h @ w_in[l]
        q = z[..., :o1].reshape(B, S, N_Q_HEADS, HEAD_DIM)
        k = z[..., o1:o2].reshape(B, S, N_KV_HEADS, HEAD_DIM)
        v = z[..., o2:o3].reshape(B, S, N_KV_HEADS, HEAD_DIM)
        f = z[..., o3:o4]
        g_a = jax.nn.sigmoid(z[..., o4:o5] + b_gate[l, :D_MODEL])
        g_f = jax.nn.sigmoid(z[..., o5:] + b_gate[l, D_MODEL:])
        q = apply_rope(rms_norm(q, q_norm_g[l]), cos, sin)
        k = apply_rope(rms_norm(k, k_norm_g[l]), cos, sin)
        y_attn = block_attention(q, k, v) @ w_attn_branch[l]
        y_four = fourier_mix(f) @ w_fourier_branch[l]
        y = (g_a * y_attn + g_f * y_four) @ w_out[l]
        x = x + gate1 * rms_norm(y, mix_post_g[l])

        h = rms_norm(x, ffn_pre_g[l]) * (1.0 + scale2) + shift2
        u = depthwise_conv_centred(h @ w_up[l], conv_w[l], conv_b[l])
        a, bval = jnp.split(u, 2, axis=-1)
        y = (jax.nn.gelu(a, approximate=True) * bval) @ w_down[l]
        x = x + gate2 * rms_norm(y, ffn_post_g[l])
    return x


_drawn_inputs = setup_inputs


def setup_inputs(seed=0):
    import zlib

    import numpy as np

    out = dict(_drawn_inputs(seed))
    spreads = {}
    factors = {'b_ada': 3.787,
     'mix_pre_g': 8.0,
     'q_norm_g': 8.0,
     'k_norm_g': 8.0,
     'b_gate': 38.752,
     'mix_post_g': 8.0,
     'ffn_pre_g': 19.392,
     'conv_b': 40.302,
     'ffn_post_g': 33.136}
    for name, (base, spread) in spreads.items():
        noise = np.random.default_rng([zlib.crc32(name.encode()), seed]).standard_normal(out[name].shape)
        drawn = base * np.exp(spread * noise) if base else spread * noise
        out[name] = __import__('jax').numpy.asarray(drawn.astype(out[name].dtype))
    for name, factor in factors.items():
        out[name] = (out[name] * factor).astype(out[name].dtype)
    return out
```

```python
import math
from contextlib import ExitStack

import numpy as np

import concourse.bass as bass
from concourse import mybir

F32 = mybir.dt.float32
F32R = mybir.dt.float32r
ALU = mybir.AluOpType
ACT = mybir.ActivationFunctionType
AX = mybir.AxisListType

P = 128
D = 1024
S = 2048
KD = D // P
NT = S // P
BLK = 512
NB = S // BLK
HD = 64
NH = 8
NQC = NH * HD // P
NKV = 2
NG = 4
FW = NG * P
DFF = 2816
NP = DFF // P
HALF = S // 2
EPS = 1e-6
N1 = 16
K1 = N1 // 2 + 1


class Res:

    def __init__(self, nc, tag):
        self.nc, self.tag, self.ctx, self.sem_nums = nc, tag, ExitStack(), []

    def __enter__(self):
        return self

    def __exit__(self, *a):
        return self.ctx.__exit__(*a)

    def sb(self, name, shape, dt=F32):
        return self.ctx.enter_context(self.nc.sbuf_tensor(f"{self.tag}_{name}", shape, dt))

    def ps(self, name, shape, dt=F32):
        return self.ctx.enter_context(self.nc.psum_tensor(f"{self.tag}_{name}", shape, dt))

    def sem(self, name):
        handle = self.ctx.enter_context(self.nc.semaphore(f"{self.tag}_{name}"))
        self.sem_nums.append(handle.num)
        return handle

    def pool_dma_sem(self, name):
        return self.nc.alloc_semaphore(name=f"{self.tag}_{name}")

    def block(self):
        return self.nc.Block()


def product3(pe, out, w_hi, w_lo, x_hi, x_lo, first, last):
    pe.matmul(out, w_hi, x_hi, start=first, stop=False)
    pe.matmul(out, w_hi, x_lo, start=False, stop=False)
    return pe.matmul(out, w_lo, x_hi, start=False, stop=last)


def load_constants(nc, ident_d, ident, ones):
    with Res(nc, "const") as r:
        loaded = r.sem("loaded")
        with r.block() as block:

            @block.sync
            def _(sp):
                sp.dma_start(ident[:], ident_d).then_inc(loaded, 16)
                sp.wait_ge(loaded, 16)

            @block.vector
            def _(dve):
                dve.memset(ones[:], 1.0)
        return loaded.num


def ada_phase(nc, c_d, w_ada, b_ada, pre_g, post_g, ident, ones, mod, gate_rows):
    W6 = 6 * D
    with Res(nc, "ada") as r:
        c_raw = r.sb("c_raw", [P, KD])
        c_act = r.sb("c_act", [P, KD])
        w = [r.sb(f"w{i}", [P, W6]) for i in range(2)]
        acc = r.sb("acc", [P, W6])
        bias = r.sb("bias", [1, W6])
        gains = r.sb("gains", [P, 2, KD])
        post = r.sb("post", [P, 2, D])
        rows = r.sb("rows", [P, 2, D])
        cols = r.sb("cols", [P, 4, KD])
        ps_cols = r.ps("ps_cols", [P, 512])
        ps_rows = r.ps("ps_rows", [P, 4, 512])
        s_small, s_bias = r.sem("small"), r.sem("bias")
        s_w = [r.sem(f"w_loaded{i}") for i in range(2)]
        s_silu, s_acc, s_cols, s_rows, s_fin, s_out = (r.sem(n) for n in ("silu", "acc", "cols", "rows", "fin", "out"))
        with r.block() as block:

            @block.sync
            def _(sp):
                sp.dma_start(c_raw[:], c_d).then_inc(s_small, 16)
                for k in range(KD):
                    if k >= 2:
                        sp.wait_ge(s_acc, k - 1)
                    sp.dma_start(w[k % 2][:], w_ada[k]).then_inc(s_w[k % 2], 16)
                sp.dma_start(bias[:], b_ada).then_inc(s_bias, 16)
                sp.dma_start(gains[:], pre_g).then_inc(s_bias, 16)
                for j in range(2):
                    sp.dma_start(post[:, j, :], post_g[j:j + 1, :].broadcast_to([P, D])).then_inc(s_bias, 16)
                sp.wait_ge(s_fin, 4)
                sp.dma_start(gate_rows, rows[:]).then_inc(s_out, 16)
                sp.wait_ge(s_out, 16)

            @block.scalar
            def _(act):
                act.wait_ge(s_small, 16)
                act.activation(c_act[:], c_raw[:], ACT.Silu).then_inc(s_silu, 1)

            @block.vector
            def _(dve):
                dve.wait_ge(s_silu, 1)
                for k in range(KD):
                    dve.wait_ge(s_w[k % 2], 16 * (k // 2 + 1))
                    if k == 0:
                        dve.tensor_scalar(acc[:], w[0][:], c_act[:, 0:1], None, ALU.mult).then_inc(s_acc, 1)
                    else:
                        dve.wait_ge(s_acc, k)
                        dve.scalar_tensor_tensor(acc[:], w[k % 2][:], c_act[:, k:k + 1], acc[:],
                                                 ALU.mult, ALU.add).then_inc(s_acc, 1)
                dve.wait_ge(s_bias, 64)
                dve.wait_ge(s_acc, KD)
                dve.tensor_tensor(acc[0:1, :], acc[0:1, :], bias[:], ALU.add).then_inc(s_acc, 1)
                dve.wait_ge(s_cols, 1)
                dve.tensor_copy(cols[:], ps_cols[:, 0:4 * KD].rearrange("p (a k) -> p a k", a=4)).then_inc(s_fin, 1)
                dve.wait_ge(s_fin, 1)
                for j in range(2):
                    dve.scalar_tensor_tensor(mod[:, 2 * j, :], cols[:, 2 * j + 1, :], 1.0, gains[:, j, :],
                                             ALU.add, ALU.mult)
                    ins = dve.tensor_copy(mod[:, 2 * j + 1, :], cols[:, 2 * j, :])
                ins.then_inc(s_fin, 1)
                dve.wait_ge(s_rows, 1)
                for j in range(2):
                    dve.tensor_tensor(rows[:, j, :], ps_rows[:, 2 * j:2 * j + 2, :].rearrange("p a b -> p (a b)"),
                                      post[:, j, :], ALU.mult).then_inc(s_fin, 1)

            @block.tensor
            def _(pe):
                pe.wait_ge(s_acc, KD + 1)
                for a, part in enumerate((0, 1, 3, 4)):
                    for k in range(KD):
                        at = part * D + k * P
                        m = pe.matmul(ps_cols[:, a * KD + k:a * KD + k + 1], acc[:, at:at + P], ones[:, 0:1],
                                      start=True, stop=True)
                m.then_inc(s_cols, 1)
                for j, part in enumerate((2, 5)):
                    for n in range(2):
                        at = part * D + n * 512
                        m = pe.matmul(ps_rows[:, 2 * j + n, :], ones[:], acc[:, at:at + 512], start=True, stop=True)
                m.then_inc(s_rows, 1)


def norm_phase(nc, tag, x_d, nblocks, ident, scale, shift, hT_hi, hT_lo):
    TB = BLK // P
    assert nblocks % 2 == 0
    with Res(nc, tag) as r:
        x = [r.sb(f"x{i}", [P, TB, D]) for i in range(2)]
        junk = r.sb("junk", [P, D])
        sums = [r.sb(f"sums{i}", [P, TB]) for i in range(2)]
        mean = [r.sb(f"mean{i}", [P, TB]) for i in range(2)]
        std = [r.sb(f"std{i}", [P, TB]) for i in range(2)]
        rstd = [r.sb(f"rstd{i}", [P, TB]) for i in range(2)]
        full = r.sb("full", [P, 2, BLK])
        ps = r.ps("ps", [P, 4, BLK])
        s_x = [r.sem(f"x{i}") for i in range(2)]
        names = ("sq", "mean", "std", "rstd", "xn", "tr", "full", "hi", "lo")
        s_sq, s_mean, s_std, s_rstd, s_xn, s_tr, s_full, s_hi, s_lo = (r.sem(n) for n in names)
        with r.block() as block:

            @block.sync
            def _(sp):
                with sp.Fori(0, nblocks // 2) as i:
                    for u in range(2):
                        sp.wait_ge(s_tr, (2 * i + u + 1) * KD)
                        sp.dma_start(x[u][:], x_d[bass.ds((2 * i + u) * TB, TB), :, :].rearrange("t p d -> p t d"))\
                            .then_inc(s_x[u], 16)

            @block.scalar
            def _(act):
                with act.Fori(0, nblocks // 2) as i:
                    for u in range(2):
                        b = 2 * i + u
                        act.wait_ge(s_x[u], 16 * i + 16)
                        for j in range(TB):
                            act.wait_ge(s_sq, b * TB + j + 1)
                            act.activation(junk[:], x[u][:, j, :], ACT.Square, accum_out=sums[u][:, j:j + 1])\
                                .then_inc(s_sq, 1)
                        act.wait_ge(s_mean, b + 1)
                        act.activation(std[u][:], mean[u][:], ACT.Sqrt).then_inc(s_std, 1)
                        for k in range(KD):
                            act.wait_ge(s_tr, (b + 2) * KD + k + 1)
                            act.wait_ge(s_lo, b * KD + k + 1)
                            act.wait_ge(s_full, b * KD + k + 1)
                            act.activation(full[:, k % 2, :], ps[:, k % 4, :], ACT.Identity,
                                           bias=shift[:, k:k + 1], scale=scale[:, k:k + 1]).then_inc(s_full, 1)

            @block.vector
            def _(dve):
                dve.sem_inc(s_lo, 2)
                with dve.Fori(0, nblocks // 2) as i:
                    for u in range(2):
                        b = 2 * i + u
                        dve.wait_ge(s_sq, b * TB + TB + 1)
                        dve.tensor_scalar(mean[u][:], sums[u][:], 1.0 / D, EPS, ALU.mult, ALU.add).then_inc(s_mean, 1)
                        dve.wait_ge(s_std, b + 1)
                        dve.reciprocal(rstd[u][:], std[u][:]).then_inc(s_rstd, 1)
                        dve.wait_ge(s_rstd, b + 1)
                        for j in range(TB):
                            dve.tensor_scalar(x[u][:, j, :], x[u][:, j, :], rstd[u][:, j:j + 1], None, ALU.mult)\
                                .then_inc(s_xn, 1)
                        for k in range(KD):
                            cols = bass.ds(b * BLK, BLK)
                            dve.wait_ge(s_full, b * KD + k + 2)
                            dve.tensor_copy(hT_hi[:, k, cols], full[:, k % 2, :]).then_inc(s_hi, 1)
                            dve.wait_ge(s_hi, b * KD + k + 1)
                            dve.tensor_tensor(hT_lo[:, k, cols], full[:, k % 2, :], hT_hi[:, k, cols], ALU.subtract)\
                                .then_inc(s_lo, 1)

            @block.tensor
            def _(pe):
                pe.sem_inc(s_tr, 2 * KD)
                pe.sem_inc(s_sq, 1)
                pe.sem_inc(s_full, 1)
                with pe.Fori(0, nblocks // 2) as i:
                    for u in range(2):
                        b = 2 * i + u
                        pe.wait_ge(s_xn, (b + 1) * TB)
                        for k in range(KD):
                            if k >= 4:
                                pe.wait_ge(s_full, b * KD + k - 3 + 1)
                            elif k == 0:
                                pe.wait_ge(s_full, b * KD + 1)
                            for j in range(TB):
                                m = pe.transpose(ps[:, k % 4, j * P:(j + 1) * P], x[u][:, j, k * P:(k + 1) * P],
                                                 ident[:])
                            m.then_inc(s_tr, 1)


def f_phase(nc, w_f, hT_hi, hT_lo, f_d):
    with Res(nc, "fin") as r:
        w_st = r.sb("w_st", [P, 2, FW])
        w_hi = r.sb("w_hi", [P, KD, FW], F32R)
        w_lo = r.sb("w_lo", [P, KD, FW], F32R)
        out = r.sb("out", [P, 4, FW])
        ps = r.ps("ps", [P, 4, FW])
        s_w = [r.sem(f"w{i}") for i in range(2)]
        s_hi, s_lo, s_mm, s_ev = (r.sem(n) for n in ("hi", "lo", "mm", "ev"))
        s_out = [r.sem(f"out{i}") for i in range(4)]
        with r.block() as block:

            @block.sync
            def _(sp):
                for k in range(KD):
                    if k >= 2:
                        sp.wait_ge(s_lo, k - 1)
                    sp.dma_start(w_st[:, k % 2, :], w_f[k]).then_inc(s_w[k % 2], 16)
                for t in range(NT):
                    sp.wait_ge(s_ev, t + 1)
                    sp.dma_start(f_d[t], out[:, t % 4, :]).then_inc(s_out[t % 4], 16)
                for i in range(4):
                    sp.wait_ge(s_out[i], 16 * NT // 4)

            @block.vector
            def _(dve):
                for k in range(KD):
                    dve.wait_ge(s_w[k % 2], 16 * (k // 2 + 1))
                    dve.tensor_copy(w_hi[:, k, :], w_st[:, k % 2, :]).then_inc(s_hi, 1)
                    dve.wait_ge(s_hi, k + 1)
                    dve.tensor_tensor(w_lo[:, k, :], w_st[:, k % 2, :], w_hi[:, k, :], ALU.subtract).then_inc(s_lo, 1)

            @block.scalar
            def _(act):
                for t in range(NT):
                    act.wait_ge(s_mm, t + 1)
                    if t >= 4:
                        act.wait_ge(s_out[t % 4], 16 * (t // 4))
                    act.activation(out[:, t % 4, :], ps[:, t % 4, :], ACT.Copy).then_inc(s_ev, 1)

            @block.tensor
            def _(pe):
                for t in range(NT):
                    if t >= 4:
                        pe.wait_ge(s_ev, t - 3)
                    for k in range(KD):
                        if t == 0:
                            pe.wait_ge(s_lo, k + 1)
                        cols = slice(t * P, (t + 1) * P)
                        m = product3(pe, ps[:, t % 4, :], hT_hi[:, k, cols], hT_lo[:, k, cols],
                                     w_hi[:, k, :], w_lo[:, k, :], k == 0, k == KD - 1)
                    m.then_inc(s_mm, 1)


def proj_phase(nc, w_z, hT_hi, hT_lo, b_gate, qk_g, rope_cos, rope_sin, swap_d, head_mean_d, qkv_d, gates_d):
    NQKV = NQC + 2
    NC = NQKV + 2 * KD
    with Res(nc, "proj") as r:
        w_st = r.sb("w_st", [P, 2, KD, P])
        w_hi = [r.sb(f"w_hi{i}", [P, KD, P], F32R) for i in range(2)]
        w_lo = [r.sb(f"w_lo{i}", [P, KD, P], F32R) for i in range(2)]
        out = r.sb("out", [P, NB, BLK])
        cos = r.sb("cos", [P, S])
        sin = r.sb("sin", [P, S])
        bg = r.sb("bg", [P, 2 * KD])
        gains = r.sb("gains", [P, NQC + 1])
        swap = r.sb("swap", [P, P])
        head_mean = r.sb("head_mean", [P, P])
        eps = r.sb("eps", [P, 1])
        bcol = r.sb("bcol", [P, 2])
        zg, sq, std, rot = (r.sb(n, [P, 2, BLK]) for n in ("zg", "sq", "std", "rot"))
        ps = r.ps("ps", [P, NB, BLK])
        ps_ms = r.ps("ps_ms", [P, 2, BLK])
        ps_sw = r.ps("ps_sw", [P, 2, BLK])
        s_c, s_eps, s_bcol = r.sem("consts"), r.sem("eps_written"), r.sem("bias_at_hand")
        s_w = [r.sem(f"w_loaded{i}") for i in range(2)]
        s_hi, s_lo, s_mm, s_zg, s_ms, s_std, s_rot, s_out, s_rope = (
            r.sem(n) for n in ("w_hi_made", "w_lo_made", "products", "zg_sq", "mean_swap", "root", "rotated", "v_or_gate", "rope"))
        s_st = [r.pool_dma_sem(f"stored{n}") for n in range(NB)]
        with r.block() as block:

            @block.sync
            def _(sp):
                for dst, src in ((cos, rope_cos), (sin, rope_sin), (bg, b_gate), (gains, qk_g), (swap, swap_d),
                                 (head_mean, head_mean_d)):
                    sp.dma_start(dst[:], src).then_inc(s_c, 16)

                def load(c, u):
                    sp.dma_start(w_st[:, u:u + 1, :, :],
                                 w_z[bass.ds(c, 1), :, :].rearrange("o p (k m) -> p o k m", k=KD)).then_inc(s_w[u], 16)

                load(0, 0)
                load(1, 1)
                with sp.Fori(0, NC // 2 - 1) as i:
                    for u in range(2):
                        sp.wait_ge(s_lo, 2 * i + u + 1)
                        load(2 * i + u + 2, u)

            @block.gpsimd
            def _(pool):
                with pool.Fori(0, NQC + 1) as c:
                    for n in range(NB):
                        pool.wait_ge(s_rot, 4 * c + n + 1)
                        pool.dma_start(qkv_d[bass.ds(c, 1), :, n * BLK:(n + 1) * BLK], out[:, n, :]).then_inc(s_st[n], 16)
                for n in range(NB):
                    pool.wait_ge(s_out, n + 1)
                    pool.dma_start(qkv_d[NQC + 1, :, n * BLK:(n + 1) * BLK], out[:, n, :]).then_inc(s_st[n], 16)
                with pool.Fori(0, 2 * KD) as g:
                    for n in range(NB):
                        pool.wait_ge(s_out, 4 * g + 4 + n + 1)
                        pool.dma_start(gates_d[n, bass.ds(g, 1), :, :], out[:, n, :]).then_inc(s_st[n], 16)
                for n in range(NB):
                    pool.wait_ge(s_st[n], 16 * NC)

            @block.scalar
            def _(act):
                def hi_part(c, i, u):
                    act.wait_ge(s_w[u], 16 * i + 16)
                    act.activation(w_hi[u][:], w_st[:, u, :, :], ACT.Copy).then_inc(s_hi, 1)

                def root(c, n):
                    act.wait_ge(s_ms, 4 * c + n + 1)
                    if c or n >= 2:
                        act.wait_ge(s_rot, 4 * c + n - 1)
                    act.activation(std[:, n % 2, :], ps_ms[:, n % 2, :], ACT.Sqrt, bias=eps[:, 0:1]).then_inc(s_std, 1)

                hi_part(0, 0, 0)
                act.wait_ge(s_c, 16 * 6)
                act.wait_ge(s_eps, 1)
                for c in range(NQC + 1):
                    if c:
                        act.wait_ge(s_mm, 4 * c)
                    hi_part(c + 1, (c + 1) // 2, (c + 1) % 2)
                    for n in range(NB):
                        act.wait_ge(s_mm, 4 * c + n + 1)
                        if c or n >= 2:
                            act.wait_ge(s_rot, 4 * c + n - 1)
                        act.activation(zg[:, n % 2, :], ps[:, n, :], ACT.Copy, scale=gains[:, c:c + 1])
                        act.activation(sq[:, n % 2, :], ps[:, n, :], ACT.Square).then_inc(s_zg, 1)
                        if n:
                            root(c, n - 1)
                    root(c, NB - 1)

                def next_hi(c, i, u):
                    act.wait_ge(s_mm, 4 * c)
                    hi_part(c + 1, i + u, 1 - u)

                def chunk_out(c, func, **bias):
                    for n in range(NB):
                        act.wait_ge(s_mm, 4 * c + n + 1)
                        act.wait_ge(s_st[n], 16 * c)
                        act.activation(out[:, n, :], ps[:, n, :], func, **bias).then_inc(s_out, 1)

                next_hi(NQC + 1, (NQC + 1) // 2, 1)
                chunk_out(NQC + 1, ACT.Copy)
                with act.Fori(0, KD - 1) as i:
                    for u in range(2):
                        next_hi(2 * i + NQKV + u, i + NQKV // 2, u)
                        act.activation(bcol[:, u:u + 1], bg[:, bass.ds(2 * i + u, 1)], ACT.Copy).then_inc(s_bcol, 1)
                        act.wait_ge(s_bcol, 2 * i + u + 1)
                        chunk_out(2 * i + NQKV + u, ACT.Sigmoid, bias=bcol[:, u:u + 1])
                next_hi(NC - 2, (NC - 2) // 2, 0)
                chunk_out(NC - 2, ACT.Sigmoid, bias=bg[:, 2 * KD - 2:2 * KD - 1])
                chunk_out(NC - 1, ACT.Sigmoid, bias=bg[:, 2 * KD - 1:2 * KD])

            @block.vector
            def _(dve):
                def lo_part(c, u):
                    dve.wait_ge(s_hi, c + 1)
                    dve.tensor_tensor(w_lo[u][:], w_st[:, u, :, :], w_hi[u][:], ALU.subtract).then_inc(s_lo, 1)

                dve.memset(eps[:], EPS).then_inc(s_eps, 1)
                lo_part(0, 0)
                dve.wait_ge(s_c, 16 * 6)
                for c in range(NQC + 1):
                    lo_part(c + 1, (c + 1) % 2)
                    for n in range(NB):
                        cols = slice(n * BLK, (n + 1) * BLK)
                        done = 4 * (4 * c + n)
                        zc, rc, sc = zg[:, n % 2, :], rot[:, n % 2, :], std[:, n % 2, :]
                        dve.wait_ge(s_ms, 4 * c + n + 1)
                        if c:
                            dve.wait_ge(s_st[n], 16 * c)
                        dve.tensor_tensor(rc, ps_sw[:, n % 2, :], sin[:, cols], ALU.mult).then_inc(s_rope, 1)
                        dve.tensor_tensor(zc, zc, cos[:, cols], ALU.mult).then_inc(s_rope, 1)
                        dve.wait_ge(s_rope, done + 2)
                        dve.tensor_tensor(rc, rc, zc, ALU.add).then_inc(s_rope, 1)
                        dve.wait_ge(s_std, 4 * c + n + 1)
                        dve.reciprocal(sc, sc).then_inc(s_rope, 1)
                        dve.wait_ge(s_rope, done + 4)
                        dve.tensor_tensor(out[:, n, :], rc, sc, ALU.mult).then_inc(s_rot, 1)
                with dve.Fori(0, KD) as i:
                    for u in range(2):
                        lo_part(2 * i + NQKV + u, u)

            @block.tensor
            def _(pe):
                def block_products(n, u):
                    for k in range(KD):
                        m = product3(pe, ps[:, n, :], w_hi[u][:, k, :], w_lo[u][:, k, :],
                                     hT_hi[:, k, n * BLK:(n + 1) * BLK], hT_lo[:, k, n * BLK:(n + 1) * BLK],
                                     k == 0, k == KD - 1)
                    m.then_inc(s_mm, 1)

                def rope_products(c, n):
                    pe.wait_ge(s_zg, 4 * c + n + 1)
                    if c or n >= 2:
                        pe.wait_ge(s_rot, 4 * c + n - 1)
                    pe.matmul(ps_sw[:, n % 2, :], swap[:], zg[:, n % 2, :], start=True, stop=True)
                    pe.matmul(ps_ms[:, n % 2, :], head_mean[:], sq[:, n % 2, :], start=True, stop=True).then_inc(s_ms, 1)

                pe.wait_ge(s_c, 16 * 6)
                for c in range(NQC + 2):
                    pe.wait_ge(s_lo, c + 1)
                    for n in range(NB):
                        if c:
                            pe.wait_ge(s_zg, 4 * (c - 1) + n + 1)
                        if c <= NQC and n >= 2:
                            rope_products(c, n - 2)
                        if c and n < 2:
                            rope_products(c - 1, n + 2)
                        block_products(n, c % 2)
                with pe.Fori(0, KD) as i:
                    for u in range(2):
                        pe.wait_ge(s_lo, 2 * i + NQKV + u + 1)
                        for n in range(NB):
                            pe.wait_ge(s_out, 8 * i + 4 * u + n + 1)
                            block_products(n, u)
        return s_st


def fourier_phase(nc, f_d, t_pos, t_chan, yT_d):
    C1, C2, C3 = (math.cos(2 * math.pi * n / N1) for n in (1, 2, 3))
    GW = 2 * P * K1
    with Res(nc, "fft") as r:
        f = r.sb("f", [P, N1, FW])
        eo = r.sb("eo", [P, N1, FW])
        z_hi = r.sb("z_hi", [P, N1, FW], F32R)
        z_lo = r.sb("z_lo", [P, N1, FW], F32R)
        tp_st = r.sb("tp_st", [P, 3 * P])
        tp_hi = r.sb("tp_hi", [P, K1, 3 * P], F32R)
        tp_lo = r.sb("tp_lo", [P, K1, 3 * P], F32R)
        tc_st = r.sb("tc_st", [P, 3 * P])
        tc_hi = r.sb("tc_hi", [P, 3 * P], F32R)
        tc_lo = r.sb("tc_lo", [P, 3 * P], F32R)
        ps_g = r.ps("ps_g", [P, 2, 512])
        ps_y = r.ps("ps_y", [P, 5, 512])
        g_hi = r.sb("g_hi", [P, 2, K1, P], F32R)
        g_lo = r.sb("g_lo", [P, 2, K1, P], F32R)
        g_full = eo[:, 0:5, :].rearrange("p a c -> p (a c)")[:, 0:GW].rearrange("p (c k m) -> p c k m", c=2, k=K1)
        yT_flat = f[:, 0:4, :].rearrange("p a c -> p (a c)")
        yT = yT_flat.rearrange("p (k2 k1) -> p k1 k2", k1=N1)
        NBK = (K1 + 1) // 2
        PIECES = [(0, 3, False), (3, 3, False), (6, 3, False), (1, 4, True), (5, 3, True)]
        s_f, s_tc, s_tp, s_v, s_z, s_tabs, s_g, s_gev, s_gs, s_y, s_yev, s_out = (
            r.sem(n) for n in ("f", "tc", "tp", "v", "z", "tabs", "g", "gev", "gs", "y", "yev", "out"))
        z = f
        with r.block() as block:

            @block.sync
            def _(sp):
                sp.dma_start(f[:], f_d.rearrange("t p c -> p t c")).then_inc(s_f, 16)
                sp.dma_start(tc_st[:], t_chan).then_inc(s_tc, 16)
                for k in range(K1):
                    if k:
                        sp.wait_ge(s_tabs, 2 * k + 2)
                    sp.dma_start(tp_st[:], t_pos[k]).then_inc(s_tp, 16)
                for g in range(NG):
                    sp.wait_ge(s_yev, 5 * g + 5)
                    sp.dma_start(yT_d[g], yT_flat).then_inc(s_out, 16)
                sp.wait_ge(s_out, 16 * NG)

            @block.gpsimd
            def _(pool):
                n = 0

                def split(hi, lo, src):
                    nonlocal n
                    pool.tensor_copy(hi, src).then_inc(s_tabs, 1)
                    pool.wait_ge(s_tabs, n + 1)
                    pool.tensor_tensor(lo, src, hi, ALU.subtract).then_inc(s_tabs, 1)
                    n += 2

                pool.wait_ge(s_tc, 16)
                split(tc_hi[:], tc_lo[:], tc_st[:])
                for k in range(K1):
                    pool.wait_ge(s_tp, 16 * k + 16)
                    split(tp_hi[:, k, :], tp_lo[:, k, :], tp_st[:])

            @block.vector
            def _(dve):
                n = 0

                def step(ins):
                    nonlocal n
                    n += 1
                    ins.then_inc(s_v, 1)
                    dve.wait_ge(s_v, n)

                def add(o, a, b):
                    step(dve.tensor_tensor(o, a, b, ALU.add))

                def sub(o, a, b):
                    step(dve.tensor_tensor(o, a, b, ALU.subtract))

                def axpy(o, c, a, b, op=ALU.add):
                    step(dve.scalar_tensor_tensor(o, a, c, b, ALU.mult, op))

                dve.wait_ge(s_f, 16)
                add(eo[:, 0:8, :], f[:, 0:8, :], f[:, 8:16, :])
                sub(eo[:, 8:16, :], f[:, 0:8, :], f[:, 8:16, :])
                e, o = (lambda i: eo[:, i, :]), (lambda i: eo[:, 8 + i, :])
                re, im = (lambda k: z[:, k, :]), (lambda k: z[:, 8 + k, :])
                t = [z[:, i, :] for i in range(4)]
                add(z[:, 0:4, :], eo[:, 0:4, :], eo[:, 4:8, :])
                sub(eo[:, 0:4, :], eo[:, 0:4, :], eo[:, 4:8, :])
                add(e(4), t[0], t[2])
                add(e(5), t[1], t[3])
                sub(re(4), t[0], t[2])
                sub(im(4), t[3], t[1])
                add(re(0), e(4), e(5))
                sub(re(8), e(4), e(5))
                sub(e(4), e(1), e(3))
                add(e(5), e(1), e(3))
                axpy(re(2), C2, e(4), e(0))
                axpy(re(6), -C2, e(4), e(0))
                axpy(im(2), -C2, e(5), e(2), ALU.subtract)
                axpy(im(6), -C2, e(5), e(2))
                pq = [None] + [(e(n), e(3 + n)) for n in (1, 2, 3)]
                for j in (1, 2, 3):
                    sub(pq[j][0], o(j), o(8 - j))
                    add(pq[j][1], o(j), o(8 - j))
                (p1, q1), (p2, q2), (p3, q3) = pq[1:]
                u, v, w = o(1), o(2), o(3)
                axpy(u, C2, p2, o(0))
                axpy(v, -C2, p2, o(0))
                step(dve.tensor_scalar(w, p3, C3, None, ALU.mult))
                axpy(w, C1, p1, w)
                add(re(1), u, w)
                sub(re(7), u, w)
                step(dve.tensor_scalar(w, p3, C1, None, ALU.mult))
                axpy(w, C3, p1, w, ALU.subtract)
                add(re(3), v, w)
                sub(re(5), v, w)
                axpy(u, C2, q2, o(4))
                axpy(v, C2, q2, o(4), ALU.subtract)
                step(dve.tensor_scalar(w, q3, C1, None, ALU.mult))
                axpy(w, C3, q1, w)
                sub(im(7), u, w)
                add(w, u, w)
                step(dve.tensor_scalar(im(1), w, -1.0, None, ALU.mult))
                step(dve.tensor_scalar(w, q3, C3, None, ALU.mult))
                axpy(w, C1, q1, w, ALU.subtract)
                sub(im(5), v, w)
                add(w, v, w)
                step(dve.tensor_scalar(im(3), w, -1.0, None, ALU.mult))
                for h in range(4):
                    part = slice(4 * h, 4 * h + 4)
                    dve.tensor_copy(z_hi[:, part, :], z[:, part, :]).then_inc(s_z, 1)
                    dve.wait_ge(s_z, 2 * h + 1)
                    dve.tensor_tensor(z_lo[:, part, :], z[:, part, :], z_hi[:, part, :], ALU.subtract).then_inc(s_z, 1)
                dve.wait_ge(s_z, 8)
                for g in range(NG):
                    for b in range((K1 + 1) // 2):
                        m = min(2, K1 - 2 * b)
                        src = g_full[:, :, 2 * b:2 * b + m, :]
                        c = g * ((K1 + 1) // 2) + b
                        dve.wait_ge(s_gev, c + 1)
                        if g:
                            dve.wait_ge(s_y, 5 * g)
                        dve.tensor_copy(g_hi[:, :, 2 * b:2 * b + m, :], src).then_inc(s_gs, 1)
                        dve.wait_ge(s_gs, 2 * c + 1)
                        dve.tensor_tensor(g_lo[:, :, 2 * b:2 * b + m, :], src, g_hi[:, :, 2 * b:2 * b + m, :],
                                          ALU.subtract).then_inc(s_gs, 1)

            @block.scalar
            def _(act):
                act.wait_ge(s_z, 8)
                for g in range(NG):
                    for b in range(NBK):
                        c = g * NBK + b
                        m = min(2, K1 - 2 * b)
                        act.wait_ge(s_g, c + 1)
                        if g:
                            act.wait_ge(s_gs, 2 * (c - NBK) + 2)
                        act.activation(g_full[:, :, 2 * b:2 * b + m, :].rearrange("p c k m -> p k c m"),
                                       ps_g[:, c % 2, 0:m * 2 * P].rearrange("p (k c m) -> p k c m", k=m, c=2),
                                       ACT.Copy).then_inc(s_gev, 1)
                    if g:
                        act.wait_ge(s_out, 16 * g)
                    for j, (kk, m, mirrored) in enumerate(PIECES):
                        act.wait_ge(s_y, 5 * g + j + 1)
                        src = ps_y[:, j, 0:m * P].rearrange("p (k m) -> p k m", k=m)
                        dst = yT[:, kk:kk + m, :]
                        if mirrored:
                            dst = yT[:, N1 - kk - m + 1:N1 - kk + 1, :][:, ::-1, ::-1]
                        act.activation(dst, src, ACT.Copy).then_inc(s_yev, 1)

            @block.tensor
            def _(pe):
                pe.wait_ge(s_tabs, 2 + 2 * K1)
                pe.wait_ge(s_z, 8)
                for g in range(NG):
                    ch = slice(g * P, (g + 1) * P)
                    for b in range(NBK):
                        c = g * NBK + b
                        if c >= 2:
                            pe.wait_ge(s_gev, c - 1)
                        m = min(2, K1 - 2 * b)
                        for j in range(m):
                            k = 2 * b + j
                            at = ps_g[:, c % 2, j * 2 * P:(j + 1) * 2 * P]
                            imag = 0 < k < K1 - 1
                            q = product3(pe, at, z_hi[:, k, ch], z_lo[:, k, ch], tp_hi[:, k, P:3 * P],
                                         tp_lo[:, k, P:3 * P], True, not imag)
                            if imag:
                                q = product3(pe, at, z_hi[:, 8 + k, ch], z_lo[:, 8 + k, ch], tp_hi[:, k, 0:2 * P],
                                             tp_lo[:, k, 0:2 * P], False, True)
                        q.then_inc(s_g, 1)
                    pe.wait_ge(s_gs, 2 * NBK * (g + 1))
                    if g:
                        pe.wait_ge(s_yev, 5 * g)
                    for j, (kk, m, mirrored) in enumerate(PIECES):
                        sine = slice(2 * P, 3 * P) if mirrored else slice(P, 2 * P)
                        at = ps_y[:, j, 0:m * P]
                        product3(pe, at, tc_hi[:, 0:P], tc_lo[:, 0:P], g_hi[:, 0, kk:kk + m, :],
                                 g_lo[:, 0, kk:kk + m, :], True, False)
                        product3(pe, at, tc_hi[:, sine], tc_lo[:, sine], g_hi[:, 1, kk:kk + m, :],
                                 g_lo[:, 1, kk:kk + m, :], False, True).then_inc(s_y, 1)


def kv_phase(nc, qkv_d, ident, kv_d):
    with Res(nc, "kv") as r:
        k_st = r.sb("k_st", [P, NKV, S])
        v_st = r.sb("v_st", [P, S])
        kv = r.sb("kv", [P, NKV, 3, S], F32R)
        ps = r.ps("ps", [P, 4, 512])
        s_k, s_v, s_hi, s_kd, s_z, s_tr, s_vhi, s_vd, s_out = (
            r.sem(n) for n in ("k", "v", "khi", "kd", "zero", "tr", "vhi", "vd", "out"))
        with r.block() as block:

            @block.sync
            def _(sp):
                sp.dma_start(v_st[:], qkv_d[NQC + 1]).then_inc(s_v, 16)
                for g in range(NKV):
                    for half in range(2):
                        sp.dma_start(k_st[half * HD:(half + 1) * HD, g, :], qkv_d[NQC, g * HD:(g + 1) * HD, :])\
                            .then_inc(s_k, 16)
                sp.wait_ge(s_kd, NKV)
                sp.wait_ge(s_vd, 8)
                sp.dma_start(kv_d.rearrange("g p a s -> p g a s"), kv[:].bitcast(F32)).then_inc(s_out, 16)
                sp.wait_ge(s_out, 16)

            @block.tensor
            def _(pe):
                pe.wait_ge(s_v, 16)
                for t in range(NT):
                    m = pe.transpose(ps[:, t // 4, (t % 4) * P:(t % 4 + 1) * P], v_st[:, t * P:(t + 1) * P], ident[:])
                    if t % 4 == 3:
                        m.then_inc(s_tr, 1)

            @block.vector
            def _(dve):
                vv = kv[:, :, 2, :].rearrange("p g (t c) -> p g t c", c=P)
                for b in range(4):
                    src = ps[:, b, :].rearrange("p (t g d) -> p g t d", g=NKV, d=HD)
                    dve.wait_ge(s_tr, b + 1)
                    for g in range(NKV):
                        hi, lo = (vv[:, g, 4 * b:4 * b + 4, j * HD:(j + 1) * HD] for j in range(2))
                        dve.tensor_copy(hi, src[:, g]).then_inc(s_vhi, 1)
                        dve.wait_ge(s_vhi, 2 * b + g + 1)
                        dve.tensor_tensor(lo, src[:, g], hi, ALU.subtract).then_inc(s_vd, 1)
                dve.wait_ge(s_k, 64)
                for g in range(NKV):
                    dve.tensor_copy(kv[:, g, 1, :], k_st[:, g, :]).then_inc(s_hi, 1)
                    dve.tensor_copy(kv[0:HD, g, 0, :], k_st[0:HD, g, :]).then_inc(s_hi, 1)
                    dve.wait_ge(s_hi, 3 * g + 2)
                    dve.tensor_tensor(kv[HD:P, g, 0, :], k_st[HD:P, g, :], kv[HD:P, g, 1, :], ALU.subtract)\
                        .then_inc(s_hi, 1)
                    dve.wait_ge(s_hi, 3 * g + 3)
                    dve.memset(kv[HD:P, g, 1, :].bitcast(F32), 0.0).then_inc(s_z, 1)
                    dve.wait_ge(s_z, g + 1)
                    dve.memset(kv[HD:HD + 1, g, 1, :].bitcast(F32), 1.0).then_inc(s_kd, 1)


def attention_phase(nc, qkv_d, kv_d, ident, ones, o_d):
    KP = NT // 2
    ST = NB * KP
    LAG = 3
    FIRST, LAST = 3, 28
    subs = [[] for _ in range(ST)]
    for m in range(2 * NT):
        subs[FIRST + m * (LAST - FIRST) // (2 * NT)].append(m)
    SCALE = HD ** -0.5
    with Res(nc, "att") as r:
        kv = [r.sb(f"kv{i}", [P, 3, S], F32R) for i in range(2)]
        kmax = r.sb("kmax", [P, NKV, S], F32R)
        q_st = r.sb("q_st", [P, S])
        q1 = [r.sb(f"q1_{i}", [P, S], F32R) for i in range(2)]
        q2 = [r.sb(f"q2_{i}", [P, S], F32R) for i in range(2)]
        prob = r.sb("prob", [P, 8, 2 * BLK])
        prob_hi = r.sb("prob_hi", [P, 4, 2 * BLK], F32R)
        prob_lo = r.sb("prob_lo", [P, 4, 2 * BLK], F32R)
        acc = r.sb("acc", [P, 2, 2 * BLK])
        o_sb = r.sb("o_sb", [P, 2, BLK])
        rec = r.sb("rec", [P, BLK])
        mx = r.sb("mx", [P, 2 * NT])
        mx2 = r.sb("mx2", [P, NT])
        mrow = r.sb("mrow", [NT, P], F32R)
        ps_s = r.ps("ps_s", [P, 2, 2 * BLK])
        ps_m = r.ps("ps_m", [P, 2 * BLK])
        ps_o = r.ps("ps_o", [P, BLK])
        ps_r = r.ps("ps_r", [P, BLK])
        s_q, s_km = r.sem("q_loaded"), r.sem("kmax_loaded")
        s_kv = [r.sem(f"kv_loaded{i}") for i in range(2)]
        s_zero, s_q1, s_q2, s_s, s_exp, s_hi, s_lo, s_pv = (
            r.sem(n) for n in ("zeroed", "q1_made", "q2_made", "scores", "exp", "p_hi", "p_lo", "pv"))
        s_add, s_sum, s_rec, s_oc, s_on = (r.sem(n) for n in ("added", "sum", "reciprocal", "o_copied", "o_scaled"))
        s_m, s_mr, s_m2, s_mt, s_mc = (r.sem(n) for n in ("max_scores", "max_read", "max_of_row", "max_turned", "max_row"))
        s_row = [r.sem(f"row_placed{i}") for i in range(2)]
        s_st = [r.sem(f"o_stored{i}") for i in range(2)]
        with r.block() as block:

            @block.sync
            def _(sp):
                def load_q(h):
                    chunk = h // 2
                    for half in range(2):
                        src = qkv_d[chunk, (h % 2) * HD:(h % 2 + 1) * HD, :]
                        sp.dma_start(q_st[half * HD:(half + 1) * HD, :], src).then_inc(s_q, 16)

                def place_row(h, u):
                    sp.wait_ge(s_mc, h + 1)
                    sp.dma_start(q2[u][HD:HD + 1, :].bitcast(F32), mrow[:].bitcast(F32)).then_inc(s_row[u], 16)

                for g in range(NKV):
                    sp.dma_start(kmax[:, g, :].bitcast(F32), kv_d[g, :, 0, :]).then_inc(s_km, 16)
                load_q(0)
                sp.dma_start(kv[0][:].bitcast(F32), kv_d[0]).then_inc(s_kv[0], 16)
                sp.wait_ge(s_q2, NB)
                load_q(1)
                place_row(0, 0)

                def store(h, qb, first=False):
                    sp.wait_ge(s_on, NB * h + qb + 1)
                    at = o_d[:, bass.ds(h, 1), :, qb * BLK:(qb + 1) * BLK]
                    for half in range(2):
                        sp.dma_start(at[half:half + 1].rearrange("a h d q -> (a h d) q"),
                                     o_sb[half * HD:(half + 1) * HD, qb % 2, :]).then_inc(s_st[qb % 2], 16)

                def body(h, u, load_kv, more_q, is_first, has_next):
                    if has_next:
                        if not is_first:
                            sp.wait_ge(s_pv, ST * h)
                        load_kv()
                    if not is_first:
                        store(h - 1, NB - 1)
                    if more_q:
                        sp.wait_ge(s_q2, NB * (h + 2))
                        more_q()
                    for qb in range(NB - 1):
                        store(h, qb)
                    if has_next:
                        place_row(h + 1, 1 - u)

                for h in range(NH):
                    body(h, h % 2,
                         lambda: sp.dma_start(kv[(h + 1) % 2][:].bitcast(F32), kv_d[(h + 1) * NKV // NH]).then_inc(s_kv[(h + 1) % 2], 16),
                         (lambda: load_q(h + 2)) if h + 2 < NH else None, h == 0, h + 1 < NH)
                store(NH - 1, NB - 1)
                for i in range(2):
                    sp.wait_ge(s_st[i], 16 * NH * NB)

            @block.scalar
            def _(act):
                def exp(h, s):
                    g = ST * h + s
                    act.wait_ge(s_s, g + 1)
                    if not isinstance(g, int) or g >= 8:
                        act.wait_ge(s_lo, g - 7)
                        old = s - 8
                        act.wait_ge(s_add, ST * h + (old // KP) * KP + max(old % KP, 1))
                    act.activation(prob[:, s % 8, :], ps_s[:, s % 2, :], ACT.Exp, scale=SCALE).then_inc(s_exp, 1)

                def hi(h, s):
                    g = ST * h + s
                    act.wait_ge(s_exp, g + 1)
                    if not isinstance(g, int) or g >= 4:
                        act.wait_ge(s_pv, g - 3)
                    act.activation(prob_hi[:, s % 4, :], prob[:, s % 8, :], ACT.Copy).then_inc(s_hi, 1)

                def o_copy(h, qb):
                    n = NB * h + qb
                    act.wait_ge(s_pv, KP * (n + 1))
                    if not isinstance(n, int) or n >= 2:
                        act.wait_ge(s_st[qb % 2], 32 * (NB // 2 * h + qb // 2))
                    act.activation(o_sb[:, qb % 2, :], ps_o[:], ACT.Copy).then_inc(s_oc, 1)

                def body(h, first_head):
                    for s in range(ST):
                        exp(h, s)
                        if s % KP == LAG - 1 and not (first_head and s < KP):
                            o_copy(*((h, s // KP - 1) if s >= KP else (h - 1, NB - 1)))
                        if s:
                            hi(h, s - 1)
                        elif not first_head:
                            hi(h - 1, ST - 1)

                body(0, True)
                with act.Fori(1, NH) as h:
                    body(h, False)
                hi(NH - 1, ST - 1)
                o_copy(NH - 1, NB - 1)

            @block.gpsimd
            def _(pool):
                def body(h, first_head):
                    for qb in range(NB):
                        for kp in range(1, KP):
                            s = qb * KP + kp
                            n = ST * h + qb * KP
                            pool.wait_ge(s_exp, ST * h + s + 1)
                            if kp == 1:
                                if not (first_head and qb < 2):
                                    pool.wait_ge(s_sum, NB * h + qb - 1)
                                pool.tensor_tensor(acc[:, qb % 2, :], prob[:, (s - 1) % 8, :], prob[:, s % 8, :],
                                                   ALU.add).then_inc(s_add, 1)
                            else:
                                pool.wait_ge(s_add, n + kp - 1)
                                pool.tensor_tensor(acc[:, qb % 2, :], acc[:, qb % 2, :], prob[:, s % 8, :],
                                                   ALU.add).then_inc(s_add, 1)
                        pool.wait_ge(s_add, n + KP - 1)
                        pool.tensor_tensor(acc[:, qb % 2, 0:BLK], acc[:, qb % 2, 0:BLK], acc[:, qb % 2, BLK:2 * BLK],
                                           ALU.add).then_inc(s_add, 1)

                body(0, True)
                with pool.Fori(1, NH) as h:
                    body(h, False)

            @block.vector
            def _(dve):
                def split_q(h, u, piece):
                    cols = slice(piece * BLK, (piece + 1) * BLK)
                    dve.tensor_copy(q1[u][:, cols], q_st[:, cols]).then_inc(s_q1, 1)
                    dve.wait_ge(s_q1, NB * h + piece + 1)
                    dve.tensor_tensor(q2[u][0:HD, cols], q_st[0:HD, cols], q1[u][0:HD, cols], ALU.subtract)\
                        .then_inc(s_q2, 1)

                def read_max(h, m):
                    dve.wait_ge(s_m, 2 * NT * h + m + 1)
                    dve.tensor_reduce(mx[:, m:m + 1], ps_m[:], AX.X, ALU.max).then_inc(s_mr, 1)

                def row_max(h):
                    dve.wait_ge(s_mr, 2 * NT * (h + 1))
                    dve.tensor_reduce(mx2[:], mx[:].rearrange("p (t a) -> p t a", a=2), AX.X, ALU.max).then_inc(s_m2, 1)

                def row_copy(h, first):
                    dve.wait_ge(s_mt, h + 1)
                    if not first:
                        row_before(h)
                    dve.tensor_scalar(mrow[:], ps_r[0:NT, 0:P], -1.0, None, ALU.mult).then_inc(s_mc, 1)

                def row_before(h):
                    dve.wait_ge(s_s, ST * (h - 1) + 1)

                def lo(h, s):
                    dve.wait_ge(s_hi, ST * h + s + 1)
                    dve.tensor_tensor(prob_lo[:, s % 4, :], prob[:, s % 8, :], prob_hi[:, s % 4, :], ALU.subtract)\
                        .then_inc(s_lo, 1)

                def scale_o(h, qb):
                    n = NB * h + qb
                    dve.wait_ge(s_sum, n + 1)
                    dve.reciprocal(rec[:], ps_r[:]).then_inc(s_rec, 1)
                    dve.wait_ge(s_rec, n + 1)
                    dve.wait_ge(s_oc, n + 1)
                    dve.tensor_tensor(o_sb[:, qb % 2, :], o_sb[:, qb % 2, :], rec[:], ALU.mult).then_inc(s_on, 1)

                def body(h, u, first_head, has_next):
                    for s in range(ST):
                        if has_next and s < 2:
                            if s == 0:
                                dve.wait_ge(s_q, 32 * (h + 2))
                                if not first_head:
                                    dve.wait_ge(s_s, ST * h)
                            for piece in (2 * s, 2 * s + 1):
                                split_q(h + 1, 1 - u, piece)
                        if has_next:
                            for m in subs[s]:
                                read_max(h + 1, m)
                            if s == LAST:
                                row_max(h + 1)
                            if s == LAST + 2:
                                row_copy(h + 1, False)
                        if s:
                            lo(h, s - 1)
                        elif not first_head:
                            lo(h - 1, ST - 1)
                        if s % KP == LAG + 1 and not (first_head and s < KP):
                            scale_o(*((h, s // KP - 1) if s >= KP else (h - 1, NB - 1)))

                for u in range(2):
                    dve.memset(q2[u][HD:P, :].bitcast(F32), 0.0).then_inc(s_zero, 1)
                dve.wait_ge(s_q, 32)
                for piece in range(NB):
                    split_q(0, 0, piece)
                for m in range(2 * NT):
                    read_max(0, m)
                row_max(0)
                dve.wait_ge(s_zero, 2)
                row_copy(0, True)
                body(0, 0, True, True)
                body(1, 1, False, True)
                with dve.Fori(1, NH // 2 - 1) as i:
                    for u in range(2):
                        body(2 * i + u, u, False, True)
                body(NH - 2, 0, False, True)
                body(NH - 1, 1, False, False)
                lo(NH - 1, ST - 1)
                scale_o(NH - 1, NB - 1)

            @block.tensor
            def _(pe):
                def scores(h, u, s):
                    g = ST * h + s
                    qb, kp = divmod(s, KP)
                    cols = slice(qb * BLK, (qb + 1) * BLK)
                    if not isinstance(g, int) or g >= 2:
                        pe.wait_ge(s_exp, g - 1)
                    for j in range(2):
                        keys = slice((2 * kp + j) * P, (2 * kp + j + 1) * P)
                        at = ps_s[:, s % 2, j * BLK:(j + 1) * BLK]
                        pe.matmul(at, kv[u][:, 0, keys], q1[u][:, cols], start=True, stop=False)
                        m = pe.matmul(at, kv[u][:, 1, keys], q2[u][:, cols], start=False, stop=True)
                    m.then_inc(s_s, 1)

                def maxima(h, u, m, g):
                    tile, half = divmod(m, 2)
                    if half == 0 and tile % 4 == 0:
                        pe.wait_ge(s_q1, NB * h + tile // 4 + 1)
                    if not isinstance(h, int) or h or m:
                        pe.wait_ge(s_mr, 2 * NT * h + m)
                    for j in range(2):
                        keys = slice((2 * half + j) * BLK, (2 * half + j + 1) * BLK)
                        q = pe.matmul(ps_m[:, j * BLK:(j + 1) * BLK], q1[u][:, tile * P:(tile + 1) * P],
                                      kmax[:, g, keys], start=True, stop=True)
                    q.then_inc(s_m, 1)

                def turn_max(h):
                    pe.wait_ge(s_m2, h + 1)
                    if not isinstance(h, int) or h:
                        pe.wait_ge(s_rec, NB * (h - 1) + NB - 1)
                    pe.transpose(ps_r[0:NT, 0:P], mx2[:], ident[:]).then_inc(s_mt, 1)

                def pv(h, u, s):
                    qb, kp = divmod(s, KP)
                    pe.wait_ge(s_lo, ST * h + s + 1)
                    if kp == 0 and (not isinstance(h, int) or h or qb):
                        pe.wait_ge(s_oc, NB * h + qb)
                    for j in range(2):
                        t = 2 * kp + j
                        v = kv[u][:, 2, t * P:(t + 1) * P]
                        for part, src in enumerate((prob_hi, prob_lo)):
                            m = pe.matmul(ps_o[:], v, src[:, s % 4, j * BLK:(j + 1) * BLK],
                                          start=t == 0 and part == 0, stop=t == NT - 1 and part == 1)
                    m.then_inc(s_pv, 1)

                def row_sum(h, qb):
                    n = NB * h + qb
                    pe.wait_ge(s_add, KP * (n + 1))
                    if not isinstance(n, int) or n:
                        pe.wait_ge(s_rec, n)
                    if qb == NB - 1 and not (isinstance(h, int) and h == NH - 1):
                        pe.wait_ge(s_mc, h + 2)
                    elif qb == 0:
                        pe.wait_ge(s_mc, h + 1)
                    pe.matmul(ps_r[:], ones[:], acc[:, qb % 2, 0:BLK], start=True, stop=True).then_inc(s_sum, 1)

                def body(i, u, has_next, first_head=False):
                    h = 2 * i + u
                    pe.wait_ge(s_kv[u], 16 * i + 16)
                    pe.wait_ge(s_row[u], 16 * i + 16)
                    pe.wait_ge(s_q2, NB * (h + 1))
                    for s in range(ST):
                        scores(h, u, s)
                        if has_next:
                            g = ((h + 1) * NKV // NH) if isinstance(h, int) else bass.ds((h + 1) // (NH // NKV), 1)
                            for m in subs[s]:
                                maxima(h + 1, 1 - u, m, g)
                            if s == LAST + 1:
                                turn_max(h + 1)
                        if s >= LAG:
                            pv(h, u, s - LAG)
                        elif not first_head:
                            pv(h - 1, 1 - u, ST + s - LAG)
                        if s % KP == LAG and not (first_head and s < KP):
                            row_sum(*((h, s // KP - 1) if s >= KP else (h - 1, NB - 1)))

                pe.wait_ge(s_km, 16 * NKV)
                for m in range(2 * NT):
                    maxima(0, 0, m, 0)
                turn_max(0)
                body(0, 0, True, True)
                body(0, 1, True)
                with pe.Fori(1, NH // 2 - 1) as i:
                    for u in range(2):
                        body(i, u, True)
                body(NH // 2 - 1, 0, True)
                body(NH // 2 - 1, 1, False)
                for s in range(ST - LAG, ST):
                    pv(NH - 1, 1, s)
                row_sum(NH - 1, NB - 1)


def merge_phase(nc, x_d, w_branch, w_out_d, o_d, yT_d, gates_d, gate_rows, x1_d, first_sem, kept):
    TB = BLK // P
    KB = NQC
    with Res(nc, "merge") as r:
        w_st = r.sb("w_st", [P, 2, D])
        wb_hi, wb_lo = (r.sb(n, [P, 2, KD, P], F32R) for n in ("wb_hi", "wb_lo"))
        wo_hi, wo_lo = (r.sb(n, [P, KD, D], F32R) for n in ("wo_hi", "wo_lo"))
        st_a, st_b = (r.sb(n, [P, KB, BLK]) for n in ("st_a", "st_b"))
        act_hi, act_lo = (r.sb(n, [P, KD, BLK], F32R) for n in ("act_hi", "act_lo"))
        mg_hi, mg_lo = (r.sb(n, [P, KD, BLK], F32R) for n in ("mg_hi", "mg_lo"))
        gate = r.sb("gate", [P, 2, 2, BLK])
        g1 = r.sb("g1", [P, D])
        x = r.sb("x", [P, 2, D])
        x1 = r.sb("x1", [P, 2, D])
        junk = r.sb("junk", [P, D], mybir.dt.bfloat16)
        sums, mean, std, rstd = (r.sb(n, [P, 2]) for n in ("sums", "mean", "std", "rstd"))
        ps_b = r.ps("ps_b", [P, 2, 2, BLK])
        ps_y = r.ps("ps_y", [P, 2, D])
        s_w = [r.sem(f"w_loaded{i}") for i in range(2)]
        s_gate = [r.sem(f"gates_loaded{i}") for i in range(2)]
        s_x = [r.sem(f"x_loaded{i}") for i in range(2)]
        s_st = [r.pool_dma_sem(f"x1_stored{i}") for i in range(2)]
        s_o, s_yt, s_g1 = r.sem("o_loaded"), r.sem("yT_loaded"), r.sem("g1_loaded")
        s_whi, s_wlo, s_act, s_br, s_mg, s_y = (
            r.sem(n) for n in ("w_hi_made", "w_lo_made", "act_steps", "branch", "merge_steps", "y"))
        s_sq, s_mean, s_std, s_rstd, s_n1, s_x1 = (r.sem(n) for n in ("squares", "mean", "root", "rstd", "scaled", "x1"))
        with r.block() as block:

            @block.sync
            def _(sp):
                def load_w(src, i, u, first):
                    if not first:
                        sp.wait_ge(s_wlo, 2 * i + u - 1)
                    sp.dma_start(w_st[:, u, :], src).then_inc(s_w[u], 16)

                def load_o(b):
                    cols = bass.ds(b * BLK, BLK)
                    if not isinstance(b, int) or b:
                        sp.wait_ge(s_act, 6 * b)
                    for half, dst in ((0, st_a), (1, st_b)):
                        for t in range(2):
                            src = o_d[half].rearrange("(c t) d s -> t d c s", t=2)[t][:, :, cols]
                            sp.dma_start(dst[t * HD:(t + 1) * HD, :, :], src).then_inc(s_o, 16)

                def load_y(b):
                    sp.wait_ge(s_act, 6 * b + 1)
                    sp.dma_start(st_b[:], yT_d.rearrange("g c s -> c g s")[:, :, bass.ds(b * BLK, BLK)])\
                        .then_inc(s_yt, 16)

                def body(b, last):
                    for m in range(KD):
                        if m >= 2:
                            load_w(w_branch[m], KD // 2 * (b + 1) + m // 2, m % 2, False)
                        if m >= 2 or not isinstance(b, int) or b:
                            sp.wait_ge(s_mg, 5 * (KD * b + m - 1))
                        for j in range(2):
                            at = gates_d[bass.ds(b, 1), 2 * m + j, :, :].rearrange("o p s -> (o p) s")
                            sp.dma_start(gate[:, m % 2, j, :], at).then_inc(s_gate[m % 2], 16)
                    if not last:
                        load_o(b + 1)
                        for u in range(2):
                            load_w(w_branch[u], KD // 2 * (b + 2), u, False)
                    for j in range(TB):
                        n = TB * b + j
                        if j >= 2 or not isinstance(b, int) or b:
                            sp.wait_ge(s_x1, n - 1)
                        sp.dma_start(x[:, j % 2, :], x_d[bass.ds(n, 1), :, :].rearrange("o p d -> (o p) d"))\
                            .then_inc(s_x[j % 2], 16)
                        if j == 0 and not last:
                            load_y(b + 1)
                sp.sem_clear(range(first_sem, kept[0].num))
                sp.sem_clear(range(kept[-1].num + 1, min(r.sem_nums)))
                sp.dma_start(g1[:], gate_rows).then_inc(s_g1, 16)
                for k in range(KD):
                    load_w(w_out_d[k], k // 2, k % 2, k < 2)
                load_o(0)
                for m in range(2):
                    load_w(w_branch[m], KD // 2, m, False)
                load_y(0)
                body(0, False)
                with sp.Fori(1, NB - 1) as b:
                    body(b, False)
                body(NB - 1, True)

            @block.gpsimd
            def _(pool):
                with pool.Fori(0, NB) as b:
                    for j in range(TB):
                        pool.wait_ge(s_x1, TB * b + j + 1)
                        pool.dma_start(x1_d[bass.ds(TB * b + j, 1), :, :].rearrange("o p d -> (o p) d"), x1[:, j % 2, :])\
                            .then_inc(s_st[j % 2], 16)
                for i in range(2):
                    pool.wait_ge(s_st[i], 16 * NT // 2)

            @block.scalar
            def _(act):
                def hi_part(dst, i, u):
                    act.wait_ge(s_w[u], 16 * i + 16)
                    act.activation(dst, w_st[:, u, :], ACT.Copy).then_inc(s_whi, 1)

                def branch_hi(b, m):
                    if m >= 2 or not isinstance(b, int) or b:
                        act.wait_ge(s_br, KD * b + m - 1)
                    hi_part(wb_hi[:, m % 2, :, :].rearrange("p k m -> p (k m)"), KD // 2 * (b + 1) + m // 2, m % 2)

                def body(b, last):
                    for m in range(KD):
                        if m < KD - 1:
                            branch_hi(b, m + 1)
                        elif not last:
                            branch_hi(b + 1, 0)
                    for j in range(TB):
                        n = TB * b + j
                        act.wait_ge(s_y, n + 1)
                        if j or not isinstance(b, int) or b:
                            act.wait_ge(s_sq, n)
                        act.activation(junk[:], ps_y[:, j % 2, :], ACT.Square, accum_out=sums[:, j % 2:j % 2 + 1])\
                            .then_inc(s_sq, 1)
                        act.wait_ge(s_mean, n + 1)
                        act.activation(std[:, j % 2:j % 2 + 1], mean[:, j % 2:j % 2 + 1], ACT.Sqrt).then_inc(s_std, 1)

                for k in range(KD):
                    hi_part(wo_hi[:, k, :], k // 2, k % 2)
                branch_hi(0, 0)
                body(0, False)
                with act.Fori(1, NB - 1) as b:
                    body(b, False)
                body(NB - 1, True)

            @block.vector
            def _(dve):
                def branch_lo(b, m):
                    piece = KD * (b + 1) + m
                    dve.wait_ge(s_whi, piece + 1)
                    dve.tensor_tensor(wb_lo[:, m % 2, :, :].rearrange("p k m -> p (k m)"), w_st[:, m % 2, :],
                                      wb_hi[:, m % 2, :, :].rearrange("p k m -> p (k m)"), ALU.subtract).then_inc(s_wlo, 1)

                def split_acts(b):
                    n = 6 * b
                    dve.wait_ge(s_o, 64 * (b + 1))
                    if not isinstance(b, int) or b:
                        dve.wait_ge(s_br, KD * b)
                    dve.tensor_tensor(st_a[:], st_a[:], st_b[:], ALU.add).then_inc(s_act, 1)
                    dve.wait_ge(s_act, n + 1)
                    dve.tensor_copy(act_hi[:, 0:KB, :], st_a[:]).then_inc(s_act, 1)
                    dve.wait_ge(s_act, n + 2)
                    dve.tensor_tensor(act_lo[:, 0:KB, :], st_a[:], act_hi[:, 0:KB, :], ALU.subtract).then_inc(s_act, 1)
                    dve.wait_ge(s_yt, 16 * (b + 1))
                    dve.tensor_copy(act_hi[:, KB:KD, :], st_b[:]).then_inc(s_act, 1)
                    dve.wait_ge(s_act, n + 4)
                    dve.tensor_tensor(act_lo[:, KB:KD, :], st_b[:], act_hi[:, KB:KD, :], ALU.subtract).then_inc(s_act, 2)

                def merge(b, m):
                    n = 5 * (KD * b + m)
                    dve.wait_ge(s_gate[m % 2], 32 * (KD // 2 * b + m // 2 + 1))
                    dve.wait_ge(s_br, KD * b + m + 1)
                    if m == 0 and (not isinstance(b, int) or b):
                        dve.wait_ge(s_y, TB * b)
                    ga, gf = gate[:, m % 2, 0, :], gate[:, m % 2, 1, :]
                    dve.tensor_tensor(ga, ps_b[:, m % 2, 0, :], ga, ALU.mult).then_inc(s_mg, 1)
                    dve.tensor_tensor(gf, ps_b[:, m % 2, 1, :], gf, ALU.mult).then_inc(s_mg, 1)
                    dve.wait_ge(s_mg, n + 2)
                    dve.tensor_tensor(ga, ga, gf, ALU.add).then_inc(s_mg, 1)
                    dve.wait_ge(s_mg, n + 3)
                    dve.tensor_copy(mg_hi[:, m, :], ga).then_inc(s_mg, 1)
                    dve.wait_ge(s_mg, n + 4)
                    dve.tensor_tensor(mg_lo[:, m, :], ga, mg_hi[:, m, :], ALU.subtract).then_inc(s_mg, 1)

                def body(b, last):
                    for m in range(KD):
                        if m < KD - 1:
                            branch_lo(b, m + 1)
                        elif not last:
                            branch_lo(b + 1, 0)
                        merge(b, m)
                    if not last:
                        split_acts(b + 1)
                    for j in range(TB):
                        n = TB * b + j
                        u = j % 2
                        dve.wait_ge(s_sq, n + 1)
                        dve.tensor_scalar(mean[:, u:u + 1], sums[:, u:u + 1], 1.0 / D, EPS, ALU.mult, ALU.add)\
                            .then_inc(s_mean, 1)
                        dve.wait_ge(s_std, n + 1)
                        dve.reciprocal(rstd[:, u:u + 1], std[:, u:u + 1]).then_inc(s_rstd, 1)
                        dve.wait_ge(s_rstd, n + 1)
                        if j >= 2 or not isinstance(b, int) or b:
                            dve.wait_ge(s_st[u], 16 * (TB // 2 * b + j // 2))
                        dve.scalar_tensor_tensor(x1[:, u, :], ps_y[:, u, :], rstd[:, u:u + 1], g1[:], ALU.mult, ALU.mult)\
                            .then_inc(s_n1, 1)
                        dve.wait_ge(s_n1, n + 1)
                        dve.wait_ge(s_x[u], 16 * (TB // 2 * b + j // 2 + 1))
                        dve.tensor_tensor(x1[:, u, :], x1[:, u, :], x[:, u, :], ALU.add).then_inc(s_x1, 1)

                for k in range(KD):
                    dve.wait_ge(s_whi, k + 1)
                    dve.tensor_tensor(wo_lo[:, k, :], w_st[:, k % 2, :], wo_hi[:, k, :], ALU.subtract).then_inc(s_wlo, 1)
                branch_lo(0, 0)
                split_acts(0)
                dve.wait_ge(s_g1, 16)
                body(0, False)
                with dve.Fori(1, NB - 1) as b:
                    body(b, False)
                body(NB - 1, True)

            @block.tensor
            def _(pe):
                def body(b):
                    pe.wait_ge(s_act, 6 * (b + 1))
                    for m in range(KD):
                        u = m % 2
                        pe.wait_ge(s_wlo, KD * (b + 1) + m + 1)
                        if m >= 2 or not isinstance(b, int) or b:
                            pe.wait_ge(s_mg, 5 * (KD * b + m - 1))
                        for branch in range(2):
                            for k in range(KB):
                                kk = branch * KB + k
                                q = product3(pe, ps_b[:, u, branch, :], wb_hi[:, u, kk, :], wb_lo[:, u, kk, :],
                                             act_hi[:, kk, :], act_lo[:, kk, :], k == 0, k == KB - 1)
                        q.then_inc(s_br, 1)
                    for j in range(TB):
                        rows = slice(j * P, (j + 1) * P)
                        if j >= 2 or not isinstance(b, int) or b:
                            pe.wait_ge(s_n1, TB * b + j - 1)
                        for n in range(2):
                            cols = slice(n * BLK, (n + 1) * BLK)
                            for k in range(KD):
                                if j == 0 and n == 0:
                                    pe.wait_ge(s_mg, 5 * (KD * b + k + 1))
                                q = product3(pe, ps_y[:, j % 2, cols], mg_hi[:, k, rows], mg_lo[:, k, rows],
                                             wo_hi[:, k, cols], wo_lo[:, k, cols], k == 0, k == KD - 1)
                        q.then_inc(s_y, 1)

                body(0)
                with pe.Fori(1, NB) as b:
                    body(b)


def ffn_phase(nc, half, h_hi, h_lo, w_up, w_dn, conv, gate_rows, carry, gc_hi, gc_lo, x1_d, out_d):
    NCV = HALF + 1
    G0 = P - 1
    tiles = NT // 2 - 1 if half == 0 else NT // 2 + 1
    t0 = 0 if half == 0 else NT // 2 - 1
    off = P if half == 0 else 0
    with Res(nc, f"ffn{half}") as r:
        w_st = r.sb("w_st", [P, 2, D])
        wu_hi, wu_lo = (r.sb(n, [P, 2, KD, P], F32R) for n in ("wu_hi", "wu_lo"))
        wd_st = r.sb("wd_st", [P, D])
        wd_hi, wd_lo = (r.sb(n, [P, 2, D], F32R) for n in ("wd_hi", "wd_lo"))
        u = r.sb("u", [P, 2, HALF + 3])
        cv = r.sb("cv", [P, 2, NCV])
        g_hi, g_lo = (r.sb(n, [P, 2, HALF + P], F32R) for n in ("g_hi", "g_lo"))
        y = r.sb("y", [P, tiles, D])
        cw = r.sb("cw", [P, 2 * NP, 4])
        sums, mean, std, rstd = (r.sb(n, [P, tiles]) for n in ("sums", "mean", "std", "rstd"))
        ps_u = r.ps("ps_u", [P, 2, 2, BLK])
        ps_d = r.ps("ps_d", [P, 2, D])
        s_w = [r.sem(f"wu_loaded{i}") for i in range(2)]
        s_x = [r.sem(f"x_loaded{i}") for i in range(2)]
        s_st = [r.pool_dma_sem(f"out_stored{i}") for i in range(2)]
        s_cw, s_wd, s_init, s_g2 = (r.sem(n) for n in ("conv_loaded", "wd_loaded", "init", "g2_loaded"))
        s_whi, s_wlo, s_dhi, s_dlo = (r.sem(n) for n in ("wu_hi_made", "wu_lo_made", "wd_hi_made", "wd_lo_made"))
        s_up, s_u, s_cs, s_cd, s_ge, s_g, s_ghi, s_glo, s_gc = (
            r.sem(n) for n in ("up", "u_copied", "conv_steps", "conv", "gelu", "g", "g_hi_made", "g_lo_made", "g_carry"))
        s_dn, s_y, s_sq, s_mean, s_std, s_rstd, s_n, s_o = (
            r.sem(n) for n in ("down", "y_added", "squares", "mean", "root", "rstd", "scaled", "out"))
        CS = 8
        with r.block() as block:

            @block.sync
            def _(sp):
                def load_up(p, j, first=False):
                    if not first:
                        sp.wait_ge(s_wlo, 2 * p + j - 1)
                    sp.dma_start(w_st[:, j:j + 1, :], w_up[bass.ds(2 * p + j, 1), :, :].rearrange("o p d -> p o d"))\
                        .then_inc(s_w[j], 16)

                def load_dn(p, first=False):
                    if not first:
                        sp.wait_ge(s_dlo, p)
                    sp.dma_start(wd_st[:], w_dn[bass.ds(p, 1), :, :].rearrange("o p d -> (o p) d")).then_inc(s_wd, 16)

                load_up(0, 0, True)
                load_up(0, 1, True)
                sp.dma_start(cw[:], conv).then_inc(s_cw, 16)
                load_dn(0, True)
                with sp.Fori(0, NP - 1) as p:
                    load_up(p + 1, 0)
                    load_up(p + 1, 1)
                    load_dn(p + 1)
                sp.wait_ge(s_dlo, NP)
                sp.dma_start(wd_st[:], gate_rows).then_inc(s_g2, 16)
                sp.wait_ge(s_glo, NP)
                for t in range(tiles):
                    if t >= 2:
                        sp.wait_ge(s_o, t - 1)
                    sp.dma_start(cv[:, t % 2, 0:D], x1_d[t0 + t]).then_inc(s_x[t % 2], 16)

            @block.gpsimd
            def _(pool):
                pool.memset(y[:], 0.0).then_inc(s_init, 1)
                pool.memset(u[:, :, 0:2], 0.0).then_inc(s_init, 1)
                pool.memset(u[:, :, HALF + 2:HALF + 3], 0.0).then_inc(s_init, 1)

                def kept_columns(p, v):
                    if half == 0:
                        pool.wait_ge(s_glo, p + 1)
                    elif not isinstance(p, int):
                        pool.wait_ge(s_dn, tiles * (p - 1))
                    for kept, whole in ((gc_hi, g_hi), (gc_lo, g_lo)):
                        kept = kept[:, bass.ds(p, 1), :].rearrange("p o c -> p (o c)")
                        if half == 0:
                            m = pool.tensor_copy(kept, whole[:, v, HALF:HALF + G0])
                        else:
                            m = pool.tensor_copy(whole[:, v, 0:G0], kept)
                    m.then_inc(s_gc, 1)

                kept_columns(0, 0)
                kept_columns(1, 1)
                with pool.Fori(1, NP // 2) as i:
                    for v in range(2):
                        kept_columns(2 * i + v, v)
                for t in range(tiles):
                    pool.wait_ge(s_o, t + 1)
                    pool.dma_start(out_d[t0 + t], y[:, t, :]).then_inc(s_st[t % 2], 16)
                pool.wait_ge(s_st[0], 16 * ((tiles + 1) // 2))
                pool.wait_ge(s_st[1], 16 * (tiles // 2))

            @block.scalar
            def _(act):
                def up_hi(p, j):
                    act.wait_ge(s_w[j], 16 * p + 16)
                    if not isinstance(p, int) or p:
                        act.wait_ge(s_up, 4 * (p - 1) + 2 * j + 2)
                    act.activation(wu_hi[:, j, :, :].rearrange("p k m -> p (k m)"), w_st[:, j, :], ACT.Copy)\
                        .then_inc(s_whi, 1)

                def body(p, v, last, first):
                    for j in range(2):
                        for n in range(2):
                            act.wait_ge(s_up, 4 * p + 2 * j + n + 1)
                            if not first:
                                act.wait_ge(s_cd, 2 * (p - 1) + j + 1)
                            act.activation(u[:, j, 2 + n * BLK:2 + (n + 1) * BLK], ps_u[:, j, n, :], ACT.Copy)\
                                .then_inc(s_u, 1)
                        if not last:
                            up_hi(p + 1, j)
                    act.wait_ge(s_wd, 16 * p + 16)
                    if not (isinstance(p, int) and p < 2):
                        act.wait_ge(s_dn, tiles * (p - 1))
                    act.activation(wd_hi[:, v, :], wd_st[:], ACT.Copy).then_inc(s_dhi, 1)
                    act.wait_ge(s_cd, 2 * p + 1)
                    act.activation(cv[:, 0, :], cv[:, 0, :], ACT.Gelu_apprx_tanh).then_inc(s_ge, 1)
                    act.wait_ge(s_g, p + 1)
                    if half == 0 and not (isinstance(p, int) and p < 2):
                        act.wait_ge(s_gc, p - 1)
                    act.activation(g_hi[:, v, G0:G0 + NCV], cv[:, 0, :], ACT.Copy).then_inc(s_ghi, 1)

                up_hi(0, 0)
                up_hi(0, 1)
                body(0, 0, False, True)
                body(1, 1, False, False)
                with act.Fori(1, NP // 2 - 1) as i:
                    for v in range(2):
                        body(2 * i + v, v, False, False)
                body(NP - 2, 0, False, False)
                body(NP - 1, 1, True, False)
                for t in range(tiles):
                    act.wait_ge(s_y, tiles * (NP - 1) + t + 1)
                    if t:
                        act.wait_ge(s_sq, t)
                    act.activation(u[:, 0, 0:D], y[:, t, :], ACT.Square, accum_out=sums[:, t:t + 1]).then_inc(s_sq, 1)
                act.wait_ge(s_mean, 1)
                act.activation(std[:], mean[:], ACT.Sqrt).then_inc(s_std, 1)

            @block.vector
            def _(dve):
                def up_lo(p, j):
                    dve.wait_ge(s_whi, 2 * p + j + 1)
                    dve.tensor_tensor(wu_lo[:, j, :, :].rearrange("p k m -> p (k m)"), w_st[:, j, :],
                                      wu_hi[:, j, :, :].rearrange("p k m -> p (k m)"), ALU.subtract).then_inc(s_wlo, 1)

                def convolve(p, j, first):
                    n = CS * p + 4 * j
                    one = lambda i: cw[:, bass.ds(2 * p + j, 1), i:i + 1].rearrange("p o i -> p (o i)")
                    keep = carry[:, bass.ds(2 * p + j, 1), :].rearrange("p o i -> p (o i)")
                    dve.wait_ge(s_u, 4 * p + 2 * j + 2)
                    if half == 0:
                        dve.tensor_copy(keep, u[:, j, HALF:HALF + 2]).then_inc(s_cs, 1)
                    else:
                        dve.tensor_copy(u[:, j, 0:2], keep).then_inc(s_cs, 1)
                        dve.wait_ge(s_cs, n + 1)
                    if not first:
                        dve.wait_ge(s_ghi, p)
                        dve.wait_ge(s_glo, p)
                    dve.tensor_scalar(cv[:, j, :], u[:, j, 0:NCV], one(0), one(3), ALU.mult, ALU.add).then_inc(s_cs, 1)
                    dve.wait_ge(s_cs, n + 2)
                    dve.scalar_tensor_tensor(cv[:, j, :], u[:, j, 1:NCV + 1], one(1), cv[:, j, :], ALU.mult, ALU.add)\
                        .then_inc(s_cs, 1)
                    dve.wait_ge(s_cs, n + 3)
                    dve.scalar_tensor_tensor(cv[:, j, :], u[:, j, 2:NCV + 2], one(2), cv[:, j, :], ALU.mult, ALU.add)\
                        .then_inc(s_cd, 1)
                    dve.sem_inc(s_cs, 1)

                def add_down(p):
                    for t in range(tiles):
                        dve.wait_ge(s_dn, tiles * p + t + 1)
                        dve.tensor_tensor(y[:, t, :], y[:, t, :], ps_d[:, t % 2, :], ALU.add).then_inc(s_y, 1)

                def body(p, v, last, first):
                    convolve(p, 0, first)
                    if not last:
                        up_lo(p + 1, 0)
                    if not first:
                        add_down(p - 1)
                    if not last:
                        up_lo(p + 1, 1)
                    convolve(p, 1, first)
                    dve.wait_ge(s_ge, p + 1)
                    dve.wait_ge(s_cd, 2 * p + 2)
                    dve.tensor_tensor(cv[:, 0, :], cv[:, 0, :], cv[:, 1, :], ALU.mult).then_inc(s_g, 1)
                    dve.wait_ge(s_dhi, p + 1)
                    dve.tensor_tensor(wd_lo[:, v, :], wd_st[:], wd_hi[:, v, :], ALU.subtract).then_inc(s_dlo, 1)
                    dve.wait_ge(s_ghi, p + 1)
                    if half == 0 and not (isinstance(p, int) and p < 2):
                        dve.wait_ge(s_gc, p - 1)
                    dve.tensor_tensor(g_lo[:, v, G0:G0 + NCV], cv[:, 0, :], g_hi[:, v, G0:G0 + NCV], ALU.subtract)\
                        .then_inc(s_glo, 1)

                dve.wait_ge(s_cw, 16)
                dve.wait_ge(s_init, 3)
                up_lo(0, 0)
                up_lo(0, 1)
                body(0, 0, False, True)
                body(1, 1, False, False)
                with dve.Fori(1, NP // 2 - 1) as i:
                    for v in range(2):
                        body(2 * i + v, v, False, False)
                body(NP - 2, 0, False, False)
                body(NP - 1, 1, True, False)
                add_down(NP - 1)
                dve.wait_ge(s_sq, tiles)
                dve.tensor_scalar(mean[:], sums[:], 1.0 / D, EPS, ALU.mult, ALU.add).then_inc(s_mean, 1)
                dve.wait_ge(s_std, 1)
                dve.reciprocal(rstd[:], std[:]).then_inc(s_rstd, 1)
                dve.wait_ge(s_rstd, 1)
                dve.wait_ge(s_g2, 16)
                for t in range(tiles):
                    dve.scalar_tensor_tensor(y[:, t, :], y[:, t, :], rstd[:, t:t + 1], wd_st[:], ALU.mult, ALU.mult)\
                        .then_inc(s_n, 1)
                    dve.wait_ge(s_n, t + 1)
                    dve.wait_ge(s_x[t % 2], 16 * (t // 2 + 1))
                    dve.tensor_tensor(y[:, t, :], y[:, t, :], cv[:, t % 2, 0:D], ALU.add).then_inc(s_o, 1)

            @block.tensor
            def _(pe):
                def up(p, first=False):
                    for j in range(2):
                        pe.wait_ge(s_wlo, 2 * p + j + 1)
                        for n in range(2):
                            if not first:
                                pe.wait_ge(s_u, 4 * (p - 1) + 2 * j + n + 1)
                            cols = slice(n * BLK, (n + 1) * BLK)
                            for k in range(KD):
                                m = product3(pe, ps_u[:, j, n, :], wu_hi[:, j, k, :], wu_lo[:, j, k, :],
                                             h_hi[:, k, cols], h_lo[:, k, cols], k == 0, k == KD - 1)
                            m.then_inc(s_up, 1)

                def down(p, v):
                    pe.wait_ge(s_dlo, p + 1)
                    pe.wait_ge(s_glo, p + 1)
                    if half == 1:
                        pe.wait_ge(s_gc, p + 1)
                    for t in range(tiles):
                        if t >= 2 or not isinstance(p, int) or p:
                            pe.wait_ge(s_y, tiles * p + t - 1)
                        g = slice(off + t * P, off + (t + 1) * P)
                        for n in range(2):
                            cols = slice(n * BLK, (n + 1) * BLK)
                            m = product3(pe, ps_d[:, t % 2, cols], g_hi[:, v, g], g_lo[:, v, g],
                                         wd_hi[:, v, cols], wd_lo[:, v, cols], True, True)
                        m.then_inc(s_dn, 1)

                up(0, True)
                up(1)
                down(0, 0)
                with pe.Fori(0, NP // 2 - 1) as i:
                    up(2 * i + 2)
                    down(2 * i + 1, 1)
                    up(2 * i + 3)
                    down(2 * i + 2, 0)
                down(NP - 1, 1)


def program(nc, x, c, w_ada, b_ada, pre_g, post_g, w_f, w_z, b_gate, qk_g, w_branch, w_out, w_up, conv, w_dn,
            t_pos, t_chan, rope_cos, rope_sin, swap, head_mean, ident_d, out, scratch_kind="Internal"):
    def scratch(name, shape, dt=F32):
        return nc.dram_tensor(f"scratch_{name}", shape, dt, kind=scratch_kind).ap()

    gate_rows = scratch("gate_rows", [P, 2, D])
    f_d = scratch("f", [NT, P, FW])
    qkv_d = scratch("qkv", [NQC + 2, P, S])
    gates_d = scratch("gates", [NB, 2 * KD, P, BLK])
    yT_d = scratch("yT", [NG, P, S])
    kv_d = scratch("kv", [NKV, P, 3, S])
    o_d = scratch("o", [2, NH, HD, S])
    x1_d = scratch("x1", [NT, P, D])

    with Res(nc, "keep") as keep:
        ident = keep.sb("ident", [P, P])
        ones = keep.sb("ones", [P, P])
        mod = keep.sb("mod", [P, 4, KD])
        first_sem = load_constants(nc, ident_d, ident, ones)
        ada_phase(nc, c, w_ada, b_ada, pre_g, post_g, ident, ones, mod, gate_rows)
        with Res(nc, "h1") as h1:
            h_hi, h_lo = (h1.sb(n, [P, KD, S], F32R) for n in ("hi", "lo"))
            norm_phase(nc, "norm1", x, NB, ident, mod[:, 0, :], mod[:, 1, :], h_hi, h_lo)
            f_phase(nc, w_f, h_hi, h_lo, f_d)
            kept = proj_phase(nc, w_z, h_hi, h_lo, b_gate, qk_g, rope_cos, rope_sin, swap, head_mean, qkv_d, gates_d)
        fourier_phase(nc, f_d, t_pos, t_chan, yT_d)
        kv_phase(nc, qkv_d, ident, kv_d)
        attention_phase(nc, qkv_d, kv_d, ident, ones, o_d)
        merge_phase(nc, x, w_branch, w_out, o_d, yT_d, gates_d, gate_rows[:, 0, :], x1_d, first_sem, kept)
        with Res(nc, "h2") as h2:
            h_hi, h_lo = (h2.sb(n, [P, KD, HALF], F32R) for n in ("hi", "lo"))
            carry = h2.sb("carry", [P, 2 * NP, 2])
            gc_hi, gc_lo = (h2.sb(n, [P, NP, P - 1], F32R) for n in ("gc_hi", "gc_lo"))
            for half in range(2):
                norm_phase(nc, f"norm2{half}", x1_d[half * NT // 2:(half + 1) * NT // 2], NB // 2, ident,
                           mod[:, 2, :], mod[:, 3, :], h_hi, h_lo)
                ffn_phase(nc, half, h_hi, h_lo, w_up, w_dn, conv, gate_rows[:, 1, :], carry, gc_hi, gc_lo, x1_d, out)


def tables():
    n2, k2 = np.arange(P)[:, None], np.arange(P)[None, :]
    pos = np.empty((K1, P, 3, P))
    for k1 in range(K1):
        a = 2 * np.pi * ((n2 * (k1 + N1 * k2)) % S) / S
        pos[k1, :, 0], pos[k1, :, 1], pos[k1, :, 2] = np.sin(a), np.cos(a), -np.sin(a)
    a = 2 * np.pi * ((n2 * k2) % P) / P
    chan = np.stack([np.cos(a), np.sin(a), -np.sin(a)], 1) / math.sqrt(S * P)
    grid_w, pairs = 64, HD // 4
    inv = 10000.0 ** (-np.arange(pairs) / pairs)
    t = np.arange(S)
    ang = np.concatenate([(t // grid_w)[None, :] * inv[:, None], (t % grid_w)[None, :] * inv[:, None]])
    ang = np.tile(np.repeat(ang, 2, axis=0), (2, 1))
    sign = np.where(np.arange(P) % 2 == 0, -1.0, 1.0)[:, None]
    swap = np.zeros((P, P))
    swap[np.arange(P) ^ 1, np.arange(P)] = 1.0
    head_mean = np.kron(np.eye(2), np.full((HD, HD), 1.0 / HD))
    made = {"t_pos": pos.reshape(K1, P, 3 * P), "t_chan": chan.reshape(P, 3 * P), "rope_cos": np.cos(ang),
            "rope_sin": sign * np.sin(ang), "swap": swap, "head_mean": head_mean, "ident_d": np.eye(P)}
    return {k: np.ascontiguousarray(v.astype(np.float32)) for k, v in made.items()}


def layouts(a):
    w_in = a["w_in"][0].reshape(KD, P, -1)
    o1 = NH * HD
    o3 = o1 + 2 * NKV * HD
    o4 = o3 + FW

    def chunks(w):
        n = w.shape[2] // P
        return w.reshape(w.shape[0], P, n, P).transpose(2, 1, 0, 3).reshape(n, P, -1)

    def pairs(first, second):
        return np.stack([first, second], 1).reshape(-1, *first.shape[1:])

    by_channel = lambda v: v.reshape(-1, P).T
    ga, gf = chunks(w_in[:, :, o4:o4 + D]), chunks(w_in[:, :, o4 + D:])
    bga, bgf = by_channel(a["b_gate"][0, :D]), by_channel(a["b_gate"][0, D:])
    wa = chunks(a["w_attn_branch"][0].reshape(NQC, P, D))
    wf = chunks(a["w_fourier_branch"][0].reshape(NG, P, D))
    wu = a["w_up"][0].reshape(KD, P, -1)
    cw = np.concatenate([a["conv_w"][0], a["conv_b"][0][None]])
    cw = cw.reshape(4, 2, NP, P).transpose(3, 2, 1, 0).reshape(P, 2 * NP, 4)
    q_g, k_g = np.tile(a["q_norm_g"][0], 2), np.tile(a["k_norm_g"][0], 2)
    laid = {
        "x": a["x"].reshape(NT, P, D),
        "c": by_channel(a["c"][0]),
        "w_ada": a["w_ada"][0].reshape(KD, P, 6 * D),
        "b_ada": a["b_ada"],
        "pre_g": np.stack([by_channel(a["mix_pre_g"][0]), by_channel(a["ffn_pre_g"][0])], 1),
        "post_g": np.stack([a["mix_post_g"][0], a["ffn_post_g"][0]]),
        "w_f": w_in[:, :, o3:o4],
        "w_z": np.concatenate([chunks(w_in[:, :, :o3]), pairs(ga, gf)]),
        "b_gate": np.stack([bga, bgf], 2).reshape(P, 2 * KD),
        "qk_g": np.stack([q_g] * NQC + [k_g], 1),
        "w_branch": np.concatenate([wa, wf], 2),
        "w_out": a["w_out"][0].reshape(KD, P, D),
        "w_up": pairs(chunks(wu[:, :, :DFF]), chunks(wu[:, :, DFF:])),
        "conv": cw,
        "w_dn": a["w_down"][0].reshape(NP, P, D),
    }
    return {k: np.ascontiguousarray(v) for k, v in laid.items()}


def kernel(**inputs):
    import concourse.bacc as bacc
    from concourse.bass_utils import run_bass_kernel_spmd

    arrays = {**layouts({k: np.asarray(v) for k, v in inputs.items()}), **tables()}
    nc = bacc.Bacc("TRN2", target_bir_lowering=False, num_devices=1)
    args = {n: nc.dram_tensor(f"in_{n}", a.shape, mybir.dt.from_np(a.dtype), kind="ExternalInput").ap()
            for n, a in arrays.items()}
    out = nc.dram_tensor("out", [NT, P, D], F32, kind="ExternalOutput").ap()
    program(nc, out=out, **args)
    got = run_bass_kernel_spmd(nc, [{f"in_{n}": a for n, a in arrays.items()}], core_ids=[0])
    return got.results[0]["out"].reshape(1, S, D)
```

```python
import math
from contextlib import ExitStack

import numpy as np

import concourse.bass as bass
from concourse import mybir

F32 = mybir.dt.float32
F32R = mybir.dt.float32r
ALU = mybir.AluOpType
ACT = mybir.ActivationFunctionType
AX = mybir.AxisListType

P = 128
D = 1024
S = 2048
KD = D // P
NT = S // P
BLK = 512
NB = S // BLK
HD = 64
NH = 8
NQC = NH * HD // P
NKV = 2
NG = 4
FW = NG * P
DFF = 2816
NP = DFF // P
HALF = S // 2
EPS = 1e-6
NM = NB * NT
N1 = 16
K1 = N1 // 2 + 1


class Res:

    def __init__(self, nc, tag):
        self.nc, self.tag, self.ctx, self.sem_nums = nc, tag, ExitStack(), []

    def __enter__(self):
        return self

    def __exit__(self, *a):
        return self.ctx.__exit__(*a)

    def sb(self, name, shape, dt=F32):
        return self.ctx.enter_context(self.nc.sbuf_tensor(f"{self.tag}_{name}", shape, dt))

    def ps(self, name, shape, dt=F32):
        return self.ctx.enter_context(self.nc.psum_tensor(f"{self.tag}_{name}", shape, dt))

    def sem(self, name):
        handle = self.ctx.enter_context(self.nc.semaphore(f"{self.tag}_{name}"))
        self.sem_nums.append(handle.num)
        return handle

    def pool_dma_sem(self, name):
        return self.nc.alloc_semaphore(name=f"{self.tag}_{name}")

    def block(self):
        return self.nc.Block()


def product3(pe, out, w_hi, w_lo, x_hi, x_lo, first, last):
    pe.matmul(out, w_hi, x_hi, start=first, stop=False)
    pe.matmul(out, w_hi, x_lo, start=False, stop=False)
    return pe.matmul(out, w_lo, x_hi, start=False, stop=last)


def load_constants(nc, ident_d, ident, ones):
    with Res(nc, "const") as r:
        loaded = r.sem("loaded")
        with r.block() as block:

            @block.sync
            def _(sp):
                sp.dma_start(ident[:], ident_d).then_inc(loaded, 16)
                sp.wait_ge(loaded, 16)

            @block.vector
            def _(dve):
                dve.memset(ones[:], 1.0)
        return loaded.num


def ada_phase(nc, c_d, w_ada, b_ada, pre_g, post_g, ident, ones, mod, gate_rows):
    W6 = 6 * D
    with Res(nc, "ada") as r:
        c_raw = r.sb("c_raw", [P, KD])
        c_act = r.sb("c_act", [P, KD])
        w = [r.sb(f"w{i}", [P, W6]) for i in range(2)]
        acc = r.sb("acc", [P, W6])
        bias = r.sb("bias", [1, W6])
        gains = r.sb("gains", [P, 2, KD])
        post = r.sb("post", [P, 2, D])
        rows = r.sb("rows", [P, 2, D])
        cols = r.sb("cols", [P, 4, KD])
        ps_cols = r.ps("ps_cols", [P, 512])
        ps_rows = r.ps("ps_rows", [P, 4, 512])
        s_small, s_bias = r.sem("small"), r.sem("bias")
        s_w = [r.sem(f"w_loaded{i}") for i in range(2)]
        s_silu, s_acc, s_cols, s_rows, s_fin, s_out = (r.sem(n) for n in ("silu", "acc", "cols", "rows", "fin", "out"))
        with r.block() as block:

            @block.sync
            def _(sp):
                sp.dma_start(c_raw[:], c_d).then_inc(s_small, 16)
                for k in range(KD):
                    if k >= 2:
                        sp.wait_ge(s_acc, k - 1)
                    sp.dma_start(w[k % 2][:], w_ada[k]).then_inc(s_w[k % 2], 16)
                sp.dma_start(bias[:], b_ada).then_inc(s_bias, 16)
                sp.dma_start(gains[:], pre_g).then_inc(s_bias, 16)
                for j in range(2):
                    sp.dma_start(post[:, j, :], post_g[j:j + 1, :].broadcast_to([P, D])).then_inc(s_bias, 16)
                sp.wait_ge(s_fin, 4)
                sp.dma_start(gate_rows, rows[:]).then_inc(s_out, 16)
                sp.wait_ge(s_out, 16)

            @block.scalar
            def _(act):
                act.wait_ge(s_small, 16)
                act.activation(c_act[:], c_raw[:], ACT.Silu).then_inc(s_silu, 1)

            @block.vector
            def _(dve):
                dve.wait_ge(s_silu, 1)
                for k in range(KD):
                    dve.wait_ge(s_w[k % 2], 16 * (k // 2 + 1))
                    if k == 0:
                        dve.tensor_scalar(acc[:], w[0][:], c_act[:, 0:1], None, ALU.mult).then_inc(s_acc, 1)
                    else:
                        dve.wait_ge(s_acc, k)
                        dve.scalar_tensor_tensor(acc[:], w[k % 2][:], c_act[:, k:k + 1], acc[:],
                                                 ALU.mult, ALU.add).then_inc(s_acc, 1)
                dve.wait_ge(s_bias, 64)
                dve.wait_ge(s_acc, KD)
                dve.tensor_tensor(acc[0:1, :], acc[0:1, :], bias[:], ALU.add).then_inc(s_acc, 1)
                dve.wait_ge(s_cols, 1)
                dve.tensor_copy(cols[:], ps_cols[:, 0:4 * KD].rearrange("p (a k) -> p a k", a=4)).then_inc(s_fin, 1)
                dve.wait_ge(s_fin, 1)
                for j in range(2):
                    dve.scalar_tensor_tensor(mod[:, 2 * j, :], cols[:, 2 * j + 1, :], 1.0, gains[:, j, :],
                                             ALU.add, ALU.mult)
                    ins = dve.tensor_copy(mod[:, 2 * j + 1, :], cols[:, 2 * j, :])
                ins.then_inc(s_fin, 1)
                dve.wait_ge(s_rows, 1)
                for j in range(2):
                    dve.tensor_tensor(rows[:, j, :], ps_rows[:, 2 * j:2 * j + 2, :].rearrange("p a b -> p (a b)"),
                                      post[:, j, :], ALU.mult).then_inc(s_fin, 1)

            @block.tensor
            def _(pe):
                pe.wait_ge(s_acc, KD + 1)
                for a, part in enumerate((0, 1, 3, 4)):
                    for k in range(KD):
                        at = part * D + k * P
                        m = pe.matmul(ps_cols[:, a * KD + k:a * KD + k + 1], acc[:, at:at + P], ones[:, 0:1],
                                      start=True, stop=True)
                m.then_inc(s_cols, 1)
                for j, part in enumerate((2, 5)):
                    for n in range(2):
                        at = part * D + n * 512
                        m = pe.matmul(ps_rows[:, 2 * j + n, :], ones[:], acc[:, at:at + 512], start=True, stop=True)
                m.then_inc(s_rows, 1)


def norm_phase(nc, tag, x_d, nblocks, ident, scale, shift, hT_hi, hT_lo):
    TB = BLK // P
    assert nblocks % 2 == 0
    with Res(nc, tag) as r:
        x = [r.sb(f"x{i}", [P, TB, D]) for i in range(2)]
        junk = r.sb("junk", [P, D])
        sums = [r.sb(f"sums{i}", [P, TB]) for i in range(2)]
        mean = [r.sb(f"mean{i}", [P, TB]) for i in range(2)]
        std = [r.sb(f"std{i}", [P, TB]) for i in range(2)]
        rstd = [r.sb(f"rstd{i}", [P, TB]) for i in range(2)]
        full = r.sb("full", [P, 2, BLK])
        ps = r.ps("ps", [P, 4, BLK])
        s_x = [r.sem(f"x{i}") for i in range(2)]
        names = ("sq", "mean", "std", "rstd", "xn", "tr", "full", "hi", "lo")
        s_sq, s_mean, s_std, s_rstd, s_xn, s_tr, s_full, s_hi, s_lo = (r.sem(n) for n in names)
        with r.block() as block:

            @block.sync
            def _(sp):
                with sp.Fori(0, nblocks // 2) as i:
                    for u in range(2):
                        sp.wait_ge(s_tr, (2 * i + u + 1) * KD)
                        sp.dma_start(x[u][:], x_d[bass.ds((2 * i + u) * TB, TB), :, :].rearrange("t p d -> p t d"))\
                            .then_inc(s_x[u], 16)

            @block.scalar
            def _(act):
                with act.Fori(0, nblocks // 2) as i:
                    for u in range(2):
                        b = 2 * i + u
                        act.wait_ge(s_x[u], 16 * i + 16)
                        for j in range(TB):
                            act.wait_ge(s_sq, b * TB + j + 1)
                            act.activation(junk[:], x[u][:, j, :], ACT.Square, accum_out=sums[u][:, j:j + 1])\
                                .then_inc(s_sq, 1)
                        act.wait_ge(s_mean, b + 1)
                        act.activation(std[u][:], mean[u][:], ACT.Sqrt).then_inc(s_std, 1)
                        for k in range(KD):
                            act.wait_ge(s_tr, (b + 2) * KD + k + 1)
                            act.wait_ge(s_lo, b * KD + k + 1)
                            act.wait_ge(s_full, b * KD + k + 1)
                            act.activation(full[:, k % 2, :], ps[:, k % 4, :], ACT.Identity,
                                           bias=shift[:, k:k + 1], scale=scale[:, k:k + 1]).then_inc(s_full, 1)

            @block.vector
            def _(dve):
                dve.sem_inc(s_lo, 2)
                with dve.Fori(0, nblocks // 2) as i:
                    for u in range(2):
                        b = 2 * i + u
                        dve.wait_ge(s_sq, b * TB + TB + 1)
                        dve.tensor_scalar(mean[u][:], sums[u][:], 1.0 / D, EPS, ALU.mult, ALU.add).then_inc(s_mean, 1)
                        dve.wait_ge(s_std, b + 1)
                        dve.reciprocal(rstd[u][:], std[u][:]).then_inc(s_rstd, 1)
                        dve.wait_ge(s_rstd, b + 1)
                        for j in range(TB):
                            dve.tensor_scalar(x[u][:, j, :], x[u][:, j, :], rstd[u][:, j:j + 1], None, ALU.mult)\
                                .then_inc(s_xn, 1)
                        for k in range(KD):
                            cols = bass.ds(b * BLK, BLK)
                            dve.wait_ge(s_full, b * KD + k + 2)
                            dve.tensor_copy(hT_hi[:, k, cols], full[:, k % 2, :]).then_inc(s_hi, 1)
                            dve.wait_ge(s_hi, b * KD + k + 1)
                            dve.tensor_tensor(hT_lo[:, k, cols], full[:, k % 2, :], hT_hi[:, k, cols], ALU.subtract)\
                                .then_inc(s_lo, 1)

            @block.tensor
            def _(pe):
                pe.sem_inc(s_tr, 2 * KD)
                pe.sem_inc(s_sq, 1)
                pe.sem_inc(s_full, 1)
                with pe.Fori(0, nblocks // 2) as i:
                    for u in range(2):
                        b = 2 * i + u
                        pe.wait_ge(s_xn, (b + 1) * TB)
                        for k in range(KD):
                            if k >= 4:
                                pe.wait_ge(s_full, b * KD + k - 3 + 1)
                            elif k == 0:
                                pe.wait_ge(s_full, b * KD + 1)
                            for j in range(TB):
                                m = pe.transpose(ps[:, k % 4, j * P:(j + 1) * P], x[u][:, j, k * P:(k + 1) * P],
                                                 ident[:])
                            m.then_inc(s_tr, 1)


def f_phase(nc, w_f, hT_hi, hT_lo, f_d):
    with Res(nc, "fin") as r:
        w_st = r.sb("w_st", [P, 2, FW])
        w_hi = r.sb("w_hi", [P, KD, FW], F32R)
        w_lo = r.sb("w_lo", [P, KD, FW], F32R)
        out = r.sb("out", [P, 4, FW])
        ps = r.ps("ps", [P, 4, FW])
        s_w = [r.sem(f"w{i}") for i in range(2)]
        s_hi, s_lo, s_mm, s_ev = (r.sem(n) for n in ("hi", "lo", "mm", "ev"))
        s_out = [r.sem(f"out{i}") for i in range(4)]
        with r.block() as block:

            @block.sync
            def _(sp):
                for k in range(KD):
                    if k >= 2:
                        sp.wait_ge(s_lo, k - 1)
                    sp.dma_start(w_st[:, k % 2, :], w_f[k]).then_inc(s_w[k % 2], 16)
                for t in range(NT):
                    sp.wait_ge(s_ev, t + 1)
                    sp.dma_start(f_d[t], out[:, t % 4, :]).then_inc(s_out[t % 4], 16)
                for i in range(4):
                    sp.wait_ge(s_out[i], 16 * NT // 4)

            @block.vector
            def _(dve):
                for k in range(KD):
                    dve.wait_ge(s_w[k % 2], 16 * (k // 2 + 1))
                    dve.tensor_copy(w_hi[:, k, :], w_st[:, k % 2, :]).then_inc(s_hi, 1)
                    dve.wait_ge(s_hi, k + 1)
                    dve.tensor_tensor(w_lo[:, k, :], w_st[:, k % 2, :], w_hi[:, k, :], ALU.subtract).then_inc(s_lo, 1)

            @block.scalar
            def _(act):
                for t in range(NT):
                    act.wait_ge(s_mm, t + 1)
                    if t >= 4:
                        act.wait_ge(s_out[t % 4], 16 * (t // 4))
                    act.activation(out[:, t % 4, :], ps[:, t % 4, :], ACT.Copy).then_inc(s_ev, 1)

            @block.tensor
            def _(pe):
                for t in range(NT):
                    if t >= 4:
                        pe.wait_ge(s_ev, t - 3)
                    for k in range(KD):
                        if t == 0:
                            pe.wait_ge(s_lo, k + 1)
                        cols = slice(t * P, (t + 1) * P)
                        m = product3(pe, ps[:, t % 4, :], hT_hi[:, k, cols], hT_lo[:, k, cols],
                                     w_hi[:, k, :], w_lo[:, k, :], k == 0, k == KD - 1)
                    m.then_inc(s_mm, 1)


def proj_phase(nc, w_z, hT_hi, hT_lo, b_gate, qk_g, rope_cos, rope_sin, swap_d, head_mean_d, ident, f_d, qkv_d, gates_d,
               z_d, kv_d):
    NQKV = NQC + 2
    C1, C2, C3 = (math.cos(2 * math.pi * n / N1) for n in (1, 2, 3))
    NV = 44
    KVS = 8
    PER = 2 * KD // NG
    NC = NQKV + 2 * KD
    with Res(nc, "proj") as r:
        w_st = r.sb("w_st", [P, 2, KD, P])
        w_hi = [r.sb(f"w_hi{i}", [P, KD, P], F32R) for i in range(2)]
        w_lo = [r.sb(f"w_lo{i}", [P, KD, P], F32R) for i in range(2)]
        out = r.sb("out", [P, NB, BLK])
        side = r.sb("side", [P, 4, S])
        cos, sin = side[:, 0, :], side[:, 1, :]
        bg = r.sb("bg", [P, 2 * KD])
        gains = r.sb("gains", [P, NQC + 1])
        v_st = r.sb("v_st", [P, BLK])
        swap, head_mean = v_st[:, 0:P], v_st[:, P:2 * P]
        eps = r.sb("eps", [P, 1])
        bcol = r.sb("bcol", [P, 2])
        zg, sq, std, rot = (side[:, a, b * 2 * BLK:(b + 1) * 2 * BLK].rearrange("p (s q) -> p s q", s=2)
                            for a in (2, 3) for b in (0, 1))
        z, eo, z_hi, z_lo = (side[:, a, :].rearrange("p (n c) -> p n c", n=N1) for a in range(4))
        z_hi, z_lo = z_hi.bitcast(F32R), z_lo.bitcast(F32R)
        k_st = r.sb("k_st", [P, NKV, BLK])
        kv = r.sb("kv", [P, NKV, 2, BLK], F32R)
        ps = r.ps("ps", [P, NB, BLK])
        ps_ms = r.ps("ps_ms", [P, 2, BLK])
        ps_sw = r.ps("ps_sw", [P, 2, BLK])
        s_c, s_eps, s_bcol = r.sem("consts"), r.sem("eps_written"), r.sem("bias_at_hand")
        s_w = [r.sem(f"w_loaded{i}") for i in range(2)]
        s_hi, s_lo, s_mm, s_zg, s_ms, s_std, s_rot, s_out, s_rope = (
            r.sem(n) for n in ("w_hi_made", "w_lo_made", "products", "zg_sq", "mean_swap", "root", "rotated", "v_or_gate", "rope"))
        s_f, s_dft, s_z, s_zst = (r.sem(n) for n in ("f_loaded", "dft_steps", "z_split", "z_stored"))
        s_k, s_v, s_tr, s_kv, s_kvst = (r.sem(n) for n in ("k_loaded", "v_loaded", "v_turned", "kv_steps", "kv_stored"))
        s_st = [r.pool_dma_sem(f"stored{n}") for n in range(NB)]
        with r.block() as block:

            @block.sync
            def _(sp):
                for dst, src in ((cos, rope_cos), (sin, rope_sin), (bg[:], b_gate), (gains[:], qk_g), (swap, swap_d),
                                 (head_mean, head_mean_d)):
                    sp.dma_start(dst, src).then_inc(s_c, 16)

                def load(c, u):
                    sp.dma_start(w_st[:, u:u + 1, :, :],
                                 w_z[bass.ds(c, 1), :, :].rearrange("o p (k m) -> p o k m", k=KD)).then_inc(s_w[u], 16)

                load(0, 0)
                load(1, 1)
                with sp.Fori(0, NQKV // 2) as i:
                    for u in range(2):
                        sp.wait_ge(s_lo, 2 * i + u + 1)
                        load(2 * i + u + 2, u)

                def load_f(g):
                    src = f_d.rearrange("t p c -> p t c")[:, :, bass.ds(g * P, P)]
                    sp.dma_start(z, src).then_inc(s_f, 16)

                def load_kv(g):
                    cols = bass.ds(g * BLK, BLK)
                    sp.dma_start(v_st[:], qkv_d[NQC + 1][:, cols]).then_inc(s_v, 16)
                    for a in range(NKV):
                        for half in range(2):
                            sp.dma_start(k_st[half * HD:(half + 1) * HD, a, :],
                                         qkv_d[NQC, a * HD:(a + 1) * HD][:, cols]).then_inc(s_k, 16)

                def store_kv(g):
                    sp.wait_ge(s_kv, KVS * (g + 1))
                    for a in range(NKV):
                        sp.dma_start(kv_d[a][:, :, bass.ds(g * BLK, BLK)], kv[:, a].bitcast(F32)).then_inc(s_kvst, 16)

                sp.wait_ge(s_rot, NB * (NQC + 1))
                load_f(0)
                for n in range(NB):
                    sp.wait_ge(s_st[n], 16 * NQKV)
                load_kv(0)

                def body(g, first, last):
                    for j in range(PER):
                        if not (last and j >= PER - 2):
                            sp.wait_ge(s_lo, PER * g + NQKV + j + 1)
                            load(PER * g + NQKV + j + 2, j % 2)
                        if j == 0 and not first:
                            store_kv(g - 1)
                            load_kv(g)
                        if j == 2:
                            sp.wait_ge(s_z, 2 * (g + 1))
                            for part, src in enumerate((z_hi, z_lo)):
                                at = z_d[part, bass.ds(g, 1)].rearrange("o p c -> (o p) c")
                                sp.dma_start(at, side[:, 2 + part, :]).then_inc(s_zst, 16)
                            if not last:
                                load_f(g + 1)

                body(0, True, False)
                with sp.Fori(1, NG - 1) as g:
                    body(g, False, False)
                body(NG - 1, False, True)
                store_kv(NG - 1)
                sp.wait_ge(s_zst, 32 * NG)
                sp.wait_ge(s_kvst, 16 * NKV * NG)

            @block.gpsimd
            def _(pool):
                with pool.Fori(0, NQC + 1) as c:
                    for n in range(NB):
                        pool.wait_ge(s_rot, 4 * c + n + 1)
                        pool.dma_start(qkv_d[bass.ds(c, 1), :, n * BLK:(n + 1) * BLK], out[:, n, :]).then_inc(s_st[n], 16)
                for n in range(NB):
                    pool.wait_ge(s_out, n + 1)
                    pool.dma_start(qkv_d[NQC + 1, :, n * BLK:(n + 1) * BLK], out[:, n, :]).then_inc(s_st[n], 16)
                with pool.Fori(0, 2 * KD) as g:
                    for n in range(NB):
                        pool.wait_ge(s_out, 4 * g + 4 + n + 1)
                        pool.dma_start(gates_d[n, bass.ds(g, 1), :, :], out[:, n, :]).then_inc(s_st[n], 16)
                for n in range(NB):
                    pool.wait_ge(s_st[n], 16 * NC)

            @block.scalar
            def _(act):
                def hi_part(c, i, u):
                    act.wait_ge(s_w[u], 16 * i + 16)
                    act.activation(w_hi[u][:], w_st[:, u, :, :], ACT.Copy).then_inc(s_hi, 1)

                def root(c, n):
                    act.wait_ge(s_ms, 4 * c + n + 1)
                    if c or n >= 2:
                        act.wait_ge(s_rot, 4 * c + n - 1)
                    act.activation(std[:, n % 2, :], ps_ms[:, n % 2, :], ACT.Sqrt, bias=eps[:, 0:1]).then_inc(s_std, 1)

                hi_part(0, 0, 0)
                act.wait_ge(s_c, 16 * 6)
                act.wait_ge(s_eps, 1)
                for c in range(NQC + 1):
                    if c:
                        act.wait_ge(s_mm, 4 * c)
                    hi_part(c + 1, (c + 1) // 2, (c + 1) % 2)
                    for n in range(NB):
                        act.wait_ge(s_mm, 4 * c + n + 1)
                        if c or n >= 2:
                            act.wait_ge(s_rot, 4 * c + n - 1)
                        act.activation(zg[:, n % 2, :], ps[:, n, :], ACT.Copy, scale=gains[:, c:c + 1])
                        act.activation(sq[:, n % 2, :], ps[:, n, :], ACT.Square).then_inc(s_zg, 1)
                        if n:
                            root(c, n - 1)
                    root(c, NB - 1)

                def next_hi(c, i, u):
                    act.wait_ge(s_mm, 4 * c)
                    hi_part(c + 1, i + u, 1 - u)

                def chunk_out(c, func, **bias):
                    for n in range(NB):
                        act.wait_ge(s_mm, 4 * c + n + 1)
                        act.wait_ge(s_st[n], 16 * c)
                        act.activation(out[:, n, :], ps[:, n, :], func, **bias).then_inc(s_out, 1)

                next_hi(NQC + 1, (NQC + 1) // 2, 1)
                chunk_out(NQC + 1, ACT.Copy)
                with act.Fori(0, KD - 1) as i:
                    for u in range(2):
                        next_hi(2 * i + NQKV + u, i + NQKV // 2, u)
                        act.activation(bcol[:, u:u + 1], bg[:, bass.ds(2 * i + u, 1)], ACT.Copy).then_inc(s_bcol, 1)
                        act.wait_ge(s_bcol, 2 * i + u + 1)
                        chunk_out(2 * i + NQKV + u, ACT.Sigmoid, bias=bcol[:, u:u + 1])
                next_hi(NC - 2, (NC - 2) // 2, 0)
                chunk_out(NC - 2, ACT.Sigmoid, bias=bg[:, 2 * KD - 2:2 * KD - 1])
                chunk_out(NC - 1, ACT.Sigmoid, bias=bg[:, 2 * KD - 1:2 * KD])

            @block.vector
            def _(dve):
                def lo_part(c, u):
                    dve.wait_ge(s_hi, c + 1)
                    dve.tensor_tensor(w_lo[u][:], w_st[:, u, :, :], w_hi[u][:], ALU.subtract).then_inc(s_lo, 1)

                dve.memset(eps[:], EPS).then_inc(s_eps, 1)
                lo_part(0, 0)
                dve.wait_ge(s_c, 16 * 6)
                for c in range(NQC + 1):
                    lo_part(c + 1, (c + 1) % 2)
                    for n in range(NB):
                        cols = slice(n * BLK, (n + 1) * BLK)
                        done = 4 * (4 * c + n)
                        zc, rc, sc = zg[:, n % 2, :], rot[:, n % 2, :], std[:, n % 2, :]
                        dve.wait_ge(s_ms, 4 * c + n + 1)
                        if c:
                            dve.wait_ge(s_st[n], 16 * c)
                        dve.tensor_tensor(rc, ps_sw[:, n % 2, :], sin[:, cols], ALU.mult).then_inc(s_rope, 1)
                        dve.tensor_tensor(zc, zc, cos[:, cols], ALU.mult).then_inc(s_rope, 1)
                        dve.wait_ge(s_rope, done + 2)
                        dve.tensor_tensor(rc, rc, zc, ALU.add).then_inc(s_rope, 1)
                        dve.wait_ge(s_std, 4 * c + n + 1)
                        dve.reciprocal(sc, sc).then_inc(s_rope, 1)
                        dve.wait_ge(s_rope, done + 4)
                        dve.tensor_tensor(out[:, n, :], rc, sc, ALU.mult).then_inc(s_rot, 1)
                n = 0

                def step(ins):
                    nonlocal n
                    n += 1
                    ins.then_inc(s_dft, 1)
                    dve.wait_ge(s_dft, NV * group + n)

                def add(o, a, b):
                    step(dve.tensor_tensor(o, a, b, ALU.add))

                def sub(o, a, b):
                    step(dve.tensor_tensor(o, a, b, ALU.subtract))

                def axpy(o, c, a, b, op=ALU.add):
                    step(dve.scalar_tensor_tensor(o, a, c, b, ALU.mult, op))

                e, o = (lambda i: eo[:, i, :]), (lambda i: eo[:, 8 + i, :])
                re, im = (lambda k: z[:, k, :]), (lambda k: z[:, 8 + k, :])
                pq = [None] + [(e(n), e(3 + n)) for n in (1, 2, 3)]
                (p1, q1), (p2, q2), (p3, q3) = pq[1:]
                u, v, w = o(1), o(2), o(3)

                def dft_even():
                    dve.wait_ge(s_f, 16 * (group + 1))
                    add(eo[:, 0:8, :], z[:, 0:8, :], z[:, 8:16, :])
                    sub(eo[:, 8:16, :], z[:, 0:8, :], z[:, 8:16, :])
                    t = [z[:, i, :] for i in range(4)]
                    add(z[:, 0:4, :], eo[:, 0:4, :], eo[:, 4:8, :])
                    sub(eo[:, 0:4, :], eo[:, 0:4, :], eo[:, 4:8, :])
                    add(e(4), t[0], t[2])
                    add(e(5), t[1], t[3])
                    sub(re(4), t[0], t[2])
                    sub(im(4), t[3], t[1])
                    add(re(0), e(4), e(5))
                    sub(re(8), e(4), e(5))
                    sub(e(4), e(1), e(3))
                    add(e(5), e(1), e(3))
                    axpy(re(2), C2, e(4), e(0))
                    axpy(re(6), -C2, e(4), e(0))
                    axpy(im(2), -C2, e(5), e(2), ALU.subtract)
                    axpy(im(6), -C2, e(5), e(2))

                def dft_odd_re():
                    for j in (1, 2, 3):
                        sub(pq[j][0], o(j), o(8 - j))
                        add(pq[j][1], o(j), o(8 - j))
                    axpy(u, C2, p2, o(0))
                    axpy(v, -C2, p2, o(0))
                    step(dve.tensor_scalar(w, p3, C3, None, ALU.mult))
                    axpy(w, C1, p1, w)
                    add(re(1), u, w)
                    sub(re(7), u, w)
                    step(dve.tensor_scalar(w, p3, C1, None, ALU.mult))
                    axpy(w, C3, p1, w, ALU.subtract)
                    add(re(3), v, w)
                    sub(re(5), v, w)

                def dft_odd_im():
                    axpy(u, C2, q2, o(4))
                    axpy(v, C2, q2, o(4), ALU.subtract)
                    step(dve.tensor_scalar(w, q3, C1, None, ALU.mult))
                    axpy(w, C3, q1, w)
                    sub(im(7), u, w)
                    add(w, u, w)
                    step(dve.tensor_scalar(im(1), w, -1.0, None, ALU.mult))
                    step(dve.tensor_scalar(w, q3, C3, None, ALU.mult))
                    axpy(w, C1, q1, w, ALU.subtract)
                    sub(im(5), v, w)
                    add(w, v, w)
                    step(dve.tensor_scalar(im(3), w, -1.0, None, ALU.mult))

                def split_z(first):
                    if not first:
                        dve.wait_ge(s_zst, 32 * group)
                    dve.tensor_copy(z_hi, z).then_inc(s_z, 1)
                    dve.wait_ge(s_z, 2 * group + 1)
                    dve.tensor_tensor(z_lo, z, z_hi, ALU.subtract).then_inc(s_z, 1)

                def split_kv(g, first):
                    src = ps_sw[:, 0, :].rearrange("p (t a d) -> p a t d", a=NKV, d=HD)
                    dve.wait_ge(s_tr, g + 1)
                    dve.wait_ge(s_k, 64 * (g + 1))
                    if not first:
                        dve.wait_ge(s_kvst, 16 * NKV * g)
                    for a in range(NKV):
                        at = kv[:, a, 1, :].rearrange("p (t c) -> p t c", c=P)
                        dve.tensor_copy(at[:, :, 0:HD], src[:, a]).then_inc(s_kv, 1)
                        dve.tensor_copy(kv[:, a, 0, :], k_st[:, a, :]).then_inc(s_kv, 1)
                        dve.wait_ge(s_kv, KVS * g + 4 * a + 2)
                        dve.tensor_tensor(at[:, :, HD:P], src[:, a], at[:, :, 0:HD], ALU.subtract).then_inc(s_kv, 1)
                        dve.tensor_tensor(kv[HD:P, a, 0, :], k_st[HD:P, a, :], kv[HD:P, a, 0, :], ALU.subtract)\
                            .then_inc(s_kv, 1)

                def quarter(g, first):
                    nonlocal group, n
                    group, n = g, 0
                    for j, work in enumerate((dft_even, dft_odd_re, dft_odd_im, lambda: split_kv(g, first))):
                        lo_part(PER * g + NQKV + j, j % 2)
                        work()
                        if j == 2:
                            assert n == NV
                            split_z(first)

                group = 0
                quarter(0, True)
                with dve.Fori(1, NG) as g:
                    quarter(g, False)

            @block.tensor
            def _(pe):
                def block_products(n, u):
                    for k in range(KD):
                        m = product3(pe, ps[:, n, :], w_hi[u][:, k, :], w_lo[u][:, k, :],
                                     hT_hi[:, k, n * BLK:(n + 1) * BLK], hT_lo[:, k, n * BLK:(n + 1) * BLK],
                                     k == 0, k == KD - 1)
                    m.then_inc(s_mm, 1)

                def rope_products(c, n):
                    pe.wait_ge(s_zg, 4 * c + n + 1)
                    if c or n >= 2:
                        pe.wait_ge(s_rot, 4 * c + n - 1)
                    pe.matmul(ps_sw[:, n % 2, :], swap, zg[:, n % 2, :], start=True, stop=True)
                    pe.matmul(ps_ms[:, n % 2, :], head_mean, sq[:, n % 2, :], start=True, stop=True).then_inc(s_ms, 1)

                pe.wait_ge(s_c, 16 * 6)
                for c in range(NQC + 2):
                    pe.wait_ge(s_lo, c + 1)
                    for n in range(NB):
                        if c:
                            pe.wait_ge(s_zg, 4 * (c - 1) + n + 1)
                        if c <= NQC and n >= 2:
                            rope_products(c, n - 2)
                        if c and n < 2:
                            rope_products(c - 1, n + 2)
                        block_products(n, c % 2)
                def turn_v(g, first):
                    pe.wait_ge(s_v, 16 * (g + 1))
                    if first:
                        pe.wait_ge(s_rot, NB * (NQC + 1))
                    else:
                        pe.wait_ge(s_kv, KVS * g)
                    for t in range(BLK // P):
                        m = pe.transpose(ps_sw[:, 0, t * P:(t + 1) * P], v_st[:, t * P:(t + 1) * P], ident[:])
                    m.then_inc(s_tr, 1)

                def quarter(g, first):
                    for j in range(PER):
                        c = PER * g + j
                        if j == 2:
                            turn_v(g, first)
                        pe.wait_ge(s_lo, c + NQKV + 1)
                        for n in range(NB):
                            pe.wait_ge(s_out, NB * c + n + 1)
                            block_products(n, j % 2)

                quarter(0, True)
                with pe.Fori(1, NG) as g:
                    quarter(g, False)
        return s_st


def fourier_phase(nc, head0, z_d, t_pos, t_chan, qkv_d, kv_d, ident, yT_d):
    with Res(nc, "fft") as r:
        z_hi, z_lo = (r.sb(n, [P, 2, N1, P], F32R) for n in ("z_hi", "z_lo"))
        tp_st = r.sb("tp_st", [P, K1, 3 * P])
        tp_hi, tp_lo = (r.sb(n, [P, K1, 3 * P], F32R) for n in ("tp_hi", "tp_lo"))
        tc_st = r.sb("tc_st", [P, 3 * P])
        tc_hi, tc_lo = (r.sb(n, [P, 3 * P], F32R) for n in ("tc_hi", "tc_lo"))
        g_hi, g_lo = (r.sb(n, [P, 2, 2, K1, P], F32R) for n in ("g_hi", "g_lo"))
        yT = r.sb("yT", [P, 2, S])
        ps_g = r.ps("ps_g", [P, 2, BLK])
        ps_y = r.ps("ps_y", [P, 4, BLK])
        ps_m = r.ps("ps_m", [P, 2, BLK])
        s_z = [r.sem(f"z_loaded{i}") for i in range(2)]
        s_out = [r.sem(f"y_stored{i}") for i in range(2)]
        s_tp = [r.sem(f"tp_loaded{i}") for i in range(K1 // 3)]
        s_tc, s_tabs, s_g, s_ghi, s_glo, s_y, s_yev = (
            r.sem(n) for n in ("tc_loaded", "table_steps", "g", "g_hi_made", "g_lo_made", "y", "y_copied"))
        NBK = (K1 + 1) // 2
        PIECES = [(0, 3, False), (3, 3, False), (6, 3, False), (1, 4, True), (5, 3, True)]
        NY = len(PIECES)
        steps = [("G", 0, k) for k in range(K1)]
        for g in range(1, NG):
            steps += [("G", g, k) for k in range(K1)] + [("Y", g - 1, j) for j in range(NY)]
        steps += [("Y", NG - 1, j) for j in range(NY)]
        FIRST = 6
        maxima = [[] for _ in steps]
        for m in range(NM):
            maxima[FIRST + m * (len(steps) - 2 - FIRST) // NM].append(m)

        def width(b):
            return min(2, K1 - 2 * b)

        with r.block() as block:

            @block.sync
            def _(sp):
                def load_z(g):
                    if g >= 2:
                        sp.wait_ge(s_g, NBK * (g - 1))
                    for part, dst in enumerate((z_hi, z_lo)):
                        sp.dma_start(dst[:, g % 2, :, :].rearrange("p n c -> p (n c)").bitcast(F32), z_d[part, g])\
                            .then_inc(s_z[g % 2], 16)

                def store_y(g):
                    sp.wait_ge(s_yev, NY * (g + 1))
                    sp.dma_start(yT_d[g], yT[:, g % 2, :]).then_inc(s_out[g % 2], 16)

                for k in range(0, K1, 3):
                    sp.dma_start(tp_st[:, k:k + 3, :], t_pos[:, k:k + 3, :]).then_inc(s_tp[k // 3], 16)
                    if k == 0:
                        load_z(0)
                load_q(sp, head0, qkv_d, 0)
                sp.dma_start(head0.kmax[:, 0, :].bitcast(F32), kv_d[0, :, 0, :]).then_inc(head0.s_km, 16)
                sp.dma_start(tc_st[:], t_chan).then_inc(s_tc, 16)
                load_z(1)
                sp.dma_start(head0.kmax[:, 1, :].bitcast(F32), kv_d[1, :, 0, :]).then_inc(head0.s_km, 16)
                load_kv(sp, head0, head0.kv, 0, kv_d, 0)
                sp.wait_ge(head0.s_q2, NB)
                load_q(sp, head0, qkv_d, 1)
                for g in range(NG):
                    if g + 2 < NG:
                        load_z(g + 2)
                    store_y(g)
                place_row(sp, head0, 0, head0.q2, 0)
                for i in range(2):
                    sp.wait_ge(s_out[i], 16 * NG // 2)

            @block.scalar
            def _(act):
                def high_part(g, b):
                    act.wait_ge(s_g, NBK * g + b + 1)
                    if g >= 2:
                        act.wait_ge(s_y, NY * (g - 1))
                    m = width(b)
                    act.activation(g_hi[:, g % 2, :, 2 * b:2 * b + m, :].rearrange("p c k m -> p k c m"),
                                   ps_g[:, (NBK * g + b) % 2, 0:m * 2 * P].rearrange("p (k c m) -> p k c m", k=m, c=2),
                                   ACT.Copy).then_inc(s_ghi, 1)

                def copy_y(g, j):
                    kk, m, mirrored = PIECES[j]
                    at = yT[:, g % 2, :].rearrange("p (k2 k1) -> p k1 k2", k1=N1)
                    act.wait_ge(s_y, NY * g + j + 1)
                    if g >= 2:
                        act.wait_ge(s_out[g % 2], 16 * (g // 2))
                    src = ps_y[:, (NY * g + j) % 4, 0:m * P].rearrange("p (k m) -> p k m", k=m)
                    dst = at[:, kk:kk + m, :]
                    if mirrored:
                        dst = at[:, N1 - kk - m + 1:N1 - kk + 1, :][:, ::-1, ::-1]
                    act.activation(dst, src, ACT.Copy).then_inc(s_yev, 1)

                for kind, g, i in steps:
                    if kind == "Y":
                        copy_y(g, i)
                    elif i % 2 or i == K1 - 1:
                        high_part(g, i // 2)

            @block.vector
            def _(dve):
                def split_table(n, hi, lo, src):
                    dve.tensor_copy(hi, src).then_inc(s_tabs, 1)
                    dve.wait_ge(s_tabs, 2 * n + 1)
                    dve.tensor_tensor(lo, src, hi, ALU.subtract).then_inc(s_tabs, 1)

                def split_q(piece):
                    cols = slice(piece * BLK, (piece + 1) * BLK)
                    dve.tensor_copy(head0.q1[:, cols], head0.q_st[:, cols]).then_inc(head0.s_q1, 1)
                    dve.wait_ge(head0.s_q1, piece + 1)
                    dve.tensor_tensor(head0.q2[0:HD, cols], head0.q_st[0:HD, cols], head0.q1[0:HD, cols], ALU.subtract)\
                        .then_inc(head0.s_q2, 1)

                def low_part(g, b):
                    m = width(b)
                    c = NBK * g + b
                    dve.wait_ge(s_ghi, c + 1)
                    dve.tensor_tensor(g_lo[:, g % 2, :, 2 * b:2 * b + m, :].rearrange("p c k m -> p k c m"),
                                      ps_g[:, c % 2, 0:m * 2 * P].rearrange("p (k c m) -> p k c m", k=m, c=2),
                                      g_hi[:, g % 2, :, 2 * b:2 * b + m, :].rearrange("p c k m -> p k c m"),
                                      ALU.subtract).then_inc(s_glo, 1)

                def read_max(m):
                    dve.wait_ge(head0.s_m, m + 1)
                    dve.tensor_reduce(head0.mx[:, m:m + 1], ps_m[:, m % 2, :], AX.X, ALU.max).then_inc(head0.s_mr, 1)

                for k in range(K1):
                    dve.wait_ge(s_tp[k // 3], 16)
                    split_table(k, tp_hi[:, k, :], tp_lo[:, k, :], tp_st[:, k, :])
                dve.wait_ge(head0.s_q, 32)
                for piece in range(NB):
                    split_q(piece)
                dve.wait_ge(s_tc, 16)
                split_table(K1, tc_hi[:], tc_lo[:], tc_st[:])
                behind = None
                for n, (kind, g, i) in enumerate(steps):
                    for m in maxima[n]:
                        read_max(m)
                    if behind is not None:
                        low_part(*behind)
                    behind = (g, i // 2) if kind == "G" and (i % 2 or i == K1 - 1) else None
                    if n == FIRST:
                        constant_rows(dve, head0, head0.kv, head0.q2, 0)
                dve.wait_ge(head0.s_mr, NM)
                dve.tensor_reduce(head0.mx2[:], head0.mx[:].rearrange("p (t a) -> p t a", a=NB), AX.X, ALU.max)\
                    .then_inc(head0.s_m2, 1)
                dve.wait_ge(head0.s_mt, 1)
                dve.tensor_scalar(head0.mrow[:], ps_m[0:NT, 0, 0:P], -1.0, None, ALU.mult).then_inc(head0.s_mc, 1)

            @block.tensor
            def _(pe):
                def g_products(g, k):
                    c = NBK * g + k // 2
                    if k == 0:
                        pe.wait_ge(s_z[g % 2], 32 * (g // 2 + 1))
                    if k % 2 == 0 and c >= 2:
                        pe.wait_ge(s_glo, c - 1)
                    if g == 0:
                        pe.wait_ge(s_tabs, 2 * k + 2)
                    at = ps_g[:, c % 2, (k % 2) * 2 * P:(k % 2 + 1) * 2 * P]
                    imag = 0 < k < K1 - 1
                    q = product3(pe, at, z_hi[:, g % 2, k, :], z_lo[:, g % 2, k, :], tp_hi[:, k, P:3 * P],
                                 tp_lo[:, k, P:3 * P], True, not imag)
                    if imag:
                        q = product3(pe, at, z_hi[:, g % 2, 8 + k, :], z_lo[:, g % 2, 8 + k, :], tp_hi[:, k, 0:2 * P],
                                     tp_lo[:, k, 0:2 * P], False, True)
                    if k % 2 or k == K1 - 1:
                        q.then_inc(s_g, 1)

                def y_products(g, j):
                    kk, m, mirrored = PIECES[j]
                    n = NY * g + j
                    if j == 0:
                        pe.wait_ge(s_glo, NBK * (g + 1))
                    if n == 0:
                        pe.wait_ge(s_tabs, 2 * K1 + 2)
                    if n >= 4:
                        pe.wait_ge(s_yev, n - 3)
                    sine = slice(2 * P, 3 * P) if mirrored else slice(P, 2 * P)
                    at = ps_y[:, n % 4, 0:m * P]
                    product3(pe, at, tc_hi[:, 0:P], tc_lo[:, 0:P], g_hi[:, g % 2, 0, kk:kk + m, :],
                             g_lo[:, g % 2, 0, kk:kk + m, :], True, False)
                    product3(pe, at, tc_hi[:, sine], tc_lo[:, sine], g_hi[:, g % 2, 1, kk:kk + m, :],
                             g_lo[:, g % 2, 1, kk:kk + m, :], False, True).then_inc(s_y, 1)

                def max_scores(m):
                    tile, quarter = divmod(m, NB)
                    if m == 0:
                        pe.wait_ge(head0.s_km, 16)
                    if quarter == 0 and tile % (NT // NB) == 0:
                        pe.wait_ge(head0.s_q1, tile // (NT // NB) + 1)
                    if m >= 2:
                        pe.wait_ge(head0.s_mr, m - 1)
                    pe.matmul(ps_m[:, m % 2, :], head0.q1[:, tile * P:(tile + 1) * P],
                              head0.kmax[:, 0, quarter * BLK:(quarter + 1) * BLK], start=True, stop=True)\
                        .then_inc(head0.s_m, 1)

                for n, (kind, g, i) in enumerate(steps):
                    (g_products if kind == "G" else y_products)(g, i)
                    for m in maxima[n]:
                        max_scores(m)
                pe.wait_ge(head0.s_m2, 1)
                pe.transpose(ps_m[0:NT, 0, 0:P], head0.mx2[:], ident[:]).then_inc(head0.s_mt, 1)
                pe.wait_ge(head0.s_km, 16 * NKV)


class Head0:

    def __init__(self, r):
        self.kv = r.sb("kv", [P, 3, S], F32R)
        self.kmax = r.sb("kmax", [P, NKV, S], F32R)
        self.q_st = r.sb("q_st", [P, S])
        self.q1, self.q2 = r.sb("q1", [P, S], F32R), r.sb("q2", [P, S], F32R)
        self.mx, self.mx2, self.mrow = r.sb("mx", [P, NM]), r.sb("mx2", [P, NT]), r.sb("mrow", [NT, P], F32R)
        self.s_q, self.s_km, self.s_zero = r.sem("q_loaded"), r.sem("kmax_loaded"), r.sem("constant_rows")
        self.s_kv = [r.sem(f"kv_loaded{i}") for i in range(2)]
        self.s_row = [r.sem(f"row_placed{i}") for i in range(2)]
        self.s_q1, self.s_q2 = r.sem("q1_made"), r.sem("q2_made")
        self.s_m, self.s_mr, self.s_m2 = r.sem("max_scores"), r.sem("max_read"), r.sem("max_of_row")
        self.s_mt, self.s_mc = r.sem("max_turned"), r.sem("max_row")


def load_q(sp, head0, qkv_d, h):
    for half in range(2):
        src = qkv_d[h // 2, (h % 2) * HD:(h % 2 + 1) * HD, :]
        sp.dma_start(head0.q_st[half * HD:(half + 1) * HD, :], src).then_inc(head0.s_q, 16)


def load_kv(sp, head0, slot, u, kv_d, g):
    sp.dma_start(slot[:, 0:2, :].bitcast(F32), kv_d[g]).then_inc(head0.s_kv[u], 16)
    sp.dma_start(slot[0:HD, 2, :].bitcast(F32), kv_d[g, 0:HD, 0, :]).then_inc(head0.s_kv[u], 16)


def place_row(sp, head0, h, q2, u):
    sp.wait_ge(head0.s_mc, h + 1)
    sp.dma_start(q2[HD:HD + 1, :].bitcast(F32), head0.mrow[:].bitcast(F32)).then_inc(head0.s_row[u], 16)


def constant_rows(dve, head0, kv, q2, u):
    dve.memset(q2[HD:P, :].bitcast(F32), 0.0).then_inc(head0.s_zero, 1)
    dve.memset(kv[HD:P, 2, :].bitcast(F32), 0.0).then_inc(head0.s_zero, 1)
    dve.wait_ge(head0.s_zero, 3 * u + 2)
    dve.memset(kv[HD:HD + 1, 2, :].bitcast(F32), 1.0).then_inc(head0.s_zero, 1)
    dve.wait_ge(head0.s_zero, 3 * u + 3)


def attention_phase(nc, head0, qkv_d, kv_d, ident, ones, o_d, sums_d):
    KP = NT // 2
    ST = NB * KP
    LAG = 4
    LO_LAG = 2
    FIRST, LAST = 1, 27
    subs = [[] for _ in range(ST)]
    for m in range(NM):
        subs[FIRST + m * (LAST + 1 - FIRST) // NM].append(m)
    SPLIT = [0, 5, 11, 17]
    SCALE = HD ** -0.5
    with Res(nc, "att") as r:
        kmax, q_st, mx, mx2, mrow = head0.kmax, head0.q_st, head0.mx, head0.mx2, head0.mrow
        kv = [head0.kv, r.sb("kv1", [P, 3, S], F32R)]
        q1 = [head0.q1, r.sb("q1_1", [P, S], F32R)]
        q2 = [head0.q2, r.sb("q2_1", [P, S], F32R)]
        prob = r.sb("prob", [P, 8, 2 * BLK])
        prob_hi = r.sb("prob_hi", [P, 4, 2 * BLK], F32R)
        prob_lo = r.sb("prob_lo", [P, 4, 2 * BLK], F32R)
        acc = r.sb("acc", [P, 2, 2 * BLK])
        o_sb = r.sb("o_sb", [P, 2, BLK])
        row = r.sb("row", [1, 2, BLK])
        ps_s = r.ps("ps_s", [P, 2, 2 * BLK])
        ps_m = r.ps("ps_m", [P, 2, BLK])
        ps_o = r.ps("ps_o", [P, BLK])
        ps_r = r.ps("ps_r", [P, BLK])
        s_q, s_kv, s_zero, s_q1, s_q2 = head0.s_q, head0.s_kv, head0.s_zero, head0.s_q1, head0.s_q2
        s_m, s_mr, s_m2, s_mt, s_mc, s_row = head0.s_m, head0.s_mr, head0.s_m2, head0.s_mt, head0.s_mc, head0.s_row
        s_s, s_exp, s_hi, s_lo, s_pv = (r.sem(n) for n in ("scores", "exp", "p_hi", "p_lo", "pv"))
        s_add, s_sum, s_rc, s_oc = (r.sem(n) for n in ("added", "sum", "sum_copied", "o_copied"))
        s_st = [r.sem(f"o_stored{i}") for i in range(2)]
        s_rst = [r.sem(f"sum_stored{i}") for i in range(2)]
        with r.block() as block:

            @block.sync
            def _(sp):
                def store(h, qb, first=False):
                    sp.wait_ge(s_oc, NB * h + qb + 1)
                    at = o_d[:, bass.ds(h, 1), :, qb * BLK:(qb + 1) * BLK]
                    for half in range(2):
                        sp.dma_start(at[half:half + 1].rearrange("a h d q -> (a h d) q"),
                                     o_sb[half * HD:(half + 1) * HD, qb % 2, :]).then_inc(s_st[qb % 2], 16)
                    sp.wait_ge(s_rc, NB * h + qb + 1)
                    sp.dma_start(sums_d[bass.ds(h, 1), qb * BLK:(qb + 1) * BLK], row[:, qb % 2, :])\
                        .then_inc(s_rst[qb % 2], 16)

                def body(h, u, is_first, has_next):
                    if has_next:
                        if not is_first:
                            sp.wait_ge(s_pv, ST * h)
                        load_kv(sp, head0, kv[1 - u], 1 - u, kv_d, (h + 1) * NKV // NH)
                    if not is_first:
                        store(h - 1, NB - 1)
                    for qb in range(NB - 1):
                        if h + 2 < NH and qb == NB - 2:
                            sp.wait_ge(s_q2, NB * (h + 2))
                            load_q(sp, head0, qkv_d, h + 2)
                        store(h, qb)
                    if has_next:
                        place_row(sp, head0, h + 1, q2[1 - u], 1 - u)

                for h in range(NH):
                    body(h, h % 2, h == 0, h + 1 < NH)
                store(NH - 1, NB - 1)
                for i in range(2):
                    sp.wait_ge(s_st[i], 16 * NH * NB)
                    sp.wait_ge(s_rst[i], 8 * NH * NB)

            @block.scalar
            def _(act):
                def exp(h, s):
                    g = ST * h + s
                    act.wait_ge(s_s, g + 1)
                    if not isinstance(g, int) or g >= 8:
                        act.wait_ge(s_lo, g - 7)
                        old = s - 8
                        act.wait_ge(s_add, ST * h + (old // KP) * KP + max(old % KP, 1))
                    act.activation(prob[:, s % 8, :], ps_s[:, s % 2, :], ACT.Exp, scale=SCALE).then_inc(s_exp, 1)

                def hi(h, s):
                    g = ST * h + s
                    act.wait_ge(s_exp, g + 1)
                    if not isinstance(g, int) or g >= 4:
                        act.wait_ge(s_pv, g - 3)
                    act.activation(prob_hi[:, s % 4, :], prob[:, s % 8, :], ACT.Copy).then_inc(s_hi, 1)

                def o_copy(h, qb):
                    n = NB * h + qb
                    act.wait_ge(s_pv, KP * (n + 1))
                    if not isinstance(n, int) or n >= 2:
                        act.wait_ge(s_st[qb % 2], 32 * (NB // 2 * h + qb // 2))
                    act.activation(o_sb[:, qb % 2, :], ps_o[:], ACT.Copy).then_inc(s_oc, 1)

                def sum_copy(h, qb):
                    n = NB * h + qb
                    act.wait_ge(s_sum, n + 1)
                    if not isinstance(n, int) or n >= 2:
                        act.wait_ge(s_rst[qb % 2], 16 * (NB // 2 * h + qb // 2))
                    act.activation(row[:, qb % 2, :], ps_r[0:1, :], ACT.Copy).then_inc(s_rc, 1)

                def body(h, first_head):
                    for s in range(ST):
                        if s % KP == LAG and not (first_head and s < KP):
                            o_copy(*((h, s // KP - 1) if s >= KP else (h - 1, NB - 1)))
                        exp(h, s)
                        if s % KP == LAG + 2 and not (first_head and s < KP):
                            sum_copy(*((h, s // KP - 1) if s >= KP else (h - 1, NB - 1)))
                        if s:
                            hi(h, s - 1)
                        elif not first_head:
                            hi(h - 1, ST - 1)

                body(0, True)
                with act.Fori(1, NH) as h:
                    body(h, False)
                hi(NH - 1, ST - 1)
                o_copy(NH - 1, NB - 1)
                sum_copy(NH - 1, NB - 1)

            @block.gpsimd
            def _(pool):
                def body(h, first_head):
                    for qb in range(NB):
                        for kp in range(1, KP):
                            s = qb * KP + kp
                            n = ST * h + qb * KP
                            pool.wait_ge(s_exp, ST * h + s + 1)
                            if kp == 1:
                                if not (first_head and qb < 2):
                                    pool.wait_ge(s_sum, NB * h + qb - 1)
                                pool.tensor_tensor(acc[:, qb % 2, :], prob[:, (s - 1) % 8, :], prob[:, s % 8, :],
                                                   ALU.add).then_inc(s_add, 1)
                            else:
                                pool.wait_ge(s_add, n + kp - 1)
                                pool.tensor_tensor(acc[:, qb % 2, :], acc[:, qb % 2, :], prob[:, s % 8, :],
                                                   ALU.add).then_inc(s_add, 1)
                        pool.wait_ge(s_add, n + KP - 1)
                        pool.tensor_tensor(acc[:, qb % 2, 0:BLK], acc[:, qb % 2, 0:BLK], acc[:, qb % 2, BLK:2 * BLK],
                                           ALU.add).then_inc(s_add, 1)

                body(0, True)
                with pool.Fori(1, NH) as h:
                    body(h, False)

            @block.vector
            def _(dve):
                def split_q_hi(u, piece):
                    cols = slice(piece * BLK, (piece + 1) * BLK)
                    dve.tensor_copy(q1[u][:, cols], q_st[:, cols]).then_inc(s_q1, 1)

                def split_q_lo(h, u, piece):
                    cols = slice(piece * BLK, (piece + 1) * BLK)
                    dve.wait_ge(s_q1, NB * h + piece + 1)
                    dve.tensor_tensor(q2[u][0:HD, cols], q_st[0:HD, cols], q1[u][0:HD, cols], ALU.subtract)\
                        .then_inc(s_q2, 1)

                def read_max(h, m):
                    dve.wait_ge(s_m, NM * h + m + 1)
                    dve.tensor_reduce(mx[:, m:m + 1], ps_m[:, m % 2, :], AX.X, ALU.max).then_inc(s_mr, 1)

                def row_max(h):
                    dve.wait_ge(s_mr, NM * (h + 1))
                    dve.tensor_reduce(mx2[:], mx[:].rearrange("p (t a) -> p t a", a=NB), AX.X, ALU.max).then_inc(s_m2, 1)

                def row_copy(h):
                    dve.wait_ge(s_mt, h + 1)
                    dve.wait_ge(s_s, ST * (h - 1) + 1)
                    dve.tensor_scalar(mrow[:], ps_r[0:NT, 0:P], -1.0, None, ALU.mult).then_inc(s_mc, 1)

                def lo(h, s):
                    dve.wait_ge(s_hi, ST * h + s + 1)
                    dve.tensor_tensor(prob_lo[:, s % 4, :], prob[:, s % 8, :], prob_hi[:, s % 4, :], ALU.subtract)\
                        .then_inc(s_lo, 1)

                def body(h, u, first_head, has_next):
                    for s in range(ST):
                        if has_next and s in SPLIT:
                            if s == 0:
                                dve.wait_ge(s_q, 32 * (h + 2))
                                if not first_head:
                                    dve.wait_ge(s_s, ST * h)
                            split_q_hi(1 - u, SPLIT.index(s))
                        if has_next:
                            for m in subs[s][:2]:
                                read_max(h + 1, m)
                        if s >= LO_LAG:
                            lo(h, s - LO_LAG)
                        elif not first_head:
                            lo(h - 1, ST + s - LO_LAG)
                        if has_next:
                            if s in SPLIT:
                                split_q_lo(h + 1, 1 - u, SPLIT.index(s))
                            for m in subs[s][2:]:
                                read_max(h + 1, m)
                            if s == LAST:
                                row_max(h + 1)
                            if s == LAST + 1:
                                row_copy(h + 1)

                constant_rows(dve, head0, kv[1], q2[1], 1)
                body(0, 0, True, True)
                body(1, 1, False, True)
                with dve.Fori(1, NH // 2 - 1) as i:
                    for u in range(2):
                        body(2 * i + u, u, False, True)
                body(NH - 2, 0, False, True)
                body(NH - 1, 1, False, False)
                for s in range(ST - LO_LAG, ST):
                    lo(NH - 1, s)

            @block.tensor
            def _(pe):
                def scores(h, u, s):
                    g = ST * h + s
                    qb, kp = divmod(s, KP)
                    cols = slice(qb * BLK, (qb + 1) * BLK)
                    if not isinstance(g, int) or g >= 2:
                        pe.wait_ge(s_exp, g - 1)
                    for j in range(2):
                        keys = slice((2 * kp + j) * P, (2 * kp + j + 1) * P)
                        at = ps_s[:, s % 2, j * BLK:(j + 1) * BLK]
                        pe.matmul(at, kv[u][:, 0, keys], q1[u][:, cols], start=True, stop=False)
                        m = pe.matmul(at, kv[u][:, 2, keys], q2[u][:, cols], start=False, stop=True)
                    m.then_inc(s_s, 1)

                def maxima(h, u, m, g):
                    tile, quarter = divmod(m, NB)
                    if quarter == 0 and tile % (NT // NB) == 0:
                        pe.wait_ge(s_q1, NB * h + tile // (NT // NB) + 1)
                    pe.wait_ge(s_mr, NM * h + m - 1)
                    pe.matmul(ps_m[:, m % 2, :], q1[u][:, tile * P:(tile + 1) * P],
                              kmax[:, g, quarter * BLK:(quarter + 1) * BLK], start=True, stop=True).then_inc(s_m, 1)

                def turn_max(h):
                    pe.wait_ge(s_m2, h + 1)
                    pe.wait_ge(s_rc, NB * (h - 1) + NB - 2)
                    pe.transpose(ps_r[0:NT, 0:P], mx2[:], ident[:]).then_inc(s_mt, 1)

                def pv(h, u, s):
                    qb, kp = divmod(s, KP)
                    pe.wait_ge(s_lo, ST * h + s + 1)
                    if kp == 0 and (not isinstance(h, int) or h or qb):
                        pe.wait_ge(s_oc, NB * h + qb)
                    for j in range(2):
                        t = 2 * kp + j
                        v = kv[u][:, 1, t * P:(t + 1) * P]
                        for part, src in enumerate((prob_hi, prob_lo)):
                            m = pe.matmul(ps_o[:], v, src[:, s % 4, j * BLK:(j + 1) * BLK],
                                          start=t == 0 and part == 0, stop=t == NT - 1 and part == 1)
                    m.then_inc(s_pv, 1)

                def row_sum(h, qb):
                    n = NB * h + qb
                    pe.wait_ge(s_add, KP * (n + 1))
                    if not isinstance(n, int) or n:
                        pe.wait_ge(s_rc, n)
                    if qb == NB - 2 and not (isinstance(h, int) and h == NH - 1):
                        pe.wait_ge(s_mc, h + 2)
                    pe.matmul(ps_r[:], ones[:], acc[:, qb % 2, 0:BLK], start=True, stop=True).then_inc(s_sum, 1)

                def body(i, u, has_next, first_head=False):
                    h = 2 * i + u
                    pe.wait_ge(s_kv[u], 32 * i + 32)
                    pe.wait_ge(s_row[u], 16 * i + 16)
                    pe.wait_ge(s_q2, NB * (h + 1))
                    g = ((h + 1) * NKV // NH) if isinstance(h, int) else bass.ds((h + 1) // (NH // NKV), 1)

                    def maxima_of_step(s, a, b):
                        if has_next:
                            for m in subs[s][a:b]:
                                maxima(h + 1, 1 - u, m, g)

                    for s in range(ST):
                        maxima_of_step(s, 0, 1)
                        scores(h, u, s)
                        maxima_of_step(s, 1, 2)
                        if has_next and s == LAST + 1:
                            turn_max(h + 1)
                        if s >= LAG:
                            pv(h, u, s - LAG)
                        elif not first_head:
                            pv(h - 1, 1 - u, ST + s - LAG)
                        maxima_of_step(s, 2, 3)
                        if s % KP == LAG + 1 and not (first_head and s < KP):
                            row_sum(*((h, s // KP - 1) if s >= KP else (h - 1, NB - 1)))

                body(0, 0, True, True)
                body(0, 1, True)
                with pe.Fori(1, NH // 2 - 1) as i:
                    for u in range(2):
                        body(i, u, True)
                body(NH // 2 - 1, 0, True)
                body(NH // 2 - 1, 1, False)
                for s in range(ST - LAG, ST):
                    pv(NH - 1, 1, s)
                row_sum(NH - 1, NB - 1)


def merge_phase(nc, x_d, w_branch, w_out_d, o_d, sums_d, rec_d, yT_d, gates_d, gate_rows, x1_d, first_sem, kept):
    TB = BLK // P
    KB = NQC
    AS = 6
    with Res(nc, "merge") as r:
        w_st = r.sb("w_st", [P, 2, D])
        wb_hi, wb_lo = (r.sb(n, [P, 2, KD, P], F32R) for n in ("wb_hi", "wb_lo"))
        wo_hi, wo_lo = (r.sb(n, [P, KD, D], F32R) for n in ("wo_hi", "wo_lo"))
        st_a, st_b = (r.sb(n, [P, KB, BLK]) for n in ("st_a", "st_b"))
        act_hi, act_lo = (r.sb(n, [P, KD, BLK], F32R) for n in ("act_hi", "act_lo"))
        mg_hi, mg_lo = (r.sb(n, [P, KD, BLK], F32R) for n in ("mg_hi", "mg_lo"))
        gate = r.sb("gate", [P, 2, 2, BLK])
        g1 = r.sb("g1", [P, D])
        x = r.sb("x", [P, 2, D])
        x1 = r.sb("x1", [P, 2, D])
        junk = r.sb("junk", [P, D], mybir.dt.bfloat16)
        sums, mean, std, rstd = (r.sb(n, [P, 2]) for n in ("sums", "mean", "std", "rstd"))
        ps_b = r.ps("ps_b", [P, 2, 2, BLK])
        ps_y = r.ps("ps_y", [P, 2, D])
        s_w = [r.sem(f"w_loaded{i}") for i in range(2)]
        s_gate = [r.sem(f"gates_loaded{i}") for i in range(2)]
        s_x = [r.sem(f"x_loaded{i}") for i in range(2)]
        s_st = [r.pool_dma_sem(f"x1_stored{i}") for i in range(2)]
        s_o, s_yt, s_g1 = r.sem("o_loaded"), r.sem("yT_loaded"), r.sem("g1_loaded")
        s_sums, s_rec, s_recst, s_rb = (r.sem(n) for n in ("sums_loaded", "rec_made", "rec_stored", "rec_loaded"))
        total = r.sb("total", [P, NH * S // P])
        s_whi, s_wlo, s_act, s_br, s_mg, s_y = (
            r.sem(n) for n in ("w_hi_made", "w_lo_made", "act_steps", "branch", "merge_steps", "y"))
        s_sq, s_mean, s_std, s_rstd, s_n1, s_x1 = (r.sem(n) for n in ("squares", "mean", "root", "rstd", "scaled", "x1"))
        with r.block() as block:

            @block.sync
            def _(sp):
                def load_w(src, i, u, first):
                    if not first:
                        sp.wait_ge(s_wlo, 2 * i + u - 1)
                    sp.dma_start(w_st[:, u, :], src).then_inc(s_w[u], 16)

                def load_o(b):
                    cols = bass.ds(b * BLK, BLK)
                    if not isinstance(b, int) or b:
                        sp.wait_ge(s_act, AS * b)
                    for half, dst in ((0, st_a), (1, st_b)):
                        for t in range(2):
                            src = o_d[half].rearrange("(c t) d s -> t d c s", t=2)[t][:, :, cols]
                            sp.dma_start(dst[t * HD:(t + 1) * HD, :, :], src).then_inc(s_o, 16)

                def load_y(b):
                    sp.wait_ge(s_act, AS * b + 1)
                    for t in range(2):
                        src = rec_d.rearrange("(c t) s -> t c s", t=2)[t:t + 1, :, bass.ds(b * BLK, BLK)]
                        sp.dma_start(st_b[t * HD:(t + 1) * HD, :, :], src.broadcast_to([HD, KB, BLK])).then_inc(s_rb, 16)
                    sp.wait_ge(s_act, AS * b + 2)
                    sp.dma_start(st_b[:], yT_d.rearrange("g c s -> c g s")[:, :, bass.ds(b * BLK, BLK)])\
                        .then_inc(s_yt, 16)

                def body(b, last):
                    for m in range(KD):
                        if m >= 2:
                            load_w(w_branch[m], KD // 2 * (b + 1) + m // 2, m % 2, False)
                        if m >= 2 or not isinstance(b, int) or b:
                            sp.wait_ge(s_mg, 5 * (KD * b + m - 1))
                        for j in range(2):
                            at = gates_d[bass.ds(b, 1), 2 * m + j, :, :].rearrange("o p s -> (o p) s")
                            sp.dma_start(gate[:, m % 2, j, :], at).then_inc(s_gate[m % 2], 16)
                    if not last:
                        load_o(b + 1)
                        for u in range(2):
                            load_w(w_branch[u], KD // 2 * (b + 2), u, False)
                    for j in range(TB):
                        n = TB * b + j
                        if j >= 2 or not isinstance(b, int) or b:
                            sp.wait_ge(s_x1, n - 1)
                        sp.dma_start(x[:, j % 2, :], x_d[bass.ds(n, 1), :, :].rearrange("o p d -> (o p) d"))\
                            .then_inc(s_x[j % 2], 16)
                        if j == 0 and not last:
                            load_y(b + 1)
                sp.sem_clear(range(first_sem, kept[0].num))
                sp.sem_clear(range(kept[-1].num + 1, min(r.sem_nums)))
                sp.dma_start(total[:], sums_d.rearrange("h (a b) -> (h a) b", b=P)).then_inc(s_sums, 16)
                sp.dma_start(g1[:], gate_rows).then_inc(s_g1, 16)
                for k in range(KD):
                    load_w(w_out_d[k], k // 2, k % 2, k < 2)
                sp.wait_ge(s_rec, 1)
                sp.dma_start(rec_d.rearrange("h (a b) -> (h a) b", b=P), total[:]).then_inc(s_recst, 16)
                sp.wait_ge(s_recst, 16)
                load_o(0)
                for m in range(2):
                    load_w(w_branch[m], KD // 2, m, False)
                load_y(0)
                body(0, False)
                with sp.Fori(1, NB - 1) as b:
                    body(b, False)
                body(NB - 1, True)

            @block.gpsimd
            def _(pool):
                with pool.Fori(0, NB) as b:
                    for j in range(TB):
                        pool.wait_ge(s_x1, TB * b + j + 1)
                        pool.dma_start(x1_d[bass.ds(TB * b + j, 1), :, :].rearrange("o p d -> (o p) d"), x1[:, j % 2, :])\
                            .then_inc(s_st[j % 2], 16)
                for i in range(2):
                    pool.wait_ge(s_st[i], 16 * NT // 2)

            @block.scalar
            def _(act):
                def hi_part(dst, i, u):
                    act.wait_ge(s_w[u], 16 * i + 16)
                    act.activation(dst, w_st[:, u, :], ACT.Copy).then_inc(s_whi, 1)

                def branch_hi(b, m):
                    if m >= 2 or not isinstance(b, int) or b:
                        act.wait_ge(s_br, KD * b + m - 1)
                    hi_part(wb_hi[:, m % 2, :, :].rearrange("p k m -> p (k m)"), KD // 2 * (b + 1) + m // 2, m % 2)

                def body(b, last):
                    for m in range(KD):
                        if m < KD - 1:
                            branch_hi(b, m + 1)
                        elif not last:
                            branch_hi(b + 1, 0)
                    for j in range(TB):
                        n = TB * b + j
                        act.wait_ge(s_y, n + 1)
                        if j or not isinstance(b, int) or b:
                            act.wait_ge(s_sq, n)
                        act.activation(junk[:], ps_y[:, j % 2, :], ACT.Square, accum_out=sums[:, j % 2:j % 2 + 1])\
                            .then_inc(s_sq, 1)
                        act.wait_ge(s_mean, n + 1)
                        act.activation(std[:, j % 2:j % 2 + 1], mean[:, j % 2:j % 2 + 1], ACT.Sqrt).then_inc(s_std, 1)

                for k in range(KD):
                    hi_part(wo_hi[:, k, :], k // 2, k % 2)
                branch_hi(0, 0)
                body(0, False)
                with act.Fori(1, NB - 1) as b:
                    body(b, False)
                body(NB - 1, True)

            @block.vector
            def _(dve):
                def branch_lo(b, m):
                    piece = KD * (b + 1) + m
                    dve.wait_ge(s_whi, piece + 1)
                    dve.tensor_tensor(wb_lo[:, m % 2, :, :].rearrange("p k m -> p (k m)"), w_st[:, m % 2, :],
                                      wb_hi[:, m % 2, :, :].rearrange("p k m -> p (k m)"), ALU.subtract).then_inc(s_wlo, 1)

                def split_acts(b):
                    n = AS * b
                    dve.wait_ge(s_o, 64 * (b + 1))
                    if not isinstance(b, int) or b:
                        dve.wait_ge(s_br, KD * b)
                    dve.tensor_tensor(st_a[:], st_a[:], st_b[:], ALU.add).then_inc(s_act, 1)
                    dve.wait_ge(s_act, n + 1)
                    dve.wait_ge(s_rb, 32 * (b + 1))
                    dve.tensor_tensor(st_a[:], st_a[:], st_b[:], ALU.mult).then_inc(s_act, 1)
                    dve.wait_ge(s_act, n + 2)
                    dve.tensor_copy(act_hi[:, 0:KB, :], st_a[:]).then_inc(s_act, 1)
                    dve.wait_ge(s_act, n + 3)
                    dve.tensor_tensor(act_lo[:, 0:KB, :], st_a[:], act_hi[:, 0:KB, :], ALU.subtract).then_inc(s_act, 1)
                    dve.wait_ge(s_yt, 16 * (b + 1))
                    dve.tensor_copy(act_hi[:, KB:KD, :], st_b[:]).then_inc(s_act, 1)
                    dve.wait_ge(s_act, n + 5)
                    dve.tensor_tensor(act_lo[:, KB:KD, :], st_b[:], act_hi[:, KB:KD, :], ALU.subtract).then_inc(s_act, 1)

                def merge(b, m):
                    n = 5 * (KD * b + m)
                    dve.wait_ge(s_gate[m % 2], 32 * (KD // 2 * b + m // 2 + 1))
                    dve.wait_ge(s_br, KD * b + m + 1)
                    if m == 0 and (not isinstance(b, int) or b):
                        dve.wait_ge(s_y, TB * b)
                    ga, gf = gate[:, m % 2, 0, :], gate[:, m % 2, 1, :]
                    dve.tensor_tensor(ga, ps_b[:, m % 2, 0, :], ga, ALU.mult).then_inc(s_mg, 1)
                    dve.tensor_tensor(gf, ps_b[:, m % 2, 1, :], gf, ALU.mult).then_inc(s_mg, 1)
                    dve.wait_ge(s_mg, n + 2)
                    dve.tensor_tensor(ga, ga, gf, ALU.add).then_inc(s_mg, 1)
                    dve.wait_ge(s_mg, n + 3)
                    dve.tensor_copy(mg_hi[:, m, :], ga).then_inc(s_mg, 1)
                    dve.wait_ge(s_mg, n + 4)
                    dve.tensor_tensor(mg_lo[:, m, :], ga, mg_hi[:, m, :], ALU.subtract).then_inc(s_mg, 1)

                def body(b, last):
                    for m in range(KD):
                        if m < KD - 1:
                            branch_lo(b, m + 1)
                        elif not last:
                            branch_lo(b + 1, 0)
                        merge(b, m)
                    if not last:
                        split_acts(b + 1)
                    for j in range(TB):
                        n = TB * b + j
                        u = j % 2
                        dve.wait_ge(s_sq, n + 1)
                        dve.tensor_scalar(mean[:, u:u + 1], sums[:, u:u + 1], 1.0 / D, EPS, ALU.mult, ALU.add)\
                            .then_inc(s_mean, 1)
                        dve.wait_ge(s_std, n + 1)
                        dve.reciprocal(rstd[:, u:u + 1], std[:, u:u + 1]).then_inc(s_rstd, 1)
                        dve.wait_ge(s_rstd, n + 1)
                        if j >= 2 or not isinstance(b, int) or b:
                            dve.wait_ge(s_st[u], 16 * (TB // 2 * b + j // 2))
                        dve.scalar_tensor_tensor(x1[:, u, :], ps_y[:, u, :], rstd[:, u:u + 1], g1[:], ALU.mult, ALU.mult)\
                            .then_inc(s_n1, 1)
                        dve.wait_ge(s_n1, n + 1)
                        dve.wait_ge(s_x[u], 16 * (TB // 2 * b + j // 2 + 1))
                        dve.tensor_tensor(x1[:, u, :], x1[:, u, :], x[:, u, :], ALU.add).then_inc(s_x1, 1)

                dve.wait_ge(s_sums, 16)
                dve.reciprocal(total[:], total[:]).then_inc(s_rec, 1)
                for k in range(KD):
                    dve.wait_ge(s_whi, k + 1)
                    dve.tensor_tensor(wo_lo[:, k, :], w_st[:, k % 2, :], wo_hi[:, k, :], ALU.subtract).then_inc(s_wlo, 1)
                branch_lo(0, 0)
                split_acts(0)
                dve.wait_ge(s_g1, 16)
                body(0, False)
                with dve.Fori(1, NB - 1) as b:
                    body(b, False)
                body(NB - 1, True)

            @block.tensor
            def _(pe):
                def body(b):
                    pe.wait_ge(s_act, AS * (b + 1))
                    for m in range(KD):
                        u = m % 2
                        pe.wait_ge(s_wlo, KD * (b + 1) + m + 1)
                        if m >= 2 or not isinstance(b, int) or b:
                            pe.wait_ge(s_mg, 5 * (KD * b + m - 1))
                        for branch in range(2):
                            for k in range(KB):
                                kk = branch * KB + k
                                q = product3(pe, ps_b[:, u, branch, :], wb_hi[:, u, kk, :], wb_lo[:, u, kk, :],
                                             act_hi[:, kk, :], act_lo[:, kk, :], k == 0, k == KB - 1)
                        q.then_inc(s_br, 1)
                    for j in range(TB):
                        rows = slice(j * P, (j + 1) * P)
                        if j >= 2 or not isinstance(b, int) or b:
                            pe.wait_ge(s_n1, TB * b + j - 1)
                        for n in range(2):
                            cols = slice(n * BLK, (n + 1) * BLK)
                            for k in range(KD):
                                if j == 0 and n == 0:
                                    pe.wait_ge(s_mg, 5 * (KD * b + k + 1))
                                q = product3(pe, ps_y[:, j % 2, cols], mg_hi[:, k, rows], mg_lo[:, k, rows],
                                             wo_hi[:, k, cols], wo_lo[:, k, cols], k == 0, k == KD - 1)
                        q.then_inc(s_y, 1)

                body(0)
                with pe.Fori(1, NB) as b:
                    body(b)


def ffn_phase(nc, half, h_hi, h_lo, w_up, w_dn, conv, gate_rows, carry, gc_hi, gc_lo, x1_d, out_d):
    NCV = HALF + 1
    G0 = P - 1
    tiles = NT // 2 - 1 if half == 0 else NT // 2 + 1
    t0 = 0 if half == 0 else NT // 2 - 1
    off = P if half == 0 else 0
    with Res(nc, f"ffn{half}") as r:
        w_st = r.sb("w_st", [P, 2, D])
        wu_hi, wu_lo = (r.sb(n, [P, 2, KD, P], F32R) for n in ("wu_hi", "wu_lo"))
        wd_st = r.sb("wd_st", [P, D])
        wd_hi, wd_lo = (r.sb(n, [P, 2, D], F32R) for n in ("wd_hi", "wd_lo"))
        u = r.sb("u", [P, 2, HALF + 3])
        cv = r.sb("cv", [P, 2, NCV])
        g_hi, g_lo = (r.sb(n, [P, 2, HALF + P], F32R) for n in ("g_hi", "g_lo"))
        y = r.sb("y", [P, tiles, D])
        cw = r.sb("cw", [P, 2 * NP, 4])
        sums, mean, std, rstd = (r.sb(n, [P, tiles]) for n in ("sums", "mean", "std", "rstd"))
        ps_u = r.ps("ps_u", [P, 2, 2, BLK])
        ps_d = r.ps("ps_d", [P, 2, D])
        s_w = [r.sem(f"wu_loaded{i}") for i in range(2)]
        s_x = [r.sem(f"x_loaded{i}") for i in range(2)]
        s_st = [r.pool_dma_sem(f"out_stored{i}") for i in range(2)]
        s_cw, s_wd, s_init, s_g2 = (r.sem(n) for n in ("conv_loaded", "wd_loaded", "init", "g2_loaded"))
        s_whi, s_wlo, s_dhi, s_dlo = (r.sem(n) for n in ("wu_hi_made", "wu_lo_made", "wd_hi_made", "wd_lo_made"))
        s_up, s_u, s_cs, s_cd, s_ge, s_g, s_ghi, s_glo, s_gc = (
            r.sem(n) for n in ("up", "u_copied", "conv_steps", "conv", "gelu", "g", "g_hi_made", "g_lo_made", "g_carry"))
        s_dn, s_y, s_sq, s_mean, s_std, s_rstd, s_n, s_o = (
            r.sem(n) for n in ("down", "y_added", "squares", "mean", "root", "rstd", "scaled", "out"))
        CS = 8
        with r.block() as block:

            @block.sync
            def _(sp):
                def load_up(p, j, first=False):
                    if not first:
                        sp.wait_ge(s_wlo, 2 * p + j - 1)
                    sp.dma_start(w_st[:, j:j + 1, :], w_up[bass.ds(2 * p + j, 1), :, :].rearrange("o p d -> p o d"))\
                        .then_inc(s_w[j], 16)

                def load_dn(p, first=False):
                    if not first:
                        sp.wait_ge(s_dlo, p)
                    sp.dma_start(wd_st[:], w_dn[bass.ds(p, 1), :, :].rearrange("o p d -> (o p) d")).then_inc(s_wd, 16)

                load_up(0, 0, True)
                load_up(0, 1, True)
                sp.dma_start(cw[:], conv).then_inc(s_cw, 16)
                load_dn(0, True)
                with sp.Fori(0, NP - 1) as p:
                    load_up(p + 1, 0)
                    load_up(p + 1, 1)
                    load_dn(p + 1)
                sp.wait_ge(s_dlo, NP)
                sp.dma_start(wd_st[:], gate_rows).then_inc(s_g2, 16)
                sp.wait_ge(s_glo, NP)
                for t in range(tiles):
                    if t >= 2:
                        sp.wait_ge(s_o, t - 1)
                    sp.dma_start(cv[:, t % 2, 0:D], x1_d[t0 + t]).then_inc(s_x[t % 2], 16)

            @block.gpsimd
            def _(pool):
                pool.memset(y[:], 0.0).then_inc(s_init, 1)
                pool.memset(u[:, :, 0:2], 0.0).then_inc(s_init, 1)
                pool.memset(u[:, :, HALF + 2:HALF + 3], 0.0).then_inc(s_init, 1)

                def kept_columns(p, v):
                    if half == 0:
                        pool.wait_ge(s_glo, p + 1)
                    elif not isinstance(p, int):
                        pool.wait_ge(s_dn, tiles * (p - 1))
                    for kept, whole in ((gc_hi, g_hi), (gc_lo, g_lo)):
                        kept = kept[:, bass.ds(p, 1), :].rearrange("p o c -> p (o c)")
                        if half == 0:
                            m = pool.tensor_copy(kept, whole[:, v, HALF:HALF + G0])
                        else:
                            m = pool.tensor_copy(whole[:, v, 0:G0], kept)
                    m.then_inc(s_gc, 1)

                kept_columns(0, 0)
                kept_columns(1, 1)
                with pool.Fori(1, NP // 2) as i:
                    for v in range(2):
                        kept_columns(2 * i + v, v)
                for t in range(tiles):
                    pool.wait_ge(s_o, t + 1)
                    pool.dma_start(out_d[t0 + t], y[:, t, :]).then_inc(s_st[t % 2], 16)
                pool.wait_ge(s_st[0], 16 * ((tiles + 1) // 2))
                pool.wait_ge(s_st[1], 16 * (tiles // 2))

            @block.scalar
            def _(act):
                def up_hi(p, j):
                    act.wait_ge(s_w[j], 16 * p + 16)
                    if not isinstance(p, int) or p:
                        act.wait_ge(s_up, 4 * (p - 1) + 2 * j + 2)
                    act.activation(wu_hi[:, j, :, :].rearrange("p k m -> p (k m)"), w_st[:, j, :], ACT.Copy)\
                        .then_inc(s_whi, 1)

                def body(p, v, last, first):
                    for j in range(2):
                        for n in range(2):
                            act.wait_ge(s_up, 4 * p + 2 * j + n + 1)
                            if not first:
                                act.wait_ge(s_cd, 2 * (p - 1) + j + 1)
                            act.activation(u[:, j, 2 + n * BLK:2 + (n + 1) * BLK], ps_u[:, j, n, :], ACT.Copy)\
                                .then_inc(s_u, 1)
                        if not last:
                            up_hi(p + 1, j)
                    act.wait_ge(s_wd, 16 * p + 16)
                    if not (isinstance(p, int) and p < 2):
                        act.wait_ge(s_dn, tiles * (p - 1))
                    act.activation(wd_hi[:, v, :], wd_st[:], ACT.Copy).then_inc(s_dhi, 1)
                    act.wait_ge(s_cd, 2 * p + 1)
                    act.activation(cv[:, 0, :], cv[:, 0, :], ACT.Gelu_apprx_tanh).then_inc(s_ge, 1)
                    act.wait_ge(s_g, p + 1)
                    if half == 0 and not (isinstance(p, int) and p < 2):
                        act.wait_ge(s_gc, p - 1)
                    act.activation(g_hi[:, v, G0:G0 + NCV], cv[:, 0, :], ACT.Copy).then_inc(s_ghi, 1)

                up_hi(0, 0)
                up_hi(0, 1)
                body(0, 0, False, True)
                body(1, 1, False, False)
                with act.Fori(1, NP // 2 - 1) as i:
                    for v in range(2):
                        body(2 * i + v, v, False, False)
                body(NP - 2, 0, False, False)
                body(NP - 1, 1, True, False)
                for t in range(tiles):
                    act.wait_ge(s_y, tiles * (NP - 1) + t + 1)
                    if t:
                        act.wait_ge(s_sq, t)
                    act.activation(u[:, 0, 0:D], y[:, t, :], ACT.Square, accum_out=sums[:, t:t + 1]).then_inc(s_sq, 1)
                act.wait_ge(s_mean, 1)
                act.activation(std[:], mean[:], ACT.Sqrt).then_inc(s_std, 1)

            @block.vector
            def _(dve):
                def up_lo(p, j):
                    dve.wait_ge(s_whi, 2 * p + j + 1)
                    dve.tensor_tensor(wu_lo[:, j, :, :].rearrange("p k m -> p (k m)"), w_st[:, j, :],
                                      wu_hi[:, j, :, :].rearrange("p k m -> p (k m)"), ALU.subtract).then_inc(s_wlo, 1)

                def convolve(p, j, first):
                    n = CS * p + 4 * j
                    one = lambda i: cw[:, bass.ds(2 * p + j, 1), i:i + 1].rearrange("p o i -> p (o i)")
                    keep = carry[:, bass.ds(2 * p + j, 1), :].rearrange("p o i -> p (o i)")
                    dve.wait_ge(s_u, 4 * p + 2 * j + 2)
                    if half == 0:
                        dve.tensor_copy(keep, u[:, j, HALF:HALF + 2]).then_inc(s_cs, 1)
                    else:
                        dve.tensor_copy(u[:, j, 0:2], keep).then_inc(s_cs, 1)
                        dve.wait_ge(s_cs, n + 1)
                    if not first:
                        dve.wait_ge(s_ghi, p)
                        dve.wait_ge(s_glo, p)
                    dve.tensor_scalar(cv[:, j, :], u[:, j, 0:NCV], one(0), one(3), ALU.mult, ALU.add).then_inc(s_cs, 1)
                    dve.wait_ge(s_cs, n + 2)
                    dve.scalar_tensor_tensor(cv[:, j, :], u[:, j, 1:NCV + 1], one(1), cv[:, j, :], ALU.mult, ALU.add)\
                        .then_inc(s_cs, 1)
                    dve.wait_ge(s_cs, n + 3)
                    dve.scalar_tensor_tensor(cv[:, j, :], u[:, j, 2:NCV + 2], one(2), cv[:, j, :], ALU.mult, ALU.add)\
                        .then_inc(s_cd, 1)
                    dve.sem_inc(s_cs, 1)

                def add_down(p):
                    for t in range(tiles):
                        dve.wait_ge(s_dn, tiles * p + t + 1)
                        dve.tensor_tensor(y[:, t, :], y[:, t, :], ps_d[:, t % 2, :], ALU.add).then_inc(s_y, 1)

                def body(p, v, last, first):
                    convolve(p, 0, first)
                    if not last:
                        up_lo(p + 1, 0)
                    if not first:
                        add_down(p - 1)
                    if not last:
                        up_lo(p + 1, 1)
                    convolve(p, 1, first)
                    dve.wait_ge(s_ge, p + 1)
                    dve.wait_ge(s_cd, 2 * p + 2)
                    dve.tensor_tensor(cv[:, 0, :], cv[:, 0, :], cv[:, 1, :], ALU.mult).then_inc(s_g, 1)
                    dve.wait_ge(s_dhi, p + 1)
                    dve.tensor_tensor(wd_lo[:, v, :], wd_st[:], wd_hi[:, v, :], ALU.subtract).then_inc(s_dlo, 1)
                    dve.wait_ge(s_ghi, p + 1)
                    if half == 0 and not (isinstance(p, int) and p < 2):
                        dve.wait_ge(s_gc, p - 1)
                    dve.tensor_tensor(g_lo[:, v, G0:G0 + NCV], cv[:, 0, :], g_hi[:, v, G0:G0 + NCV], ALU.subtract)\
                        .then_inc(s_glo, 1)

                dve.wait_ge(s_cw, 16)
                dve.wait_ge(s_init, 3)
                up_lo(0, 0)
                up_lo(0, 1)
                body(0, 0, False, True)
                body(1, 1, False, False)
                with dve.Fori(1, NP // 2 - 1) as i:
                    for v in range(2):
                        body(2 * i + v, v, False, False)
                body(NP - 2, 0, False, False)
                body(NP - 1, 1, True, False)
                add_down(NP - 1)
                dve.wait_ge(s_sq, tiles)
                dve.tensor_scalar(mean[:], sums[:], 1.0 / D, EPS, ALU.mult, ALU.add).then_inc(s_mean, 1)
                dve.wait_ge(s_std, 1)
                dve.reciprocal(rstd[:], std[:]).then_inc(s_rstd, 1)
                dve.wait_ge(s_rstd, 1)
                dve.wait_ge(s_g2, 16)
                for t in range(tiles):
                    dve.scalar_tensor_tensor(y[:, t, :], y[:, t, :], rstd[:, t:t + 1], wd_st[:], ALU.mult, ALU.mult)\
                        .then_inc(s_n, 1)
                    dve.wait_ge(s_n, t + 1)
                    dve.wait_ge(s_x[t % 2], 16 * (t // 2 + 1))
                    dve.tensor_tensor(y[:, t, :], y[:, t, :], cv[:, t % 2, 0:D], ALU.add).then_inc(s_o, 1)

            @block.tensor
            def _(pe):
                def up(p, first=False):
                    for j in range(2):
                        pe.wait_ge(s_wlo, 2 * p + j + 1)
                        for n in range(2):
                            if not first:
                                pe.wait_ge(s_u, 4 * (p - 1) + 2 * j + n + 1)
                            cols = slice(n * BLK, (n + 1) * BLK)
                            for k in range(KD):
                                m = product3(pe, ps_u[:, j, n, :], wu_hi[:, j, k, :], wu_lo[:, j, k, :],
                                             h_hi[:, k, cols], h_lo[:, k, cols], k == 0, k == KD - 1)
                            m.then_inc(s_up, 1)

                def down(p, v):
                    pe.wait_ge(s_dlo, p + 1)
                    pe.wait_ge(s_glo, p + 1)
                    if half == 1:
                        pe.wait_ge(s_gc, p + 1)
                    for t in range(tiles):
                        if t >= 2 or not isinstance(p, int) or p:
                            pe.wait_ge(s_y, tiles * p + t - 1)
                        g = slice(off + t * P, off + (t + 1) * P)
                        for n in range(2):
                            cols = slice(n * BLK, (n + 1) * BLK)
                            m = product3(pe, ps_d[:, t % 2, cols], g_hi[:, v, g], g_lo[:, v, g],
                                         wd_hi[:, v, cols], wd_lo[:, v, cols], True, True)
                        m.then_inc(s_dn, 1)

                up(0, True)
                up(1)
                down(0, 0)
                with pe.Fori(0, NP // 2 - 1) as i:
                    up(2 * i + 2)
                    down(2 * i + 1, 1)
                    up(2 * i + 3)
                    down(2 * i + 2, 0)
                down(NP - 1, 1)


def program(nc, x, c, w_ada, b_ada, pre_g, post_g, w_f, w_z, b_gate, qk_g, w_branch, w_out, w_up, conv, w_dn,
            t_pos, t_chan, rope_cos, rope_sin, swap, head_mean, ident_d, out, scratch_kind="Internal"):
    def scratch(name, shape, dt=F32):
        return nc.dram_tensor(f"scratch_{name}", shape, dt, kind=scratch_kind).ap()

    gate_rows = scratch("gate_rows", [P, 2, D])
    f_d = scratch("f", [NT, P, FW])
    qkv_d = scratch("qkv", [NQC + 2, P, S])
    gates_d = scratch("gates", [NB, 2 * KD, P, BLK])
    yT_d = scratch("yT", [NG, P, S])
    z_d = scratch("z", [2, NG, P, N1 * P])
    kv_d = scratch("kv", [NKV, P, 2, S])
    o_d = scratch("o", [2, NH, HD, S])
    sums_d = scratch("sums", [NH, S])
    rec_d = scratch("rec", [NH, S])
    x1_d = scratch("x1", [NT, P, D])

    with Res(nc, "keep") as keep:
        ident = keep.sb("ident", [P, P])
        ones = keep.sb("ones", [P, P])
        mod = keep.sb("mod", [P, 4, KD])
        first_sem = load_constants(nc, ident_d, ident, ones)
        ada_phase(nc, c, w_ada, b_ada, pre_g, post_g, ident, ones, mod, gate_rows)
        with Res(nc, "h1") as h1:
            h_hi, h_lo = (h1.sb(n, [P, KD, S], F32R) for n in ("hi", "lo"))
            norm_phase(nc, "norm1", x, NB, ident, mod[:, 0, :], mod[:, 1, :], h_hi, h_lo)
            f_phase(nc, w_f, h_hi, h_lo, f_d)
            kept = proj_phase(nc, w_z, h_hi, h_lo, b_gate, qk_g, rope_cos, rope_sin, swap, head_mean, ident, f_d,
                              qkv_d, gates_d, z_d, kv_d)
        with Res(nc, "head0") as shared:
            head0 = Head0(shared)
            fourier_phase(nc, head0, z_d, t_pos, t_chan, qkv_d, kv_d, ident, yT_d)
            attention_phase(nc, head0, qkv_d, kv_d, ident, ones, o_d, sums_d)
        merge_phase(nc, x, w_branch, w_out, o_d, sums_d, rec_d, yT_d, gates_d, gate_rows[:, 0, :], x1_d, first_sem, kept)
        with Res(nc, "h2") as h2:
            h_hi, h_lo = (h2.sb(n, [P, KD, HALF], F32R) for n in ("hi", "lo"))
            carry = h2.sb("carry", [P, 2 * NP, 2])
            gc_hi, gc_lo = (h2.sb(n, [P, NP, P - 1], F32R) for n in ("gc_hi", "gc_lo"))
            for half in range(2):
                norm_phase(nc, f"norm2{half}", x1_d[half * NT // 2:(half + 1) * NT // 2], NB // 2, ident,
                           mod[:, 2, :], mod[:, 3, :], h_hi, h_lo)
                ffn_phase(nc, half, h_hi, h_lo, w_up, w_dn, conv, gate_rows[:, 1, :], carry, gc_hi, gc_lo, x1_d, out)


def tables():
    n2, k2 = np.arange(P)[:, None], np.arange(P)[None, :]
    pos = np.empty((K1, P, 3, P))
    for k1 in range(K1):
        a = 2 * np.pi * ((n2 * (k1 + N1 * k2)) % S) / S
        pos[k1, :, 0], pos[k1, :, 1], pos[k1, :, 2] = np.sin(a), np.cos(a), -np.sin(a)
    a = 2 * np.pi * ((n2 * k2) % P) / P
    chan = np.stack([np.cos(a), np.sin(a), -np.sin(a)], 1) / math.sqrt(S * P)
    grid_w, pairs = 64, HD // 4
    inv = 10000.0 ** (-np.arange(pairs) / pairs)
    t = np.arange(S)
    ang = np.concatenate([(t // grid_w)[None, :] * inv[:, None], (t % grid_w)[None, :] * inv[:, None]])
    ang = np.tile(np.repeat(ang, 2, axis=0), (2, 1))
    sign = np.where(np.arange(P) % 2 == 0, -1.0, 1.0)[:, None]
    swap = np.zeros((P, P))
    swap[np.arange(P) ^ 1, np.arange(P)] = 1.0
    head_mean = np.kron(np.eye(2), np.full((HD, HD), 1.0 / HD))
    made = {"t_pos": pos.transpose(1, 0, 2, 3).reshape(P, K1, 3 * P), "t_chan": chan.reshape(P, 3 * P), "rope_cos": np.cos(ang),
            "rope_sin": sign * np.sin(ang), "swap": swap, "head_mean": head_mean, "ident_d": np.eye(P)}
    return {k: np.ascontiguousarray(v.astype(np.float32)) for k, v in made.items()}


def layouts(a):
    w_in = a["w_in"][0].reshape(KD, P, -1)
    o1 = NH * HD
    o3 = o1 + 2 * NKV * HD
    o4 = o3 + FW

    def chunks(w):
        n = w.shape[2] // P
        return w.reshape(w.shape[0], P, n, P).transpose(2, 1, 0, 3).reshape(n, P, -1)

    def pairs(first, second):
        return np.stack([first, second], 1).reshape(-1, *first.shape[1:])

    by_channel = lambda v: v.reshape(-1, P).T
    ga, gf = chunks(w_in[:, :, o4:o4 + D]), chunks(w_in[:, :, o4 + D:])
    bga, bgf = by_channel(a["b_gate"][0, :D]), by_channel(a["b_gate"][0, D:])
    wa = chunks(a["w_attn_branch"][0].reshape(NQC, P, D))
    wf = chunks(a["w_fourier_branch"][0].reshape(NG, P, D))
    wu = a["w_up"][0].reshape(KD, P, -1)
    cw = np.concatenate([a["conv_w"][0], a["conv_b"][0][None]])
    cw = cw.reshape(4, 2, NP, P).transpose(3, 2, 1, 0).reshape(P, 2 * NP, 4)
    q_g, k_g = np.tile(a["q_norm_g"][0], 2), np.tile(a["k_norm_g"][0], 2)
    laid = {
        "x": a["x"].reshape(NT, P, D),
        "c": by_channel(a["c"][0]),
        "w_ada": a["w_ada"][0].reshape(KD, P, 6 * D),
        "b_ada": a["b_ada"],
        "pre_g": np.stack([by_channel(a["mix_pre_g"][0]), by_channel(a["ffn_pre_g"][0])], 1),
        "post_g": np.stack([a["mix_post_g"][0], a["ffn_post_g"][0]]),
        "w_f": w_in[:, :, o3:o4],
        "w_z": np.concatenate([chunks(w_in[:, :, :o3]), pairs(ga, gf)]),
        "b_gate": np.stack([bga, bgf], 2).reshape(P, 2 * KD),
        "qk_g": np.stack([q_g] * NQC + [k_g], 1),
        "w_branch": np.concatenate([wa, wf], 2),
        "w_out": a["w_out"][0].reshape(KD, P, D),
        "w_up": pairs(chunks(wu[:, :, :DFF]), chunks(wu[:, :, DFF:])),
        "conv": cw,
        "w_dn": a["w_down"][0].reshape(NP, P, D),
    }
    return {k: np.ascontiguousarray(v) for k, v in laid.items()}


def kernel(**inputs):
    import concourse.bacc as bacc
    from concourse.bass_utils import run_bass_kernel_spmd

    arrays = {**layouts({k: np.asarray(v) for k, v in inputs.items()}), **tables()}
    nc = bacc.Bacc("TRN2", target_bir_lowering=False, num_devices=1)
    args = {n: nc.dram_tensor(f"in_{n}", a.shape, mybir.dt.from_np(a.dtype), kind="ExternalInput").ap()
            for n, a in arrays.items()}
    out = nc.dram_tensor("out", [NT, P, D], F32, kind="ExternalOutput").ap()
    program(nc, out=out, **args)
    got = run_bass_kernel_spmd(nc, [{f"in_{n}": a for n, a in arrays.items()}], core_ids=[0])
    return got.results[0]["out"].reshape(1, S, D)
```

```python
import math
from contextlib import ExitStack

import numpy as np

import concourse.bass as bass
from concourse import mybir

F32 = mybir.dt.float32
F32R = mybir.dt.float32r
ALU = mybir.AluOpType
ACT = mybir.ActivationFunctionType
AX = mybir.AxisListType

P = 128
D = 1024
S = 2048
KD = D // P
NT = S // P
BLK = 512
NB = S // BLK
HD = 64
NH = 8
NQC = NH * HD // P
NKV = 2
NG = 4
FW = NG * P
DFF = 2816
NP = DFF // P
HALF = S // 2
EPS = 1e-6
NM = NB * NT
N1 = 16
K1 = N1 // 2 + 1


class Res:

    def __init__(self, nc, tag):
        self.nc, self.tag, self.ctx, self.sem_nums = nc, tag, ExitStack(), []

    def __enter__(self):
        return self

    def __exit__(self, *a):
        return self.ctx.__exit__(*a)

    def sb(self, name, shape, dt=F32):
        return self.ctx.enter_context(self.nc.sbuf_tensor(f"{self.tag}_{name}", shape, dt))

    def ps(self, name, shape, dt=F32):
        return self.ctx.enter_context(self.nc.psum_tensor(f"{self.tag}_{name}", shape, dt))

    def sem(self, name):
        handle = self.ctx.enter_context(self.nc.semaphore(f"{self.tag}_{name}"))
        self.sem_nums.append(handle.num)
        return handle

    def pool_dma_sem(self, name):
        return self.nc.alloc_semaphore(name=f"{self.tag}_{name}")

    def block(self):
        return self.nc.Block()


def product3(pe, out, w_hi, w_lo, x_hi, x_lo, first, last):
    pe.matmul(out, w_hi, x_hi, start=first, stop=False)
    pe.matmul(out, w_hi, x_lo, start=False, stop=False)
    return pe.matmul(out, w_lo, x_hi, start=False, stop=last)


def load_constants(nc, ident_d, ident, ones):
    with Res(nc, "const") as r:
        loaded = r.sem("loaded")
        with r.block() as block:

            @block.sync
            def _(sp):
                sp.dma_start(ident[:], ident_d).then_inc(loaded, 16)
                sp.wait_ge(loaded, 16)

            @block.vector
            def _(dve):
                dve.memset(ones[:], 1.0)
        return loaded.num


class Ada:
    KINDS = ("shift", "scale", "gate")

    def __init__(self, r, slots, parts, c_act, w_ada, b_cols, b_ada, pre_g, post_g, ones, mod, gate_rows):
        self.slots = slots
        self.parts, self.c_act, self.w_ada, self.b_cols, self.b_ada = parts, c_act, w_ada, b_cols, b_ada
        self.pre_g, self.post_g, self.ones, self.mod, self.gate_rows = pre_g, post_g, ones, mod, gate_rows
        self.w = r.sb("ada_w", [P, self.slots, D])
        self.acc = r.sb("ada_acc", [P, 2, D])
        self.bias = r.sb("ada_bias", [P, 6 * KD])
        self.gains = r.sb("ada_gains", [P, 2, KD])
        self.col = r.sb("ada_col", [P, KD])
        self.gates = [p for p in parts if p % 3 == 2]
        if self.gates:
            self.brow, self.row = r.sb("ada_brow", [P, D]), r.sb("ada_row", [P, D])
            self.ps_row = r.ps("ada_ps_row", [P, D])
        self.ps_col = r.ps("ada_ps_col", [P, BLK])
        self.s_small, self.s_row, self.s_out = r.sem("ada_small"), r.sem("ada_rows_loaded"), r.sem("ada_stored")
        self.s_w = [r.sem(f"ada_w{i}") for i in range(self.slots)]
        self.s_acc, self.s_sum, self.s_fin = r.sem("ada_summed"), r.sem("ada_over_partitions"), r.sem("ada_steps")

    def load_small(self, sp):
        sp.dma_start(self.bias[:], self.b_cols).then_inc(self.s_small, 16)
        sp.dma_start(self.gains[:], self.pre_g).then_inc(self.s_small, 16)

    def load(self, sp, i, first=0, last=KD):
        for k in range(first, last):
            n = KD * i + k
            if n >= self.slots:
                sp.wait_ge(self.s_acc, n - self.slots + 1)
            at = self.parts[i] * D
            sp.dma_start(self.w[:, n % self.slots, :], self.w_ada[k][:, at:at + D]).then_inc(self.s_w[n % self.slots], 16)

    def load_row(self, sp, i):
        part = self.parts[i]
        before = self.gates.index(part)
        if before:
            sp.wait_ge(self.s_out, 16 * before)
        sp.dma_start(self.brow[:], self.b_ada[:, part * D:(part + 1) * D].broadcast_to([P, D])).then_inc(self.s_row, 16)
        j = part // 3
        sp.dma_start(self.row[:], self.post_g[j:j + 1, :].broadcast_to([P, D])).then_inc(self.s_row, 16)

    def store_row(self, sp, i):
        sp.wait_ge(self.s_fin, 2 * (i + 1))
        sp.dma_start(self.gate_rows[:, self.parts[i] // 3, :], self.row[:]).then_inc(self.s_out, 16)

    def accumulate(self, dve, i):
        for k in range(KD):
            n = KD * i + k
            w, acc, c = self.w[:, n % self.slots, :], self.acc[:, i % 2, :], self.c_act[:, k:k + 1]
            dve.wait_ge(self.s_w[n % self.slots], 16 * (n // self.slots + 1))
            if k == 0:
                if i >= 2:
                    dve.wait_ge(self.s_sum, i - 1)
                dve.tensor_scalar(acc, w, c, None, ALU.mult).then_inc(self.s_acc, 1)
            else:
                dve.wait_ge(self.s_acc, n)
                dve.scalar_tensor_tensor(acc, w, c, acc, ALU.mult, ALU.add).then_inc(self.s_acc, 1)

    def over_partitions(self, pe, i):
        pe.wait_ge(self.s_acc, KD * (i + 1))
        acc = self.acc[:, i % 2, :]
        if self.parts[i] % 3 == 2:
            if self.gates.index(self.parts[i]):
                pe.wait_ge(self.s_fin, 2 * i)
            for n in range(D // BLK):
                m = pe.matmul(self.ps_row[:, n * BLK:(n + 1) * BLK], self.ones[:], acc[:, n * BLK:(n + 1) * BLK],
                              start=True, stop=True)
        else:
            for k in range(KD):
                m = pe.matmul(self.ps_col[:, KD * i + k:KD * i + k + 1], acc[:, k * P:(k + 1) * P], self.ones[:, 0:1],
                              start=True, stop=True)
        m.then_inc(self.s_sum, 1)

    def finish(self, dve, i):
        part = self.parts[i]
        j, kind = part // 3, self.KINDS[part % 3]
        dve.wait_ge(self.s_sum, i + 1)
        if kind == "gate":
            dve.wait_ge(self.s_row, 32 * (self.gates.index(part) + 1))
            dve.tensor_tensor(self.brow[:], self.ps_row[:], self.brow[:], ALU.add).then_inc(self.s_fin, 1)
            dve.wait_ge(self.s_fin, 2 * i + 1)
            dve.tensor_tensor(self.row[:], self.brow[:], self.row[:], ALU.mult).then_inc(self.s_fin, 1)
            return
        dve.wait_ge(self.s_small, 32)
        dst = self.mod[:, 2 * j + 1, :] if kind == "shift" else self.col[:]
        dve.tensor_tensor(dst, self.ps_col[:, KD * i:KD * (i + 1)], self.bias[:, part * KD:(part + 1) * KD], ALU.add)\
            .then_inc(self.s_fin, 1)
        if kind == "scale":
            dve.wait_ge(self.s_fin, 2 * i + 1)
            dve.scalar_tensor_tensor(self.mod[:, 2 * j, :], self.col[:], 1.0, self.gains[:, j, :], ALU.add, ALU.mult)\
                .then_inc(self.s_fin, 1)
        else:
            dve.sem_inc(self.s_fin, 1)


def norm_phase(nc, tag, x_d, nblocks, ident, scale, shift, hT_hi, hT_lo, make_ada=None, c_d=None, c_act=None,
               wu=None):
    TB = BLK // P
    RING = 4
    ON_DVE = (1, 4, 7)
    with Res(nc, tag) as r:
        x = [r.sb(f"x{i}", [P, TB, D]) for i in range(2)]
        junk = r.sb("junk", [P, D], mybir.dt.bfloat16)
        sums, mean, std, rstd = ([r.sb(f"{n}{i}", [P, TB]) for i in range(2)] for n in ("sums", "mean", "std", "rstd"))
        full = r.sb("full", [P, RING, BLK])
        ps = r.ps("ps", [P, RING, BLK])
        s_x = [[r.sem(f"x{i}_{j}") for j in range(TB)] for i in range(2)]
        names = ("squares", "mean", "root", "rstd", "scaled", "turned", "full", "hi", "lo_dve", "lo_pool")
        s_sq, s_mean, s_std, s_rstd, s_xn, s_tr, s_full, s_hi, s_lo_dve, s_lo_pool = (r.sem(n) for n in names)
        if make_ada:
            s_c, s_silu = r.sem("c_loaded"), r.sem("silu")
            c_raw = r.sb("c_raw", [P, KD])
            ada = make_ada(r)

        def low_done(n):
            b, k = divmod(n, KD)
            on_dve = k in ON_DVE
            each = len(ON_DVE) if on_dve else KD - len(ON_DVE)
            return s_lo_dve if on_dve else s_lo_pool, b * each + sum((j in ON_DVE) == on_dve for j in range(k + 1))

        def low_part(engine, n, done):
            b, k = divmod(n, KD)
            cols = slice(b * BLK, (b + 1) * BLK)
            engine.wait_ge(s_hi, n + 1)
            engine.tensor_tensor(hT_lo[:, k, cols], full[:, n % RING, :], hT_hi[:, k, cols], ALU.subtract).then_inc(done, 1)

        with r.block() as block:

            @block.sync
            def _(sp):
                def load_x(b):
                    if b >= 2:
                        sp.wait_ge(s_tr, (b - 1) * KD)
                    for j in range(TB):
                        sp.dma_start(x[b % 2][:, j, :], x_d[b * TB + j]).then_inc(s_x[b % 2][j], 16)

                if make_ada:
                    sp.dma_start(c_raw[:], c_d).then_inc(s_c, 16)
                    ada.load(sp, 0, 0, 4)
                    load_x(0)
                    ada.load(sp, 0, 4)
                    ada.load_small(sp)
                    ada.load(sp, 1)
                else:
                    load_x(0)
                if wu:
                    for j in range(2):
                        wu.load(sp, 0, j)
                for b in range(1, nblocks):
                    load_x(b)

            @block.scalar
            def _(act):
                def root(b):
                    u = b % 2
                    for j in range(TB):
                        act.wait_ge(s_x[u][j], 16 * (b // 2 + 1))
                        if b or j:
                            act.wait_ge(s_sq, b * TB + j)
                        act.activation(junk[:], x[u][:, j, :], ACT.Square, accum_out=sums[u][:, j:j + 1]).then_inc(s_sq, 1)
                    act.wait_ge(s_mean, b + 1)
                    act.activation(std[u][:], mean[u][:], ACT.Sqrt).then_inc(s_std, 1)

                if make_ada:
                    act.wait_ge(s_c, 16)
                    act.activation(c_act[:], c_raw[:], ACT.Silu).then_inc(s_silu, 1)
                root(0)
                for b in range(nblocks):
                    if b + 1 < nblocks:
                        root(b + 1)
                    if make_ada and b == 0:
                        act.wait_ge(ada.s_fin, 4)
                    for n in range(b * KD, (b + 1) * KD):
                        k = n % KD
                        act.wait_ge(s_tr, n + 1)
                        if n >= RING:
                            act.wait_ge(*low_done(n - RING))
                        act.activation(full[:, n % RING, :], ps[:, n % RING, :], ACT.Identity,
                                       bias=shift[:, k:k + 1], scale=scale[:, k:k + 1]).then_inc(s_full, 1)
                    if wu and b == 0:
                        for j in range(2):
                            wu.high_part(act, 0, j)

            @block.vector
            def _(dve):
                def scale_rows(b):
                    u = b % 2
                    dve.wait_ge(s_sq, (b + 1) * TB)
                    dve.tensor_scalar(mean[u][:], sums[u][:], 1.0 / D, EPS, ALU.mult, ALU.add).then_inc(s_mean, 1)
                    dve.wait_ge(s_std, b + 1)
                    dve.reciprocal(rstd[u][:], std[u][:]).then_inc(s_rstd, 1)
                    dve.wait_ge(s_rstd, b + 1)
                    for j in range(TB):
                        dve.tensor_scalar(x[u][:, j, :], x[u][:, j, :], rstd[u][:, j:j + 1], None, ALU.mult).then_inc(s_xn, 1)

                if make_ada:
                    dve.wait_ge(s_silu, 1)
                    ada.accumulate(dve, 0)
                    scale_rows(0)
                    ada.finish(dve, 0)
                    ada.accumulate(dve, 1)
                    ada.finish(dve, 1)
                else:
                    scale_rows(0)
                for b in range(nblocks):
                    if b + 1 < nblocks:
                        scale_rows(b + 1)
                    for n in range(b * KD, (b + 1) * KD):
                        k = n % KD
                        dve.wait_ge(s_full, n + 1)
                        dve.tensor_copy(hT_hi[:, k, b * BLK:(b + 1) * BLK], full[:, n % RING, :]).then_inc(s_hi, 1)
                        if k in ON_DVE:
                            low_part(dve, n, s_lo_dve)
                    if wu and b == 0:
                        for j in range(2):
                            wu.low_part(dve, 0, j)

            @block.gpsimd
            def _(pool):
                for n in range(nblocks * KD):
                    if n % KD not in ON_DVE:
                        low_part(pool, n, s_lo_pool)

            @block.tensor
            def _(pe):
                if make_ada:
                    ada.over_partitions(pe, 0)
                for b in range(nblocks):
                    pe.wait_ge(s_xn, (b + 1) * TB)
                    for k in range(KD):
                        n = b * KD + k
                        if make_ada and n == RING:
                            ada.over_partitions(pe, 1)
                        if n >= RING:
                            pe.wait_ge(s_full, n - RING + 1)
                        for j in range(TB):
                            m = pe.transpose(ps[:, n % RING, j * P:(j + 1) * P], x[b % 2][:, j, k * P:(k + 1) * P], ident[:])
                        m.then_inc(s_tr, 1)


def f_phase(nc, w_f, hT_hi, hT_lo, f_d, make_ada):
    with Res(nc, "fin") as r:
        WS = 4
        w_st = r.sb("w_st", [P, WS, FW])
        w_hi = r.sb("w_hi", [P, KD, FW], F32R)
        w_lo = r.sb("w_lo", [P, KD, FW], F32R)
        out = r.sb("out", [P, 4, FW])
        ps = r.ps("ps", [P, 4, FW])
        s_w = [r.sem(f"w{i}") for i in range(WS)]
        s_hi, s_lo, s_mm, s_ev = (r.sem(n) for n in ("hi", "lo", "mm", "ev"))
        s_out = [r.sem(f"out{i}") for i in range(4)]
        ada = make_ada(r)
        ADA_AT = [3, 6, 9, 13]
        with r.block() as block:

            @block.sync
            def _(sp):
                for k in range(KD):
                    if k >= WS:
                        sp.wait_ge(s_lo, k - WS + 1)
                    sp.dma_start(w_st[:, k % WS, :], w_f[k]).then_inc(s_w[k % WS], 16)
                ada.load_small(sp)
                for i in range(4):
                    ada.load(sp, i)
                    if ada.parts[i] in ada.gates:
                        ada.load_row(sp, i)
                        ada.store_row(sp, i)
                sp.wait_ge(ada.s_out, 32)
                for i in range(4):
                    sp.wait_ge(s_out[i], 16 * NT // 4)

            @block.vector
            def _(dve):
                for k in range(KD):
                    dve.wait_ge(s_w[k % WS], 16 * (k // WS + 1))
                    dve.tensor_copy(w_hi[:, k, :], w_st[:, k % WS, :]).then_inc(s_hi, 1)
                    dve.wait_ge(s_hi, k + 1)
                    dve.tensor_tensor(w_lo[:, k, :], w_st[:, k % WS, :], w_hi[:, k, :], ALU.subtract).then_inc(s_lo, 1)
                for i in range(4):
                    ada.accumulate(dve, i)
                    ada.finish(dve, i)

            @block.scalar
            def _(act):
                for t in range(NT):
                    act.wait_ge(s_mm, t + 1)
                    if t >= 4:
                        act.wait_ge(s_out[t % 4], 16 * (t // 4))
                    act.activation(out[:, t % 4, :], ps[:, t % 4, :], ACT.Copy).then_inc(s_ev, 1)
                    act.wait_ge(s_ev, t + 1)
                    act.dma_start(f_d[t], out[:, t % 4, :]).then_inc(s_out[t % 4], 16)

            @block.tensor
            def _(pe):
                for t in range(NT):
                    if t in ADA_AT:
                        ada.over_partitions(pe, ADA_AT.index(t))
                    if t >= 4:
                        pe.wait_ge(s_ev, t - 3)
                    for k in range(KD):
                        if t == 0:
                            pe.wait_ge(s_lo, k + 1)
                        cols = slice(t * P, (t + 1) * P)
                        m = product3(pe, ps[:, t % 4, :], hT_hi[:, k, cols], hT_lo[:, k, cols],
                                     w_hi[:, k, :], w_lo[:, k, :], k == 0, k == KD - 1)
                    m.then_inc(s_mm, 1)


def proj_phase(nc, w_z, hT_hi, hT_lo, b_gate, qk_g, rope_cos, rope_sin, swap_d, head_mean_d, ident, f_d, qkv_d, gates_d,
               z_d, kv_d):
    NQKV = NQC + 2
    C1, C2, C3 = (math.cos(2 * math.pi * n / N1) for n in (1, 2, 3))
    NV = 44
    KVS = 8
    PER = 2 * KD // NG
    NC = NQKV + 2 * KD
    with Res(nc, "proj") as r:
        w_st = r.sb("w_st", [P, 2, KD, P])
        w_hi = [r.sb(f"w_hi{i}", [P, KD, P], F32R) for i in range(2)]
        w_lo = [r.sb(f"w_lo{i}", [P, KD, P], F32R) for i in range(2)]
        out = r.sb("out", [P, NB, BLK])
        side = r.sb("side", [P, 4, S])
        cos, sin = side[:, 0, :], side[:, 1, :]
        bg = r.sb("bg", [P, 2 * KD])
        gains = r.sb("gains", [P, NQC + 1])
        v_st = r.sb("v_st", [P, BLK])
        swap, head_mean = v_st[:, 0:P], v_st[:, P:2 * P]
        eps = r.sb("eps", [P, 1])
        bcol = r.sb("bcol", [P, 2])
        zg, sq, std, rot = (side[:, a, b * 2 * BLK:(b + 1) * 2 * BLK].rearrange("p (s q) -> p s q", s=2)
                            for a in (2, 3) for b in (0, 1))
        z, eo, z_hi, z_lo = (side[:, a, :].rearrange("p (n c) -> p n c", n=N1) for a in range(4))
        z_hi, z_lo = z_hi.bitcast(F32R), z_lo.bitcast(F32R)
        k_st = r.sb("k_st", [P, NKV, BLK])
        kv = r.sb("kv", [P, NKV, 2, BLK], F32R)
        ps = r.ps("ps", [P, NB, BLK])
        ps_ms = r.ps("ps_ms", [P, 2, BLK])
        ps_sw = r.ps("ps_sw", [P, 2, BLK])
        s_c, s_eps, s_bcol = r.sem("consts"), r.sem("eps_written"), r.sem("bias_at_hand")
        s_w = [r.sem(f"w_loaded{i}") for i in range(2)]
        s_hi, s_lo, s_mm, s_zg, s_ms, s_std, s_rot, s_out, s_rope = (
            r.sem(n) for n in ("w_hi_made", "w_lo_made", "products", "zg_sq", "mean_swap", "root", "rotated", "v_or_gate", "rope"))
        s_f, s_dft, s_z, s_zst = (r.sem(n) for n in ("f_loaded", "dft_steps", "z_split", "z_stored"))
        s_k, s_v, s_tr, s_kv, s_kvst = (r.sem(n) for n in ("k_loaded", "v_loaded", "v_turned", "kv_steps", "kv_stored"))
        s_st = [r.pool_dma_sem(f"stored{n}") for n in range(NB)]
        with r.block() as block:

            @block.sync
            def _(sp):
                def load(c, u):
                    sp.dma_start(w_st[:, u:u + 1, :, :],
                                 w_z[bass.ds(c, 1), :, :].rearrange("o p (k m) -> p o k m", k=KD)).then_inc(s_w[u], 16)

                load(0, 0)
                for dst, src in ((cos, rope_cos), (sin, rope_sin), (bg[:], b_gate), (gains[:], qk_g), (swap, swap_d),
                                 (head_mean, head_mean_d)):
                    sp.dma_start(dst, src).then_inc(s_c, 16)
                load(1, 1)
                with sp.Fori(0, NQKV // 2) as i:
                    for u in range(2):
                        sp.wait_ge(s_lo, 2 * i + u + 1)
                        load(2 * i + u + 2, u)

                def load_f(g):
                    src = f_d.rearrange("t p c -> p t c")[:, :, bass.ds(g * P, P)]
                    sp.dma_start(z, src).then_inc(s_f, 16)

                def load_kv(g):
                    cols = bass.ds(g * BLK, BLK)
                    sp.dma_start(v_st[:], qkv_d[NQC + 1][:, cols]).then_inc(s_v, 16)
                    for a in range(NKV):
                        for half in range(2):
                            sp.dma_start(k_st[half * HD:(half + 1) * HD, a, :],
                                         qkv_d[NQC, a * HD:(a + 1) * HD][:, cols]).then_inc(s_k, 16)

                def store_kv(g):
                    sp.wait_ge(s_kv, KVS * (g + 1))
                    for a in range(NKV):
                        sp.dma_start(kv_d[a][:, :, bass.ds(g * BLK, BLK)], kv[:, a].bitcast(F32)).then_inc(s_kvst, 16)

                sp.wait_ge(s_rot, NB * (NQC + 1))
                load_f(0)
                for n in range(NB):
                    sp.wait_ge(s_st[n], 16 * NQKV)
                load_kv(0)

                def body(g, first, last):
                    for j in range(PER):
                        if not (last and j >= PER - 2):
                            sp.wait_ge(s_lo, PER * g + NQKV + j + 1)
                            load(PER * g + NQKV + j + 2, j % 2)
                        if j == 0 and not first:
                            store_kv(g - 1)
                            load_kv(g)
                        if j == 2:
                            sp.wait_ge(s_z, 2 * (g + 1))
                            for part, src in enumerate((z_hi, z_lo)):
                                at = z_d[part, bass.ds(g, 1)].rearrange("o p c -> (o p) c")
                                sp.dma_start(at, side[:, 2 + part, :]).then_inc(s_zst, 16)
                            if not last:
                                load_f(g + 1)

                body(0, True, False)
                with sp.Fori(1, NG - 1) as g:
                    body(g, False, False)
                body(NG - 1, False, True)
                store_kv(NG - 1)
                sp.wait_ge(s_zst, 32 * NG)
                sp.wait_ge(s_kvst, 16 * NKV * NG)

            @block.gpsimd
            def _(pool):
                with pool.Fori(0, NQC + 1) as c:
                    for n in range(NB):
                        pool.wait_ge(s_rot, 4 * c + n + 1)
                        pool.dma_start(qkv_d[bass.ds(c, 1), :, n * BLK:(n + 1) * BLK], out[:, n, :]).then_inc(s_st[n], 16)
                for n in range(NB):
                    pool.wait_ge(s_out, n + 1)
                    pool.dma_start(qkv_d[NQC + 1, :, n * BLK:(n + 1) * BLK], out[:, n, :]).then_inc(s_st[n], 16)
                with pool.Fori(0, 2 * KD) as g:
                    for n in range(NB):
                        pool.wait_ge(s_out, 4 * g + 4 + n + 1)
                        pool.dma_start(gates_d[n, bass.ds(g, 1), :, :], out[:, n, :]).then_inc(s_st[n], 16)
                for n in range(NB):
                    pool.wait_ge(s_st[n], 16 * NC)

            @block.scalar
            def _(act):
                def hi_part(c, i, u):
                    act.wait_ge(s_w[u], 16 * i + 16)
                    act.activation(w_hi[u][:], w_st[:, u, :, :], ACT.Copy).then_inc(s_hi, 1)

                def root(c, n):
                    act.wait_ge(s_ms, 4 * c + n + 1)
                    if c or n >= 2:
                        act.wait_ge(s_rot, 4 * c + n - 1)
                    act.activation(std[:, n % 2, :], ps_ms[:, n % 2, :], ACT.Sqrt, bias=eps[:, 0:1]).then_inc(s_std, 1)

                hi_part(0, 0, 0)
                act.wait_ge(s_c, 16 * 6)
                act.wait_ge(s_eps, 1)
                for c in range(NQC + 1):
                    if c:
                        act.wait_ge(s_mm, 4 * c)
                    hi_part(c + 1, (c + 1) // 2, (c + 1) % 2)
                    for n in range(NB):
                        act.wait_ge(s_mm, 4 * c + n + 1)
                        if c or n >= 2:
                            act.wait_ge(s_rot, 4 * c + n - 1)
                        act.activation(zg[:, n % 2, :], ps[:, n, :], ACT.Copy, scale=gains[:, c:c + 1])
                        act.activation(sq[:, n % 2, :], ps[:, n, :], ACT.Square).then_inc(s_zg, 1)
                        if n:
                            root(c, n - 1)
                    root(c, NB - 1)

                def next_hi(c, i, u):
                    act.wait_ge(s_mm, 4 * c)
                    hi_part(c + 1, i + u, 1 - u)

                def chunk_out(c, func, **bias):
                    for n in range(NB):
                        act.wait_ge(s_mm, 4 * c + n + 1)
                        act.wait_ge(s_st[n], 16 * c)
                        act.activation(out[:, n, :], ps[:, n, :], func, **bias).then_inc(s_out, 1)

                next_hi(NQC + 1, (NQC + 1) // 2, 1)
                chunk_out(NQC + 1, ACT.Copy)
                with act.Fori(0, KD - 1) as i:
                    for u in range(2):
                        next_hi(2 * i + NQKV + u, i + NQKV // 2, u)
                        act.activation(bcol[:, u:u + 1], bg[:, bass.ds(2 * i + u, 1)], ACT.Copy).then_inc(s_bcol, 1)
                        act.wait_ge(s_bcol, 2 * i + u + 1)
                        chunk_out(2 * i + NQKV + u, ACT.Sigmoid, bias=bcol[:, u:u + 1])
                next_hi(NC - 2, (NC - 2) // 2, 0)
                chunk_out(NC - 2, ACT.Sigmoid, bias=bg[:, 2 * KD - 2:2 * KD - 1])
                chunk_out(NC - 1, ACT.Sigmoid, bias=bg[:, 2 * KD - 1:2 * KD])

            @block.vector
            def _(dve):
                def lo_part(c, u):
                    dve.wait_ge(s_hi, c + 1)
                    dve.tensor_tensor(w_lo[u][:], w_st[:, u, :, :], w_hi[u][:], ALU.subtract).then_inc(s_lo, 1)

                dve.memset(eps[:], EPS).then_inc(s_eps, 1)
                lo_part(0, 0)
                dve.wait_ge(s_c, 16 * 6)
                for c in range(NQC + 1):
                    lo_part(c + 1, (c + 1) % 2)
                    for n in range(NB):
                        cols = slice(n * BLK, (n + 1) * BLK)
                        done = 4 * (4 * c + n)
                        zc, rc, sc = zg[:, n % 2, :], rot[:, n % 2, :], std[:, n % 2, :]
                        dve.wait_ge(s_ms, 4 * c + n + 1)
                        if c:
                            dve.wait_ge(s_st[n], 16 * c)
                        dve.tensor_tensor(rc, ps_sw[:, n % 2, :], sin[:, cols], ALU.mult).then_inc(s_rope, 1)
                        dve.tensor_tensor(zc, zc, cos[:, cols], ALU.mult).then_inc(s_rope, 1)
                        dve.wait_ge(s_rope, done + 2)
                        dve.tensor_tensor(rc, rc, zc, ALU.add).then_inc(s_rope, 1)
                        dve.wait_ge(s_std, 4 * c + n + 1)
                        dve.reciprocal(sc, sc).then_inc(s_rope, 1)
                        dve.wait_ge(s_rope, done + 4)
                        dve.tensor_tensor(out[:, n, :], rc, sc, ALU.mult).then_inc(s_rot, 1)
                n = 0

                def step(ins):
                    nonlocal n
                    n += 1
                    ins.then_inc(s_dft, 1)
                    dve.wait_ge(s_dft, NV * group + n)

                def add(o, a, b):
                    step(dve.tensor_tensor(o, a, b, ALU.add))

                def sub(o, a, b):
                    step(dve.tensor_tensor(o, a, b, ALU.subtract))

                def axpy(o, c, a, b, op=ALU.add):
                    step(dve.scalar_tensor_tensor(o, a, c, b, ALU.mult, op))

                e, o = (lambda i: eo[:, i, :]), (lambda i: eo[:, 8 + i, :])
                re, im = (lambda k: z[:, k, :]), (lambda k: z[:, 8 + k, :])
                pq = [None] + [(e(n), e(3 + n)) for n in (1, 2, 3)]
                (p1, q1), (p2, q2), (p3, q3) = pq[1:]
                u, v, w = o(1), o(2), o(3)

                def dft_even():
                    dve.wait_ge(s_f, 16 * (group + 1))
                    add(eo[:, 0:8, :], z[:, 0:8, :], z[:, 8:16, :])
                    sub(eo[:, 8:16, :], z[:, 0:8, :], z[:, 8:16, :])
                    t = [z[:, i, :] for i in range(4)]
                    add(z[:, 0:4, :], eo[:, 0:4, :], eo[:, 4:8, :])
                    sub(eo[:, 0:4, :], eo[:, 0:4, :], eo[:, 4:8, :])
                    add(e(4), t[0], t[2])
                    add(e(5), t[1], t[3])
                    sub(re(4), t[0], t[2])
                    sub(im(4), t[3], t[1])
                    add(re(0), e(4), e(5))
                    sub(re(8), e(4), e(5))
                    sub(e(4), e(1), e(3))
                    add(e(5), e(1), e(3))
                    axpy(re(2), C2, e(4), e(0))
                    axpy(re(6), -C2, e(4), e(0))
                    axpy(im(2), -C2, e(5), e(2), ALU.subtract)
                    axpy(im(6), -C2, e(5), e(2))

                def dft_odd_re():
                    for j in (1, 2, 3):
                        sub(pq[j][0], o(j), o(8 - j))
                        add(pq[j][1], o(j), o(8 - j))
                    axpy(u, C2, p2, o(0))
                    axpy(v, -C2, p2, o(0))
                    step(dve.tensor_scalar(w, p3, C3, None, ALU.mult))
                    axpy(w, C1, p1, w)
                    add(re(1), u, w)
                    sub(re(7), u, w)
                    step(dve.tensor_scalar(w, p3, C1, None, ALU.mult))
                    axpy(w, C3, p1, w, ALU.subtract)
                    add(re(3), v, w)
                    sub(re(5), v, w)

                def dft_odd_im():
                    axpy(u, C2, q2, o(4))
                    axpy(v, C2, q2, o(4), ALU.subtract)
                    step(dve.tensor_scalar(w, q3, C1, None, ALU.mult))
                    axpy(w, C3, q1, w)
                    sub(im(7), u, w)
                    add(w, u, w)
                    step(dve.tensor_scalar(im(1), w, -1.0, None, ALU.mult))
                    step(dve.tensor_scalar(w, q3, C3, None, ALU.mult))
                    axpy(w, C1, q1, w, ALU.subtract)
                    sub(im(5), v, w)
                    add(w, v, w)
                    step(dve.tensor_scalar(im(3), w, -1.0, None, ALU.mult))

                def split_z(first):
                    if not first:
                        dve.wait_ge(s_zst, 32 * group)
                    dve.tensor_copy(z_hi, z).then_inc(s_z, 1)
                    dve.wait_ge(s_z, 2 * group + 1)
                    dve.tensor_tensor(z_lo, z, z_hi, ALU.subtract).then_inc(s_z, 1)

                def split_kv(g, first):
                    src = ps_sw[:, 0, :].rearrange("p (t a d) -> p a t d", a=NKV, d=HD)
                    dve.wait_ge(s_tr, g + 1)
                    dve.wait_ge(s_k, 64 * (g + 1))
                    if not first:
                        dve.wait_ge(s_kvst, 16 * NKV * g)
                    for a in range(NKV):
                        at = kv[:, a, 1, :].rearrange("p (t c) -> p t c", c=P)
                        dve.tensor_copy(at[:, :, 0:HD], src[:, a]).then_inc(s_kv, 1)
                        dve.tensor_copy(kv[:, a, 0, :], k_st[:, a, :]).then_inc(s_kv, 1)
                        dve.wait_ge(s_kv, KVS * g + 4 * a + 2)
                        dve.tensor_tensor(at[:, :, HD:P], src[:, a], at[:, :, 0:HD], ALU.subtract).then_inc(s_kv, 1)
                        dve.tensor_tensor(kv[HD:P, a, 0, :], k_st[HD:P, a, :], kv[HD:P, a, 0, :], ALU.subtract)\
                            .then_inc(s_kv, 1)

                def quarter(g, first):
                    nonlocal group, n
                    group, n = g, 0
                    for j, work in enumerate((dft_even, dft_odd_re, dft_odd_im, lambda: split_kv(g, first))):
                        lo_part(PER * g + NQKV + j, j % 2)
                        work()
                        if j == 2:
                            assert n == NV
                            split_z(first)

                group = 0
                quarter(0, True)
                with dve.Fori(1, NG) as g:
                    quarter(g, False)

            @block.tensor
            def _(pe):
                def block_products(n, u):
                    for k in range(KD):
                        m = product3(pe, ps[:, n, :], w_hi[u][:, k, :], w_lo[u][:, k, :],
                                     hT_hi[:, k, n * BLK:(n + 1) * BLK], hT_lo[:, k, n * BLK:(n + 1) * BLK],
                                     k == 0, k == KD - 1)
                    m.then_inc(s_mm, 1)

                def rope_products(c, n):
                    if c == 0 and n == 0:
                        pe.wait_ge(s_c, 16 * 6)
                    pe.wait_ge(s_zg, 4 * c + n + 1)
                    if c or n >= 2:
                        pe.wait_ge(s_rot, 4 * c + n - 1)
                    pe.matmul(ps_sw[:, n % 2, :], swap, zg[:, n % 2, :], start=True, stop=True)
                    pe.matmul(ps_ms[:, n % 2, :], head_mean, sq[:, n % 2, :], start=True, stop=True).then_inc(s_ms, 1)

                for c in range(NQC + 2):
                    pe.wait_ge(s_lo, c + 1)
                    for n in range(NB):
                        if c:
                            pe.wait_ge(s_zg, 4 * (c - 1) + n + 1)
                        if c <= NQC and n >= 2:
                            rope_products(c, n - 2)
                        if c and n < 2:
                            rope_products(c - 1, n + 2)
                        block_products(n, c % 2)
                def turn_v(g, first):
                    pe.wait_ge(s_v, 16 * (g + 1))
                    if first:
                        pe.wait_ge(s_rot, NB * (NQC + 1))
                    else:
                        pe.wait_ge(s_kv, KVS * g)
                    for t in range(BLK // P):
                        m = pe.transpose(ps_sw[:, 0, t * P:(t + 1) * P], v_st[:, t * P:(t + 1) * P], ident[:])
                    m.then_inc(s_tr, 1)

                def quarter(g, first):
                    for j in range(PER):
                        c = PER * g + j
                        if j == 2:
                            turn_v(g, first)
                        pe.wait_ge(s_lo, c + NQKV + 1)
                        for n in range(NB):
                            pe.wait_ge(s_out, NB * c + n + 1)
                            block_products(n, j % 2)

                quarter(0, True)
                with pe.Fori(1, NG) as g:
                    quarter(g, False)
        return s_st


def fourier_phase(nc, head0, z_d, t_pos, t_chan, qkv_d, kv_d, ident, yT_d):
    with Res(nc, "fft") as r:
        z_hi, z_lo = (r.sb(n, [P, 2, N1, P], F32R) for n in ("z_hi", "z_lo"))
        tp_st = r.sb("tp_st", [P, K1, 3 * P])
        tp_hi, tp_lo = (r.sb(n, [P, K1, 3 * P], F32R) for n in ("tp_hi", "tp_lo"))
        tc_st = r.sb("tc_st", [P, 3 * P])
        tc_hi, tc_lo = (r.sb(n, [P, 3 * P], F32R) for n in ("tc_hi", "tc_lo"))
        g_hi, g_lo = (r.sb(n, [P, 2, 2, K1, P], F32R) for n in ("g_hi", "g_lo"))
        yT = r.sb("yT", [P, 2, S])
        ps_g = r.ps("ps_g", [P, 2, BLK])
        ps_y = r.ps("ps_y", [P, 4, BLK])
        ps_m = r.ps("ps_m", [P, 2, BLK])
        s_z = [[r.sem(f"z_loaded{i}_{a}") for a in range(2)] for i in range(2)]
        s_out = [r.sem(f"y_stored{i}") for i in range(2)]
        s_tp = [r.sem(f"tp_loaded{i}") for i in range(K1 // 3)]
        s_tc, s_tabs, s_g, s_ghi, s_glo, s_y, s_yev = (
            r.sem(n) for n in ("tc_loaded", "table_steps", "g", "g_hi_made", "g_lo_made", "y", "y_copied"))
        NBK = (K1 + 1) // 2
        PIECES = [(0, 3, False), (3, 3, False), (6, 3, False), (1, 4, True), (5, 3, True)]
        NY = len(PIECES)
        steps = [("G", 0, k) for k in range(K1)]
        for g in range(1, NG):
            steps += [("G", g, k) for k in range(K1)] + [("Y", g - 1, j) for j in range(NY)]
        steps += [("Y", NG - 1, j) for j in range(NY)]
        FIRST = 6
        SPLIT = [4, 8, 14, 20]
        maxima = [[] for _ in steps]
        for m in range(NM):
            maxima[FIRST + m * (len(steps) - 2 - FIRST) // NM].append(m)

        def width(b):
            return min(2, K1 - 2 * b)

        with r.block() as block:

            @block.sync
            def _(sp):
                def load_z(g):
                    if g >= 2:
                        sp.wait_ge(s_g, NBK * (g - 1))
                    for a in range(2):
                        for part, dst in enumerate((z_hi, z_lo)):
                            halves = lambda z: z.rearrange("p (b a n) -> p a b n", a=2, b=2)[:, a]
                            sp.dma_start(halves(dst[:, g % 2, :, :].rearrange("p n c -> p (n c)").bitcast(F32)),
                                         halves(z_d[part, g])).then_inc(s_z[g % 2][a], 16)

                def store_y(g):
                    sp.wait_ge(s_yev, NY * (g + 1))
                    sp.dma_start(yT_d[g], yT[:, g % 2, :]).then_inc(s_out[g % 2], 16)

                for k in range(0, K1, 3):
                    sp.dma_start(tp_st[:, k:k + 3, :], t_pos[:, k:k + 3, :]).then_inc(s_tp[k // 3], 16)
                    if k == 0:
                        load_z(0)
                load_q(sp, head0, qkv_d, 0)
                sp.dma_start(head0.kmax[:, 0, :].bitcast(F32), kv_d[0, :, 0, :]).then_inc(head0.s_km[0], 16)
                sp.dma_start(tc_st[:], t_chan).then_inc(s_tc, 16)
                load_z(1)
                sp.dma_start(head0.kmax[:, 1, :].bitcast(F32), kv_d[1, :, 0, :]).then_inc(head0.s_km[1], 16)
                load_kv(sp, head0, head0.kv, 0, kv_d, 0)
                for g in range(NG):
                    if g + 2 < NG:
                        load_z(g + 2)
                    if g == 1:
                        sp.wait_ge(head0.s_q2, NB)
                        load_q(sp, head0, qkv_d, 1)
                    store_y(g)
                sp.wait_ge(head0.s_zero, 3)
                place_row(sp, head0, 0, head0.q2, 0)
                for i in range(2):
                    sp.wait_ge(s_out[i], 16 * NG // 2)

            @block.scalar
            def _(act):
                def high_part(g, b):
                    act.wait_ge(s_g, NBK * g + b + 1)
                    if g >= 2:
                        act.wait_ge(s_y, NY * (g - 1))
                    m = width(b)
                    act.activation(g_hi[:, g % 2, :, 2 * b:2 * b + m, :].rearrange("p c k m -> p k c m"),
                                   ps_g[:, (NBK * g + b) % 2, 0:m * 2 * P].rearrange("p (k c m) -> p k c m", k=m, c=2),
                                   ACT.Copy).then_inc(s_ghi, 1)

                def copy_y(g, j):
                    kk, m, mirrored = PIECES[j]
                    at = yT[:, g % 2, :].rearrange("p (k2 k1) -> p k1 k2", k1=N1)
                    act.wait_ge(s_y, NY * g + j + 1)
                    if g >= 2:
                        act.wait_ge(s_out[g % 2], 16 * (g // 2))
                    src = ps_y[:, (NY * g + j) % 4, 0:m * P].rearrange("p (k m) -> p k m", k=m)
                    dst = at[:, kk:kk + m, :]
                    if mirrored:
                        dst = at[:, N1 - kk - m + 1:N1 - kk + 1, :][:, ::-1, ::-1]
                    act.activation(dst, src, ACT.Copy).then_inc(s_yev, 1)

                for kind, g, i in steps:
                    if kind == "Y":
                        copy_y(g, i)
                    elif i % 2 or i == K1 - 1:
                        high_part(g, i // 2)

            @block.gpsimd
            def _(pool):
                constant_rows(pool, head0, head0.kv, head0.q2, 0)

            @block.vector
            def _(dve):
                def split_table(n, hi, lo, src):
                    dve.tensor_copy(hi, src).then_inc(s_tabs, 1)
                    dve.wait_ge(s_tabs, 2 * n + 1)
                    dve.tensor_tensor(lo, src, hi, ALU.subtract).then_inc(s_tabs, 1)

                def split_q(piece):
                    cols = slice(piece * BLK, (piece + 1) * BLK)
                    dve.tensor_copy(head0.q1[:, cols], head0.q_st[:, cols]).then_inc(head0.s_q1, 1)
                    dve.wait_ge(head0.s_q1, piece + 1)
                    dve.tensor_tensor(head0.q2[0:HD, cols], head0.q_st[0:HD, cols], head0.q1[0:HD, cols], ALU.subtract)\
                        .then_inc(head0.s_q2, 1)

                def low_part(g, b):
                    m = width(b)
                    c = NBK * g + b
                    dve.wait_ge(s_ghi, c + 1)
                    dve.tensor_tensor(g_lo[:, g % 2, :, 2 * b:2 * b + m, :].rearrange("p c k m -> p k c m"),
                                      ps_g[:, c % 2, 0:m * 2 * P].rearrange("p (k c m) -> p k c m", k=m, c=2),
                                      g_hi[:, g % 2, :, 2 * b:2 * b + m, :].rearrange("p c k m -> p k c m"),
                                      ALU.subtract).then_inc(s_glo, 1)

                def read_max(m):
                    dve.wait_ge(head0.s_m, m + 1)
                    dve.tensor_reduce(head0.mx[:, m:m + 1], ps_m[:, m % 2, :], AX.X, ALU.max).then_inc(head0.s_mr, 1)

                for k in range(K1):
                    dve.wait_ge(s_tp[k // 3], 16)
                    split_table(k, tp_hi[:, k, :], tp_lo[:, k, :], tp_st[:, k, :])
                behind = None
                for n, (kind, g, i) in enumerate(steps):
                    for m in maxima[n]:
                        read_max(m)
                    if behind is not None:
                        low_part(*behind)
                    behind = (g, i // 2) if kind == "G" and (i % 2 or i == K1 - 1) else None
                    if n in SPLIT:
                        if n == SPLIT[0]:
                            dve.wait_ge(head0.s_q, 32)
                        split_q(SPLIT.index(n))
                    if n == K1:
                        dve.wait_ge(s_tc, 16)
                        split_table(K1, tc_hi[:], tc_lo[:], tc_st[:])
                dve.wait_ge(head0.s_mr, NM)
                dve.tensor_reduce(head0.mx2[:], head0.mx[:].rearrange("p (t a) -> p t a", a=NB), AX.X, ALU.max)\
                    .then_inc(head0.s_m2, 1)
                dve.wait_ge(head0.s_mt, 1)
                dve.tensor_scalar(head0.mrow[:], ps_m[0:NT, 0, 0:P], -1.0, None, ALU.mult).then_inc(head0.s_mc, 1)

            @block.tensor
            def _(pe):
                def g_products(g, k):
                    c = NBK * g + k // 2
                    if k in (0, 4):
                        pe.wait_ge(s_z[g % 2][k // 4], 32 * (g // 2 + 1))
                    if k % 2 == 0 and c >= 2:
                        pe.wait_ge(s_glo, c - 1)
                    if g == 0:
                        pe.wait_ge(s_tabs, 2 * k + 2)
                    at = ps_g[:, c % 2, (k % 2) * 2 * P:(k % 2 + 1) * 2 * P]
                    imag = 0 < k < K1 - 1
                    q = product3(pe, at, z_hi[:, g % 2, k, :], z_lo[:, g % 2, k, :], tp_hi[:, k, P:3 * P],
                                 tp_lo[:, k, P:3 * P], True, not imag)
                    if imag:
                        q = product3(pe, at, z_hi[:, g % 2, 8 + k, :], z_lo[:, g % 2, 8 + k, :], tp_hi[:, k, 0:2 * P],
                                     tp_lo[:, k, 0:2 * P], False, True)
                    if k % 2 or k == K1 - 1:
                        q.then_inc(s_g, 1)

                def y_products(g, j):
                    kk, m, mirrored = PIECES[j]
                    n = NY * g + j
                    if j == 0:
                        pe.wait_ge(s_glo, NBK * (g + 1))
                    if n == 0:
                        pe.wait_ge(s_tabs, 2 * K1 + 2)
                    if n >= 4:
                        pe.wait_ge(s_yev, n - 3)
                    sine = slice(2 * P, 3 * P) if mirrored else slice(P, 2 * P)
                    at = ps_y[:, n % 4, 0:m * P]
                    product3(pe, at, tc_hi[:, 0:P], tc_lo[:, 0:P], g_hi[:, g % 2, 0, kk:kk + m, :],
                             g_lo[:, g % 2, 0, kk:kk + m, :], True, False)
                    product3(pe, at, tc_hi[:, sine], tc_lo[:, sine], g_hi[:, g % 2, 1, kk:kk + m, :],
                             g_lo[:, g % 2, 1, kk:kk + m, :], False, True).then_inc(s_y, 1)

                def max_scores(m):
                    tile, quarter = divmod(m, NB)
                    if m == 0:
                        pe.wait_ge(head0.s_km[0], 16)
                    if quarter == 0 and tile % (NT // NB) == 0:
                        pe.wait_ge(head0.s_q1, tile // (NT // NB) + 1)
                    if m >= 2:
                        pe.wait_ge(head0.s_mr, m - 1)
                    pe.matmul(ps_m[:, m % 2, :], head0.q1[:, tile * P:(tile + 1) * P],
                              head0.kmax[:, 0, quarter * BLK:(quarter + 1) * BLK], start=True, stop=True)\
                        .then_inc(head0.s_m, 1)

                for n, (kind, g, i) in enumerate(steps):
                    (g_products if kind == "G" else y_products)(g, i)
                    for m in maxima[n]:
                        max_scores(m)
                pe.wait_ge(head0.s_m2, 1)
                pe.transpose(ps_m[0:NT, 0, 0:P], head0.mx2[:], ident[:]).then_inc(head0.s_mt, 1)
                pe.wait_ge(head0.s_km[1], 16)


class Head0:

    def __init__(self, r):
        self.kv = r.sb("kv", [P, 3, S], F32R)
        self.kmax = r.sb("kmax", [P, NKV, S], F32R)
        self.q_st = r.sb("q_st", [P, S])
        self.q1, self.q2 = r.sb("q1", [P, S], F32R), r.sb("q2", [P, S], F32R)
        self.mx, self.mx2, self.mrow = r.sb("mx", [P, NM]), r.sb("mx2", [P, NT]), r.sb("mrow", [NT, P], F32R)
        self.s_q, self.s_zero = r.sem("q_loaded"), r.sem("constant_rows")
        self.s_km = [r.sem(f"kmax_loaded{g}") for g in range(NKV)]
        self.s_kv = [r.sem(f"kv_loaded{i}") for i in range(2)]
        self.s_row = [r.sem(f"row_placed{i}") for i in range(2)]
        self.s_q1, self.s_q2 = r.sem("q1_made"), r.sem("q2_made")
        self.s_m, self.s_mr, self.s_m2 = r.sem("max_scores"), r.sem("max_read"), r.sem("max_of_row")
        self.s_mt, self.s_mc = r.sem("max_turned"), r.sem("max_row")


def load_q(sp, head0, qkv_d, h):
    for half in range(2):
        src = qkv_d[h // 2, (h % 2) * HD:(h % 2 + 1) * HD, :]
        sp.dma_start(head0.q_st[half * HD:(half + 1) * HD, :], src).then_inc(head0.s_q, 16)


def load_kv(sp, head0, slot, u, kv_d, g):
    sp.dma_start(slot[:, 0:2, :].bitcast(F32), kv_d[g]).then_inc(head0.s_kv[u], 16)
    sp.dma_start(slot[0:HD, 2, :].bitcast(F32), kv_d[g, 0:HD, 0, :]).then_inc(head0.s_kv[u], 16)


def place_row(sp, head0, h, q2, u):
    sp.wait_ge(head0.s_mc, h + 1)
    sp.dma_start(q2[HD:HD + 1, :].bitcast(F32), head0.mrow[:].bitcast(F32)).then_inc(head0.s_row[u], 16)


def constant_rows(engine, head0, kv, q2, u):
    engine.memset(q2[HD:P, :].bitcast(F32), 0.0).then_inc(head0.s_zero, 1)
    engine.memset(kv[HD:P, 2, :].bitcast(F32), 0.0).then_inc(head0.s_zero, 1)
    engine.wait_ge(head0.s_zero, 3 * u + 2)
    engine.memset(kv[HD:HD + 1, 2, :].bitcast(F32), 1.0).then_inc(head0.s_zero, 1)
    engine.wait_ge(head0.s_zero, 3 * u + 3)


def attention_phase(nc, head0, qkv_d, kv_d, ident, ones, o_d, sums_d):
    KP = NT // 2
    KA = KP - 1
    ST = NB * KP
    LAG = 4
    LO_LAG = 2
    FIRST, LAST = 1, 27
    subs = [[] for _ in range(ST)]
    for m in range(NM):
        subs[FIRST + m * (LAST + 1 - FIRST) // NM].append(m)
    SPLIT = [0, 5, 11, 17]
    SCALE = HD ** -0.5
    with Res(nc, "att") as r:
        kmax, q_st, mx, mx2, mrow = head0.kmax, head0.q_st, head0.mx, head0.mx2, head0.mrow
        kv = [head0.kv, r.sb("kv1", [P, 3, S], F32R)]
        q1 = [head0.q1, r.sb("q1_1", [P, S], F32R)]
        q2 = [head0.q2, r.sb("q2_1", [P, S], F32R)]
        prob = r.sb("prob", [P, 8, 2 * BLK])
        prob_hi = r.sb("prob_hi", [P, 4, 2 * BLK], F32R)
        prob_lo = r.sb("prob_lo", [P, 4, 2 * BLK], F32R)
        acc = r.sb("acc", [P, 2, 2 * BLK])
        o_sb = r.sb("o_sb", [P, 2, BLK])
        ones_r = r.sb("ones_r", [P, P], F32R)
        row = r.sb("row", [1, 2, BLK])
        ps_s = r.ps("ps_s", [P, 2, 2 * BLK])
        ps_m = r.ps("ps_m", [P, 2, BLK])
        ps_o = r.ps("ps_o", [P, BLK])
        ps_r = r.ps("ps_r", [P, BLK])
        s_q, s_kv, s_zero, s_q1, s_q2 = head0.s_q, head0.s_kv, head0.s_zero, head0.s_q1, head0.s_q2
        s_m, s_mr, s_m2, s_mt, s_mc, s_row = head0.s_m, head0.s_mr, head0.s_m2, head0.s_mt, head0.s_mc, head0.s_row
        s_s, s_exp, s_hi, s_lo, s_pv = (r.sem(n) for n in ("scores", "exp", "p_hi", "p_lo", "pv"))
        s_lo_pool, s_ones = r.sem("p_lo_pool"), r.sem("ones_rounded")
        s_add, s_sum, s_rc, s_oc = (r.sem(n) for n in ("added", "sum", "sum_copied", "o_copied"))
        s_st = [r.sem(f"o_stored{i}") for i in range(2)]
        s_rst = [r.sem(f"sum_stored{i}") for i in range(2)]

        def wait_low(engine, h, s):
            if s < 0:
                h, s = h - 1, s + ST
            qb, kp = divmod(s, KP)
            if kp == KP - 1:
                engine.wait_ge(s_lo_pool, NB * h + qb + 1)
            else:
                engine.wait_ge(s_lo, KA * (NB * h + qb) + kp + 1)

        with r.block() as block:

            @block.sync
            def _(sp):
                def store(h, qb, first=False):
                    sp.wait_ge(s_oc, NB * h + qb + 1)
                    at = o_d[:, bass.ds(h, 1), :, qb * BLK:(qb + 1) * BLK]
                    for half in range(2):
                        sp.dma_start(at[half:half + 1].rearrange("a h d q -> (a h d) q"),
                                     o_sb[half * HD:(half + 1) * HD, qb % 2, :]).then_inc(s_st[qb % 2], 16)
                    sp.wait_ge(s_rc, NB * h + qb + 1)
                    sp.dma_start(sums_d[bass.ds(h, 1), qb * BLK:(qb + 1) * BLK], row[:, qb % 2, :])\
                        .then_inc(s_rst[qb % 2], 16)

                def body(h, u, is_first, has_next):
                    if has_next:
                        if not is_first:
                            sp.wait_ge(s_pv, ST * h)
                        load_kv(sp, head0, kv[1 - u], 1 - u, kv_d, (h + 1) * NKV // NH)
                    if not is_first:
                        store(h - 1, NB - 1)
                    for qb in range(NB - 1):
                        if h + 2 < NH and qb == NB - 2:
                            sp.wait_ge(s_q2, NB * (h + 2))
                            load_q(sp, head0, qkv_d, h + 2)
                        store(h, qb)
                    if has_next:
                        place_row(sp, head0, h + 1, q2[1 - u], 1 - u)

                for h in range(NH):
                    body(h, h % 2, h == 0, h + 1 < NH)
                store(NH - 1, NB - 1)
                for i in range(2):
                    sp.wait_ge(s_st[i], 16 * NH * NB)
                    sp.wait_ge(s_rst[i], 8 * NH * NB)

            @block.scalar
            def _(act):
                def exp(h, s):
                    g = ST * h + s
                    act.wait_ge(s_s, g + 1)
                    if not isinstance(g, int) or g >= 8:
                        old = s - 8
                        wait_low(act, h, old)
                        if old % KP < KA:
                            act.wait_ge(s_add, KA * (NB * h + old // KP) + max(old % KP, 1))
                    act.activation(prob[:, s % 8, :], ps_s[:, s % 2, :], ACT.Exp, scale=SCALE).then_inc(s_exp, 1)

                def hi(h, s):
                    g = ST * h + s
                    act.wait_ge(s_exp, g + 1)
                    if not isinstance(g, int) or g >= 4:
                        act.wait_ge(s_pv, g - 3)
                    act.activation(prob_hi[:, s % 4, :], prob[:, s % 8, :], ACT.Copy).then_inc(s_hi, 1)

                def o_copy(h, qb):
                    n = NB * h + qb
                    act.wait_ge(s_pv, KP * (n + 1))
                    if not isinstance(n, int) or n >= 2:
                        act.wait_ge(s_st[qb % 2], 32 * (NB // 2 * h + qb // 2))
                    act.activation(o_sb[:, qb % 2, :], ps_o[:], ACT.Copy).then_inc(s_oc, 1)

                def sum_copy(h, qb):
                    n = NB * h + qb
                    act.wait_ge(s_sum, n + 1)
                    if not isinstance(n, int) or n >= 2:
                        act.wait_ge(s_rst[qb % 2], 16 * (NB // 2 * h + qb // 2))
                    act.activation(row[:, qb % 2, :], ps_r[0:1, :], ACT.Copy).then_inc(s_rc, 1)

                def split_q_hi(h, u, piece):
                    cols = slice(piece * BLK, (piece + 1) * BLK)
                    if piece == 0:
                        act.wait_ge(s_q, 32 * (h + 1))
                        if not isinstance(h, int) or h > 1:
                            act.wait_ge(s_s, ST * (h - 1))
                    act.activation(q1[u][:, cols], q_st[:, cols], ACT.Copy).then_inc(s_q1, 1)

                def body(h, u, first_head=False, has_next=True):
                    for s in range(ST):
                        if has_next and s in SPLIT:
                            split_q_hi(h + 1, 1 - u, SPLIT.index(s))
                        if s % KP == LAG and not (first_head and s < KP):
                            before = (h, s // KP - 1) if s >= KP else (h - 1, NB - 1)
                            sum_copy(*before)
                            o_copy(*before)
                        exp(h, s)
                        if s:
                            hi(h, s - 1)
                        elif not first_head:
                            hi(h - 1, ST - 1)

                body(0, 0, True)
                body(1, 1)
                with act.Fori(1, NH // 2 - 1) as i:
                    for u in range(2):
                        body(2 * i + u, u)
                body(NH - 2, 0)
                body(NH - 1, 1, False, False)
                hi(NH - 1, ST - 1)
                sum_copy(NH - 1, NB - 1)
                o_copy(NH - 1, NB - 1)

            @block.gpsimd
            def _(pool):
                def body(h, first_head):
                    for qb in range(NB):
                        for kp in range(1, KA):
                            s = qb * KP + kp
                            n = KA * (NB * h + qb)
                            pool.wait_ge(s_exp, ST * h + s + 1)
                            if kp == 1:
                                if not (first_head and qb < 2):
                                    pool.wait_ge(s_sum, NB * h + qb - 1)
                                pool.tensor_tensor(acc[:, qb % 2, :], prob[:, (s - 1) % 8, :], prob[:, s % 8, :],
                                                   ALU.add).then_inc(s_add, 1)
                            else:
                                pool.wait_ge(s_add, n + kp - 1)
                                pool.tensor_tensor(acc[:, qb % 2, :], acc[:, qb % 2, :], prob[:, s % 8, :],
                                                   ALU.add).then_inc(s_add, 1)
                        pool.wait_ge(s_add, n + KA - 1)
                        pool.tensor_tensor(acc[:, qb % 2, 0:BLK], acc[:, qb % 2, 0:BLK], acc[:, qb % 2, BLK:2 * BLK],
                                           ALU.add).then_inc(s_add, 1)
                        s = qb * KP + KP - 1
                        pool.wait_ge(s_hi, ST * h + s + 1)
                        pool.tensor_tensor(prob_lo[:, s % 4, :], prob[:, s % 8, :], prob_hi[:, s % 4, :], ALU.subtract)\
                            .then_inc(s_lo_pool, 1)

                body(0, True)
                with pool.Fori(1, NH) as h:
                    body(h, False)

            @block.vector
            def _(dve):
                def split_q_lo(h, u, piece):
                    cols = slice(piece * BLK, (piece + 1) * BLK)
                    dve.wait_ge(s_q1, NB * h + piece + 1)
                    dve.tensor_tensor(q2[u][0:HD, cols], q_st[0:HD, cols], q1[u][0:HD, cols], ALU.subtract)\
                        .then_inc(s_q2, 1)

                def read_max(h, m):
                    dve.wait_ge(s_m, NM * h + m + 1)
                    dve.tensor_reduce(mx[:, m:m + 1], ps_m[:, m % 2, :], AX.X, ALU.max).then_inc(s_mr, 1)

                def row_max(h):
                    dve.wait_ge(s_mr, NM * (h + 1))
                    dve.tensor_reduce(mx2[:], mx[:].rearrange("p (t a) -> p t a", a=NB), AX.X, ALU.max).then_inc(s_m2, 1)

                def row_copy(h):
                    dve.wait_ge(s_mt, h + 1)
                    dve.wait_ge(s_s, ST * (h - 1) + 1)
                    dve.tensor_scalar(mrow[:], ps_r[0:NT, 0:P], -1.0, None, ALU.mult).then_inc(s_mc, 1)

                def lo(h, s):
                    if s % KP == KP - 1:
                        return
                    dve.wait_ge(s_hi, ST * h + s + 1)
                    dve.tensor_tensor(prob_lo[:, s % 4, :], prob[:, s % 8, :], prob_hi[:, s % 4, :], ALU.subtract)\
                        .then_inc(s_lo, 1)

                def body(h, u, first_head, has_next):
                    for s in range(ST):
                        if has_next and s == 0:
                            dve.wait_ge(s_q, 32 * (h + 2))
                            if not first_head:
                                dve.wait_ge(s_s, ST * h)
                        if has_next:
                            for m in subs[s][:2]:
                                read_max(h + 1, m)
                        if s >= LO_LAG:
                            lo(h, s - LO_LAG)
                        elif not first_head:
                            lo(h - 1, ST + s - LO_LAG)
                        if has_next:
                            if s in SPLIT:
                                split_q_lo(h + 1, 1 - u, SPLIT.index(s))
                            for m in subs[s][2:]:
                                read_max(h + 1, m)
                            if s == LAST:
                                row_max(h + 1)
                            if s == LAST + 1:
                                row_copy(h + 1)

                constant_rows(dve, head0, kv[1], q2[1], 1)
                dve.tensor_copy(ones_r[:], ones[:]).then_inc(s_ones, 1)
                body(0, 0, True, True)
                body(1, 1, False, True)
                with dve.Fori(1, NH // 2 - 1) as i:
                    for u in range(2):
                        body(2 * i + u, u, False, True)
                body(NH - 2, 0, False, True)
                body(NH - 1, 1, False, False)
                for s in range(ST - LO_LAG, ST):
                    lo(NH - 1, s)

            @block.tensor
            def _(pe):
                def scores(h, u, s):
                    g = ST * h + s
                    qb, kp = divmod(s, KP)
                    cols = slice(qb * BLK, (qb + 1) * BLK)
                    if not isinstance(g, int) or g >= 2:
                        pe.wait_ge(s_exp, g - 1)
                    for j in range(2):
                        keys = slice((2 * kp + j) * P, (2 * kp + j + 1) * P)
                        at = ps_s[:, s % 2, j * BLK:(j + 1) * BLK]
                        pe.matmul(at, kv[u][:, 0, keys], q1[u][:, cols], start=True, stop=False)
                        m = pe.matmul(at, kv[u][:, 2, keys], q2[u][:, cols], start=False, stop=True)
                    m.then_inc(s_s, 1)

                def maxima(h, u, m, g):
                    tile, quarter = divmod(m, NB)
                    if quarter == 0 and tile % (NT // NB) == 0:
                        pe.wait_ge(s_q1, NB * h + tile // (NT // NB) + 1)
                    pe.wait_ge(s_mr, NM * h + m - 1)
                    pe.matmul(ps_m[:, m % 2, :], q1[u][:, tile * P:(tile + 1) * P],
                              kmax[:, g, quarter * BLK:(quarter + 1) * BLK], start=True, stop=True).then_inc(s_m, 1)

                def turn_max(h):
                    pe.wait_ge(s_m2, h + 1)
                    pe.wait_ge(s_rc, NB * (h - 1) + NB - 1)
                    pe.transpose(ps_r[0:NT, 0:P], mx2[:], ident[:]).then_inc(s_mt, 1)

                def pv(h, u, s):
                    qb, kp = divmod(s, KP)
                    wait_low(pe, h, s)
                    if kp == KP - 1:
                        row_sum(h, qb, s)
                    if kp == 0 and (not isinstance(h, int) or h or qb):
                        pe.wait_ge(s_oc, NB * h + qb)
                    for j in range(2):
                        t = 2 * kp + j
                        v = kv[u][:, 1, t * P:(t + 1) * P]
                        for part, src in enumerate((prob_hi, prob_lo)):
                            m = pe.matmul(ps_o[:], v, src[:, s % 4, j * BLK:(j + 1) * BLK],
                                          start=t == 0 and part == 0, stop=t == NT - 1 and part == 1)
                    m.then_inc(s_pv, 1)

                def row_sum(h, qb, s):
                    n = NB * h + qb
                    pe.wait_ge(s_add, KA * (n + 1))
                    if not isinstance(n, int) or n:
                        pe.wait_ge(s_rc, n)
                    if qb == NB - 1 and not (isinstance(h, int) and h == NH - 1):
                        pe.wait_ge(s_mc, h + 2)
                    if isinstance(n, int) and n == 0:
                        pe.wait_ge(s_ones, 1)
                    pe.matmul(ps_r[:], ones[:], acc[:, qb % 2, 0:BLK], start=True, stop=False)
                    for j in range(2):
                        for part, src in enumerate((prob_hi, prob_lo)):
                            m = pe.matmul(ps_r[:], ones_r[:], src[:, s % 4, j * BLK:(j + 1) * BLK], start=False,
                                          stop=j == 1 and part == 1)
                    m.then_inc(s_sum, 1)

                def body(i, u, has_next, first_head=False):
                    h = 2 * i + u
                    pe.wait_ge(s_kv[u], 32 * i + 32)
                    pe.wait_ge(s_row[u], 16 * i + 16)
                    pe.wait_ge(s_q2, NB * (h + 1))
                    g = ((h + 1) * NKV // NH) if isinstance(h, int) else bass.ds((h + 1) // (NH // NKV), 1)

                    def maxima_of_step(s, a, b):
                        if has_next:
                            for m in subs[s][a:b]:
                                maxima(h + 1, 1 - u, m, g)

                    for s in range(ST):
                        maxima_of_step(s, 0, 1)
                        scores(h, u, s)
                        maxima_of_step(s, 1, 2)
                        if has_next and s == LAST + 1:
                            turn_max(h + 1)
                        if s >= LAG:
                            pv(h, u, s - LAG)
                        elif not first_head:
                            pv(h - 1, 1 - u, ST + s - LAG)
                        maxima_of_step(s, 2, 3)

                body(0, 0, True, True)
                body(0, 1, True)
                with pe.Fori(1, NH // 2 - 1) as i:
                    for u in range(2):
                        body(i, u, True)
                body(NH // 2 - 1, 0, True)
                body(NH // 2 - 1, 1, False)
                for s in range(ST - LAG, ST):
                    pv(NH - 1, 1, s)


def merge_phase(nc, x_d, w_branch, w_out_d, o_d, sums_d, rec_d, yT_d, gates_d, gate_rows, x1_d, first_sem, kept):
    TB = BLK // P
    KB = NQC
    AS = 6
    with Res(nc, "merge") as r:
        w_st = r.sb("w_st", [P, 2, D])
        wb_hi, wb_lo = (r.sb(n, [P, 2, KD, P], F32R) for n in ("wb_hi", "wb_lo"))
        wo_hi, wo_lo = (r.sb(n, [P, KD, D], F32R) for n in ("wo_hi", "wo_lo"))
        st_a, st_b = (r.sb(n, [P, KB, BLK]) for n in ("st_a", "st_b"))
        act_hi, act_lo = (r.sb(n, [P, KD, BLK], F32R) for n in ("act_hi", "act_lo"))
        mg_hi, mg_lo = (r.sb(n, [P, KD, BLK], F32R) for n in ("mg_hi", "mg_lo"))
        gate = r.sb("gate", [P, 2, 2, BLK])
        g1 = r.sb("g1", [P, D])
        x = r.sb("x", [P, 2, D])
        x1 = r.sb("x1", [P, 2, D])
        x_staged, x1_staged = (b[:].rearrange("p a (c q) -> p (a c) q", q=BLK) for b in (x, x1))
        junk = r.sb("junk", [P, D], mybir.dt.bfloat16)
        sums, mean, std, rstd = (r.sb(n, [P, 2]) for n in ("sums", "mean", "std", "rstd"))
        ps_b = r.ps("ps_b", [P, 2, 2, BLK])
        ps_y = r.ps("ps_y", [P, 2, D])
        s_w = [r.sem(f"w_loaded{i}") for i in range(2)]
        s_wo = [r.sem(f"w_out_loaded{i}") for i in range(2)]
        s_wohi, s_wolo = r.sem("w_out_hi_made"), r.sem("w_out_lo_made")
        s_gate = [r.sem(f"gates_loaded{i}") for i in range(2)]
        s_x = [r.sem(f"x_loaded{i}") for i in range(2)]
        s_st = [r.pool_dma_sem(f"x1_stored{i}") for i in range(2)]
        s_o, s_yt, s_g1 = r.sem("o_loaded"), r.sem("yT_loaded"), r.sem("g1_loaded")
        s_sums, s_rec, s_recst, s_rb = (r.sem(n) for n in ("sums_loaded", "rec_made", "rec_stored", "rec_loaded"))
        total = r.sb("total", [P, NH * S // P])
        s_whi, s_wlo, s_act, s_br, s_mg, s_y = (
            r.sem(n) for n in ("w_hi_made", "w_lo_made", "act_steps", "branch", "merge_steps", "y"))
        s_sq, s_mean, s_std, s_rstd, s_n1, s_x1 = (r.sem(n) for n in ("squares", "mean", "root", "rstd", "scaled", "x1"))
        with r.block() as block:

            @block.sync
            def _(sp):
                def load_w(src, i, u, first):
                    if not first:
                        sp.wait_ge(s_wlo, 2 * i + u - 1)
                    sp.dma_start(w_st[:, u, :], src).then_inc(s_w[u], 16)

                def load_w_out(k):
                    if k >= 2:
                        sp.wait_ge(s_wolo, k - 1)
                    sp.dma_start(x[:, k % 2, :], w_out_d[k]).then_inc(s_wo[k % 2], 16)

                def load_o(b, second=st_b):
                    cols = bass.ds(b * BLK, BLK)
                    if not isinstance(b, int) or b:
                        sp.wait_ge(s_act, AS * b)
                    for half, dst in ((0, st_a), (1, second)):
                        for t in range(2):
                            src = o_d[half].rearrange("(c t) d s -> t d c s", t=2)[t][:, :, cols]
                            sp.dma_start(dst[t * HD:(t + 1) * HD, :, :], src).then_inc(s_o, 16)

                def load_rec(b, dst):
                    for t in range(2):
                        src = rec_d.rearrange("(c t) s -> t c s", t=2)[t:t + 1, :, bass.ds(b * BLK, BLK)]
                        sp.dma_start(dst[t * HD:(t + 1) * HD, :, :], src.broadcast_to([HD, KB, BLK])).then_inc(s_rb, 16)

                def load_y(b):
                    sp.dma_start(st_b[:], yT_d.rearrange("g c s -> c g s")[:, :, bass.ds(b * BLK, BLK)])\
                        .then_inc(s_yt, 16)

                def body(b, last, first=False):
                    for m in range(KD):
                        if m >= 2:
                            load_w(w_branch[m], KD // 2 * b + m // 2, m % 2, False)
                        if m >= 2 or not isinstance(b, int) or b:
                            sp.wait_ge(s_mg, 5 * (KD * b + m - 1))
                        for j in range(2):
                            at = gates_d[bass.ds(b, 1), 2 * m + j, :, :].rearrange("o p s -> (o p) s")
                            sp.dma_start(gate[:, m % 2, j, :], at).then_inc(s_gate[m % 2], 16)
                        if first:
                            load_w_out(m)
                    if not last:
                        load_o(b + 1)
                        for u in range(2):
                            load_w(w_branch[u], KD // 2 * (b + 1), u, False)
                    for j in range(TB):
                        n = TB * b + j
                        if j >= 2 or not isinstance(b, int) or b:
                            sp.wait_ge(s_x1, n - 1)
                        elif j == 0:
                            sp.wait_ge(s_wolo, KD)
                        sp.dma_start(x[:, j % 2, :], x_d[bass.ds(n, 1), :, :].rearrange("o p d -> (o p) d"))\
                            .then_inc(s_x[j % 2], 16)
                        if j == 0 and not last:
                            sp.wait_ge(s_act, AS * (b + 1) + 1)
                            load_rec(b + 1, st_b)
                        if j == 1 and not last:
                            sp.wait_ge(s_act, AS * (b + 1) + 2)
                            load_y(b + 1)
                sp.sem_clear(range(first_sem, kept[0].num))
                sp.sem_clear(range(kept[-1].num + 1, min(r.sem_nums)))
                sp.dma_start(total[:], sums_d.rearrange("h (a b) -> (h a) b", b=P)).then_inc(s_sums, 16)
                load_w(w_branch[0], 0, 0, True)
                load_y(0)
                sp.wait_ge(s_rec, 1)
                sp.dma_start(rec_d.rearrange("h (a b) -> (h a) b", b=P), total[:]).then_inc(s_recst, 16)
                load_o(0, x1_staged)
                sp.wait_ge(s_recst, 16)
                load_rec(0, x_staged)
                load_w(w_branch[1], 0, 1, True)
                sp.dma_start(g1[:], gate_rows).then_inc(s_g1, 16)
                sp.wait_ge(s_act, AS - 2)
                body(0, False, True)
                with sp.Fori(1, NB - 1) as b:
                    body(b, False)
                body(NB - 1, True)

            @block.gpsimd
            def _(pool):
                with pool.Fori(0, NB) as b:
                    for j in range(TB):
                        pool.wait_ge(s_x1, TB * b + j + 1)
                        pool.dma_start(x1_d[bass.ds(TB * b + j, 1), :, :].rearrange("o p d -> (o p) d"), x1[:, j % 2, :])\
                            .then_inc(s_st[j % 2], 16)
                for i in range(2):
                    pool.wait_ge(s_st[i], 16 * NT // 2)

            @block.scalar
            def _(act):
                def hi_part(dst, i, u):
                    act.wait_ge(s_w[u], 16 * i + 16)
                    act.activation(dst, w_st[:, u, :], ACT.Copy).then_inc(s_whi, 1)

                def branch_hi(b, m):
                    if m >= 2 or not isinstance(b, int) or b:
                        act.wait_ge(s_br, KD * b + m - 1)
                    hi_part(wb_hi[:, m % 2, :, :].rearrange("p k m -> p (k m)"), KD // 2 * b + m // 2, m % 2)

                def body(b, last, first=False):
                    for m in range(KD):
                        if m < KD - 1:
                            branch_hi(b, m + 1)
                        elif not last:
                            branch_hi(b + 1, 0)
                        if first:
                            act.wait_ge(s_wo[m % 2], 16 * (m // 2 + 1))
                            act.activation(wo_hi[:, m, :], x[:, m % 2, :], ACT.Copy).then_inc(s_wohi, 1)
                    for j in range(TB):
                        n = TB * b + j
                        act.wait_ge(s_y, n + 1)
                        if j or not isinstance(b, int) or b:
                            act.wait_ge(s_sq, n)
                        act.activation(junk[:], ps_y[:, j % 2, :], ACT.Square, accum_out=sums[:, j % 2:j % 2 + 1])\
                            .then_inc(s_sq, 1)
                        act.wait_ge(s_mean, n + 1)
                        act.activation(std[:, j % 2:j % 2 + 1], mean[:, j % 2:j % 2 + 1], ACT.Sqrt).then_inc(s_std, 1)

                branch_hi(0, 0)
                body(0, False, True)
                with act.Fori(1, NB - 1) as b:
                    body(b, False)
                body(NB - 1, True)

            @block.vector
            def _(dve):
                def branch_lo(b, m):
                    piece = KD * b + m
                    dve.wait_ge(s_whi, piece + 1)
                    dve.tensor_tensor(wb_lo[:, m % 2, :, :].rearrange("p k m -> p (k m)"), w_st[:, m % 2, :],
                                      wb_hi[:, m % 2, :, :].rearrange("p k m -> p (k m)"), ALU.subtract).then_inc(s_wlo, 1)

                def split_first_acts():
                    dve.wait_ge(s_yt, 16)
                    dve.tensor_copy(act_hi[:, KB:KD, :], st_b[:]).then_inc(s_act, 1)
                    dve.wait_ge(s_act, 1)
                    dve.tensor_tensor(act_lo[:, KB:KD, :], st_b[:], act_hi[:, KB:KD, :], ALU.subtract).then_inc(s_act, 1)
                    dve.wait_ge(s_o, 64)
                    dve.tensor_tensor(st_a[:], st_a[:], x1_staged, ALU.add).then_inc(s_act, 1)
                    dve.wait_ge(s_act, 3)
                    dve.wait_ge(s_rb, 32)
                    dve.tensor_tensor(st_a[:], st_a[:], x_staged, ALU.mult).then_inc(s_act, 1)
                    dve.wait_ge(s_act, 4)
                    dve.tensor_copy(act_hi[:, 0:KB, :], st_a[:]).then_inc(s_act, 1)
                    dve.wait_ge(s_act, 5)
                    dve.tensor_tensor(act_lo[:, 0:KB, :], st_a[:], act_hi[:, 0:KB, :], ALU.subtract).then_inc(s_act, 1)

                def split_acts(b, part):
                    n = AS * b
                    if part == 1:
                        dve.wait_ge(s_act, n + 1)
                        dve.wait_ge(s_rb, 32 * (b + 1))
                        dve.tensor_tensor(st_a[:], st_a[:], st_b[:], ALU.mult).then_inc(s_act, 1)
                        dve.wait_ge(s_act, n + 2)
                        dve.tensor_copy(act_hi[:, 0:KB, :], st_a[:]).then_inc(s_act, 1)
                        dve.wait_ge(s_act, n + 3)
                        dve.tensor_tensor(act_lo[:, 0:KB, :], st_a[:], act_hi[:, 0:KB, :], ALU.subtract).then_inc(s_act, 1)
                        return
                    if part == 2:
                        dve.wait_ge(s_yt, 16 * (b + 1))
                        dve.tensor_copy(act_hi[:, KB:KD, :], st_b[:]).then_inc(s_act, 1)
                        dve.wait_ge(s_act, n + 5)
                        dve.tensor_tensor(act_lo[:, KB:KD, :], st_b[:], act_hi[:, KB:KD, :], ALU.subtract).then_inc(s_act, 1)
                        return
                    dve.wait_ge(s_o, 64 * (b + 1))
                    dve.wait_ge(s_br, KD * b)
                    dve.tensor_tensor(st_a[:], st_a[:], st_b[:], ALU.add).then_inc(s_act, 1)

                def merge(b, m):
                    n = 5 * (KD * b + m)
                    dve.wait_ge(s_gate[m % 2], 32 * (KD // 2 * b + m // 2 + 1))
                    dve.wait_ge(s_br, KD * b + m + 1)
                    if m == 0 and (not isinstance(b, int) or b):
                        dve.wait_ge(s_y, TB * b)
                    ga, gf = gate[:, m % 2, 0, :], gate[:, m % 2, 1, :]
                    dve.tensor_tensor(ga, ps_b[:, m % 2, 0, :], ga, ALU.mult).then_inc(s_mg, 1)
                    dve.tensor_tensor(gf, ps_b[:, m % 2, 1, :], gf, ALU.mult).then_inc(s_mg, 1)
                    dve.wait_ge(s_mg, n + 2)
                    dve.tensor_tensor(ga, ga, gf, ALU.add).then_inc(s_mg, 1)
                    dve.wait_ge(s_mg, n + 3)
                    dve.tensor_copy(mg_hi[:, m, :], ga).then_inc(s_mg, 1)
                    dve.wait_ge(s_mg, n + 4)
                    dve.tensor_tensor(mg_lo[:, m, :], ga, mg_hi[:, m, :], ALU.subtract).then_inc(s_mg, 1)

                def body(b, last, first=False):
                    for m in range(KD):
                        if m < KD - 1:
                            branch_lo(b, m + 1)
                        elif not last:
                            branch_lo(b + 1, 0)
                        merge(b, m)
                        if first:
                            dve.wait_ge(s_wohi, m + 1)
                            dve.tensor_tensor(wo_lo[:, m, :], x[:, m % 2, :], wo_hi[:, m, :], ALU.subtract).then_inc(s_wolo, 1)
                    for j in range(TB):
                        if not last and j < 3:
                            split_acts(b + 1, j)
                        n = TB * b + j
                        u = j % 2
                        dve.wait_ge(s_sq, n + 1)
                        dve.tensor_scalar(mean[:, u:u + 1], sums[:, u:u + 1], 1.0 / D, EPS, ALU.mult, ALU.add)\
                            .then_inc(s_mean, 1)
                        dve.wait_ge(s_std, n + 1)
                        dve.reciprocal(rstd[:, u:u + 1], std[:, u:u + 1]).then_inc(s_rstd, 1)
                        dve.wait_ge(s_rstd, n + 1)
                        if j >= 2 or not isinstance(b, int) or b:
                            dve.wait_ge(s_st[u], 16 * (TB // 2 * b + j // 2))
                        dve.scalar_tensor_tensor(x1[:, u, :], ps_y[:, u, :], rstd[:, u:u + 1], g1[:], ALU.mult, ALU.mult)\
                            .then_inc(s_n1, 1)
                        dve.wait_ge(s_n1, n + 1)
                        dve.wait_ge(s_x[u], 16 * (TB // 2 * b + j // 2 + 1))
                        dve.tensor_tensor(x1[:, u, :], x1[:, u, :], x[:, u, :], ALU.add).then_inc(s_x1, 1)

                dve.wait_ge(s_sums, 16)
                dve.reciprocal(total[:], total[:]).then_inc(s_rec, 1)
                branch_lo(0, 0)
                split_first_acts()
                dve.wait_ge(s_g1, 16)
                body(0, False, True)
                with dve.Fori(1, NB - 1) as b:
                    body(b, False)
                body(NB - 1, True)

            @block.tensor
            def _(pe):
                def body(b):
                    pe.wait_ge(s_act, AS * (b + 1))
                    for m in range(KD):
                        u = m % 2
                        pe.wait_ge(s_wlo, KD * b + m + 1)
                        if m >= 2 or not isinstance(b, int) or b:
                            pe.wait_ge(s_mg, 5 * (KD * b + m - 1))
                        for branch in range(2):
                            for k in range(KB):
                                kk = branch * KB + k
                                q = product3(pe, ps_b[:, u, branch, :], wb_hi[:, u, kk, :], wb_lo[:, u, kk, :],
                                             act_hi[:, kk, :], act_lo[:, kk, :], k == 0, k == KB - 1)
                        q.then_inc(s_br, 1)
                    for j in range(TB):
                        rows = slice(j * P, (j + 1) * P)
                        if j >= 2 or not isinstance(b, int) or b:
                            pe.wait_ge(s_n1, TB * b + j - 1)
                        for k in range(KD):
                            if j == 0:
                                pe.wait_ge(s_mg, 5 * (KD * b + k + 1))
                                if isinstance(b, int):
                                    pe.wait_ge(s_wolo, k + 1)
                            for n in range(2):
                                cols = slice(n * BLK, (n + 1) * BLK)
                                q = product3(pe, ps_y[:, j % 2, cols], mg_hi[:, k, rows], mg_lo[:, k, rows],
                                             wo_hi[:, k, cols], wo_lo[:, k, cols], k == 0, k == KD - 1)
                        q.then_inc(s_y, 1)

                body(0)
                with pe.Fori(1, NB) as b:
                    body(b)


class UpWeights:

    def __init__(self, r, w_up):
        self.w_up = w_up
        self.st = r.sb("w_st", [P, 2, D])
        self.w_hi, self.w_lo = (r.sb(n, [P, 2, KD, P], F32R) for n in ("wu_hi", "wu_lo"))
        self.s_w = [r.sem(f"wu_loaded{i}") for i in range(2)]
        self.s_whi, self.s_wlo = r.sem("wu_hi_made"), r.sem("wu_lo_made")

    def load(self, sp, p, j):
        if not isinstance(p, int) or p:
            sp.wait_ge(self.s_wlo, 2 * p + j - 1)
        sp.dma_start(self.st[:, j:j + 1, :], self.w_up[bass.ds(2 * p + j, 1), :, :].rearrange("o p d -> p o d"))\
            .then_inc(self.s_w[j], 16)

    def high_part(self, act, p, j):
        act.wait_ge(self.s_w[j], 16 * p + 16)
        act.activation(self.w_hi[:, j, :, :].rearrange("p k m -> p (k m)"), self.st[:, j, :], ACT.Copy)\
            .then_inc(self.s_whi, 1)

    def low_part(self, dve, p, j):
        dve.wait_ge(self.s_whi, 2 * p + j + 1)
        dve.tensor_tensor(self.w_lo[:, j, :, :].rearrange("p k m -> p (k m)"), self.st[:, j, :],
                          self.w_hi[:, j, :, :].rearrange("p k m -> p (k m)"), ALU.subtract).then_inc(self.s_wlo, 1)


def ffn_phase(nc, half, h_hi, h_lo, wu, w_dn, conv, gate_rows, carry, gc_hi, gc_lo, x1_d, out_d):
    NCV = HALF + 1
    G0 = P - 1
    tiles = NT // 2 - 1 if half == 0 else NT // 2 + 1
    t0 = 0 if half == 0 else NT // 2 - 1
    off = P if half == 0 else 0
    with Res(nc, f"ffn{half}") as r:
        wu_hi, wu_lo = wu.w_hi, wu.w_lo
        wd_st = r.sb("wd_st", [P, D])
        wd_hi, wd_lo = (r.sb(n, [P, 2, D], F32R) for n in ("wd_hi", "wd_lo"))
        u = r.sb("u", [P, 2, HALF + 3])
        cv = r.sb("cv", [P, 2, NCV])
        g_hi, g_lo = (r.sb(n, [P, 2, HALF + P], F32R) for n in ("g_hi", "g_lo"))
        y = r.sb("y", [P, tiles, D])
        cw = r.sb("cw", [P, 2 * NP, 4])
        sums, std, rstd = (r.sb(n, [P, tiles]) for n in ("sums", "std", "rstd"))
        eps = r.sb("eps", [P, 1])
        x1 = [u[:, 1, 0:D], cv[:, 0, 0:D], cv[:, 1, 0:D]]
        ps_u = r.ps("ps_u", [P, 2, 2, BLK])
        ps_d = r.ps("ps_d", [P, 2, D])
        s_x = [r.sem(f"x_loaded{i}") for i in range(3)]
        s_st = r.sem("out_stored")
        s_cw, s_wd, s_init, s_g2 = (r.sem(n) for n in ("conv_loaded", "wd_loaded", "init", "g2_loaded"))
        s_whi, s_wlo, s_dhi, s_dlo = wu.s_whi, wu.s_wlo, r.sem("wd_hi_made"), r.sem("wd_lo_made")
        s_up, s_u, s_cs, s_cd, s_ge, s_g, s_ghi, s_glo, s_gc = (
            r.sem(n) for n in ("up", "u_copied", "conv_steps", "conv", "gelu", "g", "g_hi_made", "g_lo_made", "g_carry"))
        s_dn, s_y, s_sq, s_std, s_rstd, s_n, s_o = (
            r.sem(n) for n in ("down", "y_added", "squares", "root", "rstd", "scaled", "out"))
        CS = 8
        with r.block() as block:

            @block.sync
            def _(sp):
                def load_dn(p, first=False):
                    if not first:
                        sp.wait_ge(s_dlo, p)
                    sp.dma_start(wd_st[:], w_dn[bass.ds(p, 1), :, :].rearrange("o p d -> (o p) d")).then_inc(s_wd, 16)

                sp.dma_start(cw[:], conv).then_inc(s_cw, 16)
                load_dn(0, True)
                with sp.Fori(0, NP - 1) as p:
                    wu.load(sp, p + 1, 0)
                    wu.load(sp, p + 1, 1)
                    load_dn(p + 1)
                sp.wait_ge(s_dlo, NP)
                sp.dma_start(wd_st[:], gate_rows).then_inc(s_g2, 16)

                def load_x1(t):
                    if t == 0:
                        sp.wait_ge(s_cd, 2 * NP)
                    if t == 1:
                        sp.wait_ge(s_glo, NP)
                    sp.dma_start(x1[t % 3], x1_d[t0 + t]).then_inc(s_x[t % 3], 16)

                for t in range(3):
                    load_x1(t)
                for t in range(tiles):
                    sp.wait_ge(s_o, t + 1)
                    sp.dma_start(out_d[t0 + t], y[:, t, :]).then_inc(s_st, 16)
                    if t + 3 < tiles:
                        load_x1(t + 3)
                sp.wait_ge(s_st, 16 * tiles)

            @block.gpsimd
            def _(pool):
                pool.memset(y[:], 0.0).then_inc(s_init, 1)
                pool.memset(u[:, :, 0:2], 0.0).then_inc(s_init, 1)
                pool.memset(u[:, :, HALF + 2:HALF + 3], 0.0).then_inc(s_init, 1)

                def kept_columns(p, v):
                    if half == 0:
                        pool.wait_ge(s_glo, p + 1)
                    elif not isinstance(p, int):
                        pool.wait_ge(s_dn, tiles * (p - 1))
                    for kept, whole in ((gc_hi, g_hi), (gc_lo, g_lo)):
                        kept = kept[:, bass.ds(p, 1), :].rearrange("p o c -> p (o c)")
                        if half == 0:
                            m = pool.tensor_copy(kept, whole[:, v, HALF:HALF + G0])
                        else:
                            m = pool.tensor_copy(whole[:, v, 0:G0], kept)
                    m.then_inc(s_gc, 1)

                kept_columns(0, 0)
                kept_columns(1, 1)
                with pool.Fori(1, NP // 2) as i:
                    for v in range(2):
                        kept_columns(2 * i + v, v)
                for t in range(tiles):
                    pool.wait_ge(s_n, t + 1)
                    pool.wait_ge(s_x[t % 3], 16 * (t // 3 + 1))
                    pool.tensor_tensor(y[:, t, :], y[:, t, :], x1[t % 3], ALU.add).then_inc(s_o, 1)

            @block.scalar
            def _(act):
                def up_hi(p, j):
                    act.wait_ge(s_up, 4 * (p - 1) + 2 * j + 2)
                    wu.high_part(act, p, j)

                def body(p, v, last, first):
                    for j in range(2):
                        for n in range(2):
                            act.wait_ge(s_up, 4 * p + 2 * j + n + 1)
                            if not first:
                                act.wait_ge(s_cd, 2 * (p - 1) + j + 1)
                            act.activation(u[:, j, 2 + n * BLK:2 + (n + 1) * BLK], ps_u[:, j, n, :], ACT.Copy)\
                                .then_inc(s_u, 1)
                        if not last:
                            up_hi(p + 1, j)
                    act.wait_ge(s_wd, 16 * p + 16)
                    if not (isinstance(p, int) and p < 2):
                        act.wait_ge(s_dn, tiles * (p - 1))
                    act.activation(wd_hi[:, v, :], wd_st[:], ACT.Copy).then_inc(s_dhi, 1)
                    act.wait_ge(s_cd, 2 * p + 1)
                    act.activation(cv[:, 0, :], cv[:, 0, :], ACT.Gelu_apprx_tanh).then_inc(s_ge, 1)
                    act.wait_ge(s_g, p + 1)
                    if half == 0 and not (isinstance(p, int) and p < 2):
                        act.wait_ge(s_gc, p - 1)
                    act.activation(g_hi[:, v, G0:G0 + NCV], cv[:, 0, :], ACT.Copy).then_inc(s_ghi, 1)

                body(0, 0, False, True)
                body(1, 1, False, False)
                with act.Fori(1, NP // 2 - 1) as i:
                    for v in range(2):
                        body(2 * i + v, v, False, False)
                body(NP - 2, 0, False, False)
                body(NP - 1, 1, True, False)
                for t in range(tiles):
                    act.wait_ge(s_y, tiles * (NP - 1) + t + 1)
                    if t:
                        act.wait_ge(s_sq, t)
                    act.activation(u[:, 0, 0:D], y[:, t, :], ACT.Square, accum_out=sums[:, t:t + 1]).then_inc(s_sq, 1)
                    act.wait_ge(s_sq, t + 1)
                    act.activation(std[:, t:t + 1], sums[:, t:t + 1], ACT.Sqrt, bias=eps[:, 0:1], scale=1.0 / D)\
                        .then_inc(s_std, 1)

            @block.vector
            def _(dve):
                def convolve(p, j, first):
                    n = CS * p + 4 * j
                    one = lambda i: cw[:, bass.ds(2 * p + j, 1), i:i + 1].rearrange("p o i -> p (o i)")
                    keep = carry[:, bass.ds(2 * p + j, 1), :].rearrange("p o i -> p (o i)")
                    dve.wait_ge(s_u, 4 * p + 2 * j + 2)
                    if half == 0:
                        dve.tensor_copy(keep, u[:, j, HALF:HALF + 2]).then_inc(s_cs, 1)
                    else:
                        dve.tensor_copy(u[:, j, 0:2], keep).then_inc(s_cs, 1)
                        dve.wait_ge(s_cs, n + 1)
                    if not first:
                        dve.wait_ge(s_ghi, p)
                        dve.wait_ge(s_glo, p)
                    dve.tensor_scalar(cv[:, j, :], u[:, j, 0:NCV], one(0), one(3), ALU.mult, ALU.add).then_inc(s_cs, 1)
                    dve.wait_ge(s_cs, n + 2)
                    dve.scalar_tensor_tensor(cv[:, j, :], u[:, j, 1:NCV + 1], one(1), cv[:, j, :], ALU.mult, ALU.add)\
                        .then_inc(s_cs, 1)
                    dve.wait_ge(s_cs, n + 3)
                    dve.scalar_tensor_tensor(cv[:, j, :], u[:, j, 2:NCV + 2], one(2), cv[:, j, :], ALU.mult, ALU.add)\
                        .then_inc(s_cd, 1)
                    dve.sem_inc(s_cs, 1)

                def add_tile(p, t):
                    dve.wait_ge(s_dn, tiles * p + t + 1)
                    dve.tensor_tensor(y[:, t, :], y[:, t, :], ps_d[:, t % 2, :], ALU.add).then_inc(s_y, 1)

                def add_down(p):
                    for t in range(tiles):
                        add_tile(p, t)

                def norm_tile(t):
                    dve.wait_ge(s_std, t + 1)
                    dve.reciprocal(rstd[:, t:t + 1], std[:, t:t + 1]).then_inc(s_rstd, 1)
                    dve.wait_ge(s_rstd, t + 1)
                    dve.scalar_tensor_tensor(y[:, t, :], y[:, t, :], rstd[:, t:t + 1], wd_st[:], ALU.mult, ALU.mult)\
                        .then_inc(s_n, 1)

                def body(p, v, last, first):
                    convolve(p, 0, first)
                    if not last:
                        wu.low_part(dve, p + 1, 0)
                    if not first:
                        add_down(p - 1)
                    if not last:
                        wu.low_part(dve, p + 1, 1)
                    convolve(p, 1, first)
                    dve.wait_ge(s_ge, p + 1)
                    dve.wait_ge(s_cd, 2 * p + 2)
                    dve.tensor_tensor(cv[:, 0, :], cv[:, 0, :], cv[:, 1, :], ALU.mult).then_inc(s_g, 1)
                    dve.wait_ge(s_dhi, p + 1)
                    dve.tensor_tensor(wd_lo[:, v, :], wd_st[:], wd_hi[:, v, :], ALU.subtract).then_inc(s_dlo, 1)
                    dve.wait_ge(s_ghi, p + 1)
                    if half == 0 and not (isinstance(p, int) and p < 2):
                        dve.wait_ge(s_gc, p - 1)
                    dve.tensor_tensor(g_lo[:, v, G0:G0 + NCV], cv[:, 0, :], g_hi[:, v, G0:G0 + NCV], ALU.subtract)\
                        .then_inc(s_glo, 1)

                dve.memset(eps[:], EPS)
                dve.wait_ge(s_cw, 16)
                dve.wait_ge(s_init, 3)
                body(0, 0, False, True)
                body(1, 1, False, False)
                with dve.Fori(1, NP // 2 - 1) as i:
                    for v in range(2):
                        body(2 * i + v, v, False, False)
                body(NP - 2, 0, False, False)
                body(NP - 1, 1, True, False)
                for t in range(tiles):
                    add_tile(NP - 1, t)
                    if t == 0:
                        dve.wait_ge(s_g2, 16)
                    else:
                        norm_tile(t - 1)
                norm_tile(tiles - 1)

            @block.tensor
            def _(pe):
                def up(p, first=False):
                    for j in range(2):
                        pe.wait_ge(s_wlo, 2 * p + j + 1)
                        for n in range(2):
                            if not first:
                                pe.wait_ge(s_u, 4 * (p - 1) + 2 * j + n + 1)
                            cols = slice(n * BLK, (n + 1) * BLK)
                            for k in range(KD):
                                m = product3(pe, ps_u[:, j, n, :], wu_hi[:, j, k, :], wu_lo[:, j, k, :],
                                             h_hi[:, k, cols], h_lo[:, k, cols], k == 0, k == KD - 1)
                            m.then_inc(s_up, 1)

                def down(p, v):
                    pe.wait_ge(s_dlo, p + 1)
                    pe.wait_ge(s_glo, p + 1)
                    if half == 1:
                        pe.wait_ge(s_gc, p + 1)
                    for t in range(tiles):
                        if t >= 2 or not isinstance(p, int) or p:
                            pe.wait_ge(s_y, tiles * p + t - 1)
                        g = slice(off + t * P, off + (t + 1) * P)
                        for n in range(2):
                            cols = slice(n * BLK, (n + 1) * BLK)
                            m = product3(pe, ps_d[:, t % 2, cols], g_hi[:, v, g], g_lo[:, v, g],
                                         wd_hi[:, v, cols], wd_lo[:, v, cols], True, True)
                        m.then_inc(s_dn, 1)

                up(0, True)
                up(1)
                down(0, 0)
                with pe.Fori(0, NP // 2 - 1) as i:
                    up(2 * i + 2)
                    down(2 * i + 1, 1)
                    up(2 * i + 3)
                    down(2 * i + 2, 0)
                down(NP - 1, 1)


def program(nc, x, c, w_ada, b_cols, b_ada, pre_g, post_g, w_f, w_z, b_gate, qk_g, w_branch, w_out, w_up, conv, w_dn,
            t_pos, t_chan, rope_cos, rope_sin, swap, head_mean, ident_d, out, scratch_kind="Internal"):
    def scratch(name, shape, dt=F32):
        return nc.dram_tensor(f"scratch_{name}", shape, dt, kind=scratch_kind).ap()

    gate_rows = scratch("gate_rows", [P, 2, D])
    f_d = scratch("f", [NT, P, FW])
    qkv_d = scratch("qkv", [NQC + 2, P, S])
    gates_d = scratch("gates", [NB, 2 * KD, P, BLK])
    yT_d = scratch("yT", [NG, P, S])
    z_d = scratch("z", [2, NG, P, N1 * P])
    kv_d = scratch("kv", [NKV, P, 2, S])
    o_d = scratch("o", [2, NH, HD, S])
    sums_d = scratch("sums", [NH, S])
    rec_d = scratch("rec", [NH, S])
    x1_d = scratch("x1", [NT, P, D])

    with Res(nc, "keep") as keep:
        ident = keep.sb("ident", [P, P])
        ones = keep.sb("ones", [P, P])
        mod = keep.sb("mod", [P, 4, KD])
        first_sem = load_constants(nc, ident_d, ident, ones)
        c_act = keep.sb("c_act", [P, KD])

        def make_ada(slots, *parts):
            return lambda r: Ada(r, slots, parts, c_act, w_ada, b_cols, b_ada, pre_g, post_g, ones, mod, gate_rows)

        with Res(nc, "h1") as h1:
            h_hi, h_lo = (h1.sb(n, [P, KD, S], F32R) for n in ("hi", "lo"))
            norm_phase(nc, "norm1", x, NB, ident, mod[:, 0, :], mod[:, 1, :], h_hi, h_lo,
                       make_ada(4, 0, 1), c, c_act)
            f_phase(nc, w_f, h_hi, h_lo, f_d, make_ada(3, 3, 4, 2, 5))
            kept = proj_phase(nc, w_z, h_hi, h_lo, b_gate, qk_g, rope_cos, rope_sin, swap, head_mean, ident, f_d,
                              qkv_d, gates_d, z_d, kv_d)
        with Res(nc, "head0") as shared:
            head0 = Head0(shared)
            fourier_phase(nc, head0, z_d, t_pos, t_chan, qkv_d, kv_d, ident, yT_d)
            attention_phase(nc, head0, qkv_d, kv_d, ident, ones, o_d, sums_d)
        merge_phase(nc, x, w_branch, w_out, o_d, sums_d, rec_d, yT_d, gates_d, gate_rows[:, 0, :], x1_d, first_sem, kept)
        with Res(nc, "h2") as h2:
            h_hi, h_lo = (h2.sb(n, [P, KD, HALF], F32R) for n in ("hi", "lo"))
            carry = h2.sb("carry", [P, 2 * NP, 2])
            gc_hi, gc_lo = (h2.sb(n, [P, NP, P - 1], F32R) for n in ("gc_hi", "gc_lo"))
            for half in range(2):
                with Res(nc, f"up{half}") as up:
                    wu = UpWeights(up, w_up)
                    norm_phase(nc, f"norm2{half}", x1_d[half * NT // 2:(half + 1) * NT // 2], NB // 2, ident,
                               mod[:, 2, :], mod[:, 3, :], h_hi, h_lo, wu=wu)
                    ffn_phase(nc, half, h_hi, h_lo, wu, w_dn, conv, gate_rows[:, 1, :], carry, gc_hi, gc_lo, x1_d, out)


def tables():
    n2, k2 = np.arange(P)[:, None], np.arange(P)[None, :]
    pos = np.empty((K1, P, 3, P))
    for k1 in range(K1):
        a = 2 * np.pi * ((n2 * (k1 + N1 * k2)) % S) / S
        pos[k1, :, 0], pos[k1, :, 1], pos[k1, :, 2] = np.sin(a), np.cos(a), -np.sin(a)
    a = 2 * np.pi * ((n2 * k2) % P) / P
    chan = np.stack([np.cos(a), np.sin(a), -np.sin(a)], 1) / math.sqrt(S * P)
    grid_w, pairs = 64, HD // 4
    inv = 10000.0 ** (-np.arange(pairs) / pairs)
    t = np.arange(S)
    ang = np.concatenate([(t // grid_w)[None, :] * inv[:, None], (t % grid_w)[None, :] * inv[:, None]])
    ang = np.tile(np.repeat(ang, 2, axis=0), (2, 1))
    sign = np.where(np.arange(P) % 2 == 0, -1.0, 1.0)[:, None]
    swap = np.zeros((P, P))
    swap[np.arange(P) ^ 1, np.arange(P)] = 1.0
    head_mean = np.kron(np.eye(2), np.full((HD, HD), 1.0 / HD))
    made = {"t_pos": pos.transpose(1, 0, 2, 3).reshape(P, K1, 3 * P), "t_chan": chan.reshape(P, 3 * P), "rope_cos": np.cos(ang),
            "rope_sin": sign * np.sin(ang), "swap": swap, "head_mean": head_mean, "ident_d": np.eye(P)}
    return {k: np.ascontiguousarray(v.astype(np.float32)) for k, v in made.items()}


def layouts(a):
    w_in = a["w_in"][0].reshape(KD, P, -1)
    o1 = NH * HD
    o3 = o1 + 2 * NKV * HD
    o4 = o3 + FW

    def chunks(w):
        n = w.shape[2] // P
        return w.reshape(w.shape[0], P, n, P).transpose(2, 1, 0, 3).reshape(n, P, -1)

    def pairs(first, second):
        return np.stack([first, second], 1).reshape(-1, *first.shape[1:])

    by_channel = lambda v: v.reshape(-1, P).T
    ga, gf = chunks(w_in[:, :, o4:o4 + D]), chunks(w_in[:, :, o4 + D:])
    bga, bgf = by_channel(a["b_gate"][0, :D]), by_channel(a["b_gate"][0, D:])
    wa = chunks(a["w_attn_branch"][0].reshape(NQC, P, D))
    wf = chunks(a["w_fourier_branch"][0].reshape(NG, P, D))
    wu = a["w_up"][0].reshape(KD, P, -1)
    cw = np.concatenate([a["conv_w"][0], a["conv_b"][0][None]])
    cw = cw.reshape(4, 2, NP, P).transpose(3, 2, 1, 0).reshape(P, 2 * NP, 4)
    q_g, k_g = np.tile(a["q_norm_g"][0], 2), np.tile(a["k_norm_g"][0], 2)
    laid = {
        "x": a["x"].reshape(NT, P, D),
        "c": by_channel(a["c"][0]),
        "w_ada": a["w_ada"][0].reshape(KD, P, 6 * D),
        "b_ada": a["b_ada"],
        "b_cols": by_channel(a["b_ada"][0]),
        "pre_g": np.stack([by_channel(a["mix_pre_g"][0]), by_channel(a["ffn_pre_g"][0])], 1),
        "post_g": np.stack([a["mix_post_g"][0], a["ffn_post_g"][0]]),
        "w_f": w_in[:, :, o3:o4],
        "w_z": np.concatenate([chunks(w_in[:, :, :o3]), pairs(ga, gf)]),
        "b_gate": np.stack([bga, bgf], 2).reshape(P, 2 * KD),
        "qk_g": np.stack([q_g] * NQC + [k_g], 1),
        "w_branch": np.concatenate([wa, wf], 2),
        "w_out": a["w_out"][0].reshape(KD, P, D),
        "w_up": pairs(chunks(wu[:, :, :DFF]), chunks(wu[:, :, DFF:])),
        "conv": cw,
        "w_dn": a["w_down"][0].reshape(NP, P, D),
    }
    return {k: np.ascontiguousarray(v) for k, v in laid.items()}


def kernel(**inputs):
    import concourse.bacc as bacc
    from concourse.bass_utils import run_bass_kernel_spmd

    arrays = {**layouts({k: np.asarray(v) for k, v in inputs.items()}), **tables()}
    nc = bacc.Bacc("TRN2", target_bir_lowering=False, num_devices=1)
    args = {n: nc.dram_tensor(f"in_{n}", a.shape, mybir.dt.from_np(a.dtype), kind="ExternalInput").ap()
            for n, a in arrays.items()}
    out = nc.dram_tensor("out", [NT, P, D], F32, kind="ExternalOutput").ap()
    program(nc, out=out, **args)
    got = run_bass_kernel_spmd(nc, [{f"in_{n}": a for n, a in arrays.items()}], core_ids=[0])
    return got.results[0]["out"].reshape(1, S, D)
```
